# Optimizing a Trainium2 kernel written in Bass

```python
import math
import jax, jax.numpy as jnp
from jax import lax
import numpy as np

D_MODEL = 1024
BATCH = 1
SEQ = 2048
DEPTH = 1

MIX_W = 256
N_BRANCH = 4
CONV_A = 3
SC_HEADS = 4
POOL_WINDOWS = (2, 4, 8, 16)
POOL_GROUPS = len(POOL_WINDOWS)
POOL_GC = MIX_W // POOL_GROUPS
S5_GROUP_CH = 16
S5_GROUPS = MIX_W // S5_GROUP_CH
S5_STATE = 64
S5_EIG_CLIP = -1e-4
LRU_HEADS = 4
LRU_HD = MIX_W // LRU_HEADS
LRU_CONV = 4
LRU_C = 8.0
COLS_A = 3 * MIX_W
COLS_B = MIX_W
COLS_C = MIX_W
COLS_D = 2 * MIX_W
IN_COLS = COLS_A + COLS_B + COLS_C + COLS_D
N_GROUPS = 4
EXP_PER_GROUP = 8
N_EXPERTS = N_GROUPS * EXP_PER_GROUP
TOP_K = 2
D_EXPERT = 512
MOE_BLOCK = 128
EPS = 1e-6

kernel_name = "hybrid_gated_conv_pool_s5_rglru_hmoe"

def rms_norm(x, g):
    x32 = x.astype(jnp.float32)
    y = x32 * lax.rsqrt(jnp.mean(x32 * x32, axis=-1, keepdims=True) + EPS) * g.astype(jnp.float32)
    return y.astype(x.dtype)

def causal_dwconv(u, w):
    k_taps = w.shape[0]
    s = u.shape[1]
    up = jnp.pad(u, ((0, 0), (k_taps - 1, 0), (0, 0)))
    y = up[:, 0:s] * w[0]
    for k in range(1, k_taps):
        y = y + up[:, k:k + s] * w[k]
    return y

def linear_scan(a, b):
    def op(c1, c2):
        a1, b1 = c1
        a2, b2 = c2
        return a1 * a2, a2 * b1 + b2
    _, h = lax.associative_scan(op, (a, b), axis=1)
    return h

def short_conv_mixer(bg, cg, xv, conv_w):
    return bg * causal_dwconv(cg * xv, conv_w)

def pool_mixer(u, pool_w, pool_b, pool_scale):
    bn, s, _ = u.shape
    u32 = u.astype(jnp.float32)
    cs = jnp.cumsum(u32, axis=1)
    t = jnp.arange(s)
    outs = []
    for gi, w in enumerate(POOL_WINDOWS):
        c = cs[..., gi * POOL_GC:(gi + 1) * POOL_GC]
        prev = jnp.pad(c, ((0, 0), (w, 0), (0, 0)))[:, :s]
        cnt = jnp.minimum(t + 1, w).astype(jnp.float32)[None, :, None]
        outs.append((c - prev) / cnt)
    pooled = jnp.concatenate(outs, axis=-1) - u32
    pg = pooled.reshape(bn, s, POOL_GROUPS, POOL_GC)
    y = jnp.einsum('bsgc,gcd->bsgd', pg, pool_w.astype(jnp.float32)) + pool_b.astype(jnp.float32)
    return (y.reshape(bn, s, MIX_W) * pool_scale.astype(jnp.float32)).astype(u.dtype)

def s5_mixer(u, lam_re, lam_im, log_step, b_re, b_im, c_re, c_im, d, glu_w, glu_b):
    bn, s, _ = u.shape
    u32 = u.astype(jnp.float32)
    ug = u32.reshape(bn, s, S5_GROUPS, S5_GROUP_CH)
    lam = lax.complex(jnp.minimum(lam_re.astype(jnp.float32), S5_EIG_CLIP), lam_im.astype(jnp.float32))
    step = jnp.exp(log_step.astype(jnp.float32))[:, None]
    a_bar = jnp.exp(lam * step)
    coef = (a_bar - 1.0) / lam
    b_bar = coef[..., None] * lax.complex(b_re.astype(jnp.float32), b_im.astype(jnp.float32))
    bu = lax.complex(jnp.einsum('bsgh,gph->bsgp', ug, jnp.real(b_bar)),
                     jnp.einsum('bsgh,gph->bsgp', ug, jnp.imag(b_bar)))
    h = linear_scan(jnp.broadcast_to(a_bar, bu.shape), bu)
    y = (jnp.einsum('bsgp,ghp->bsgh', jnp.real(h), c_re.astype(jnp.float32))
         - jnp.einsum('bsgp,ghp->bsgh', jnp.imag(h), c_im.astype(jnp.float32)))
    y = y.reshape(bn, s, MIX_W) + d.astype(jnp.float32) * u32
    y = jax.nn.gelu(y)
    y = y * jax.nn.sigmoid(y @ glu_w.astype(jnp.float32) + glu_b.astype(jnp.float32))
    return y.astype(u.dtype)

def rglru_mixer(xb, gate_in, conv_w, conv_b, wa, ba, wx, bx, lam):
    bn, s, _ = xb.shape
    xc = (causal_dwconv(xb, conv_w) + conv_b).astype(jnp.float32)
    xh = xc.reshape(bn, s, LRU_HEADS, LRU_HD)
    r = jax.nn.sigmoid(jnp.einsum('bshc,hcd->bshd', xh, wa.astype(jnp.float32)) + ba.astype(jnp.float32)).reshape(bn, s, MIX_W)
    i = jax.nn.sigmoid(jnp.einsum('bshc,hcd->bshd', xh, wx.astype(jnp.float32)) + bx.astype(jnp.float32)).reshape(bn, s, MIX_W)
    log_a = -LRU_C * r * jax.nn.softplus(-lam.astype(jnp.float32))
    a = jnp.exp(log_a)
    mult = jnp.sqrt(-jnp.expm1(2.0 * log_a))
    h = linear_scan(a, mult * (i * xc))
    return (h * jax.nn.gelu(gate_in.astype(jnp.float32))).astype(xb.dtype)

def hybrid_mixer(xn, w_in, conv_a_w, pool_w, pool_b, pool_scale,
                 s5_lambda_re, s5_lambda_im, s5_log_step, s5_b_re, s5_b_im, s5_c_re, s5_c_im, s5_d, s5_glu_w, s5_glu_b,
                 lru_conv_w, lru_conv_b, lru_wa, lru_ba, lru_wx, lru_bx, lru_lambda,
                 merge_gate_w, merge_gate_b, branch_w, w_out):
    bn, s, d = xn.shape
    proj = xn @ w_in
    o0 = 0
    a_b = proj[..., o0:o0 + MIX_W]; a_c = proj[..., o0 + MIX_W:o0 + 2 * MIX_W]; a_x = proj[..., o0 + 2 * MIX_W:o0 + 3 * MIX_W]
    o1 = COLS_A
    p_u = proj[..., o1:o1 + COLS_B]
    o2 = o1 + COLS_B
    s_u = proj[..., o2:o2 + COLS_C]
    o3 = o2 + COLS_C
    l_x = proj[..., o3:o3 + MIX_W]; l_g = proj[..., o3 + MIX_W:o3 + 2 * MIX_W]

    ya = short_conv_mixer(a_b, a_c, a_x, conv_a_w)
    yb = pool_mixer(p_u, pool_w, pool_b, pool_scale)
    yc = s5_mixer(s_u, s5_lambda_re, s5_lambda_im, s5_log_step, s5_b_re, s5_b_im, s5_c_re, s5_c_im, s5_d, s5_glu_w, s5_glu_b)
    yd = rglru_mixer(l_x, l_g, lru_conv_w, lru_conv_b, lru_wa, lru_ba, lru_wx, lru_bx, lru_lambda)

    ys = jnp.stack([ya, yb, yc, yd], axis=2)
    branch = jnp.einsum('bskw,kwd->bskd', ys, branch_w)
    gates = jax.nn.sigmoid(xn @ merge_gate_w + merge_gate_b).reshape(bn, s, N_BRANCH, d)
    merged = jnp.sum(gates * branch, axis=2)
    return merged @ w_out

def hier_moe(xn, rg_w, rg_b, re_w, re_b, w1, w3, w2):
    bn, s, d = xn.shape
    x = xn.reshape(-1, d)
    t_tok = x.shape[0]
    x32 = x.astype(jnp.float32)
    g_prob = jax.nn.softmax(x32 @ rg_w.astype(jnp.float32) + rg_b.astype(jnp.float32), axis=-1)
    g_val, g_idx = lax.top_k(g_prob, 1)
    e_logits = (x32 @ re_w.astype(jnp.float32) + re_b.astype(jnp.float32)).reshape(t_tok, N_GROUPS, EXP_PER_GROUP)
    sel = jnp.take_along_axis(e_logits, g_idx[:, :, None], axis=1)[:, 0]
    e_val, e_idx = lax.top_k(sel, TOP_K)
    weights = jax.nn.softmax(e_val, axis=-1) * g_val
    expert_ids = g_idx * EXP_PER_GROUP + e_idx

    tk = t_tok * TOP_K
    flat_e = expert_ids.reshape(-1).astype(jnp.int32)
    flat_w = weights.reshape(-1)
    flat_tok = jnp.repeat(jnp.arange(t_tok, dtype=jnp.int32), TOP_K)
    order = jnp.argsort(flat_e)
    se = flat_e[order]
    counts = jnp.bincount(flat_e, length=N_EXPERTS)
    padded = ((counts + MOE_BLOCK - 1) // MOE_BLOCK) * MOE_BLOCK
    pad_end = jnp.cumsum(padded)
    pad_start = pad_end - padded
    start = jnp.cumsum(counts) - counts
    rank = jnp.arange(tk, dtype=jnp.int32) - start[se]
    dest = pad_start[se] + rank
    n_rows = (-(-tk // MOE_BLOCK)) * MOE_BLOCK + N_EXPERTS * MOE_BLOCK
    n_blocks = n_rows // MOE_BLOCK
    buf_tok = jnp.zeros((n_rows,), jnp.int32).at[dest].set(flat_tok[order])
    buf_w = jnp.zeros((n_rows,), jnp.float32).at[dest].set(flat_w[order])
    block_e = jnp.minimum(jnp.searchsorted(pad_end, jnp.arange(n_blocks) * MOE_BLOCK, side='right'), N_EXPERTS - 1)
    xs = x[buf_tok].reshape(n_blocks, MOE_BLOCK, d)

    def expert_block(args):
        xb, e = args
        h = jax.nn.silu(xb @ w1[e]) * (xb @ w3[e])
        return h @ w2[e]

    ys = lax.map(expert_block, (xs, block_e)).reshape(n_rows, d).astype(jnp.float32) * buf_w[:, None]
    out = jnp.zeros((t_tok, d), jnp.float32).at[buf_tok].add(ys)
    return out.reshape(bn, s, d).astype(xn.dtype)

def setup_inputs(seed: int = 0) -> dict:
    key = jax.random.key(seed)
    ks = iter(jax.random.split(key, 64))
    L, D, W = DEPTH, D_MODEL, MIX_W

    def nrm(shape, scale):
        return jax.random.normal(next(ks), shape, jnp.float32) * scale

    def unif(shape, lo, hi):
        return jax.random.uniform(next(ks), shape, jnp.float32, lo, hi)

    x = nrm((BATCH, SEQ, D), 1.0)
    norm1_g = 1.0 + nrm((L, D), 0.02)
    w_in = nrm((L, D, IN_COLS), D ** -0.5)
    conv_a_w = nrm((L, CONV_A, W), CONV_A ** -0.5)
    pool_w = nrm((L, POOL_GROUPS, POOL_GC, POOL_GC), POOL_GC ** -0.5)
    pool_b = nrm((L, POOL_GROUPS, POOL_GC), 0.01)
    pool_scale = 1.0 + nrm((L, W), 0.02)
    s5_lambda_re = -0.5 + nrm((L, S5_GROUPS, S5_STATE), 0.01)
    s5_lambda_im = math.pi * jnp.broadcast_to(jnp.arange(S5_STATE, dtype=jnp.float32), (L, S5_GROUPS, S5_STATE)) + nrm((L, S5_GROUPS, S5_STATE), 0.01)
    s5_log_step = unif((L, S5_GROUPS), math.log(1e-3), math.log(1e-1))
    s5_b_re = nrm((L, S5_GROUPS, S5_STATE, S5_GROUP_CH), (2.0 * S5_GROUP_CH) ** -0.5)
    s5_b_im = nrm((L, S5_GROUPS, S5_STATE, S5_GROUP_CH), (2.0 * S5_GROUP_CH) ** -0.5)
    s5_c_re = nrm((L, S5_GROUPS, S5_GROUP_CH, S5_STATE), 0.5)
    s5_c_im = nrm((L, S5_GROUPS, S5_GROUP_CH, S5_STATE), 0.5)
    s5_d = nrm((L, W), 0.5)
    s5_glu_w = nrm((L, W, W), W ** -0.5)
    s5_glu_b = nrm((L, W), 0.01)
    lru_conv_w = nrm((L, LRU_CONV, W), LRU_CONV ** -0.5)
    lru_conv_b = nrm((L, W), 0.01)
    lru_wa = nrm((L, LRU_HEADS, LRU_HD, LRU_HD), LRU_HD ** -0.5)
    lru_ba = nrm((L, LRU_HEADS, LRU_HD), 0.01)
    lru_wx = nrm((L, LRU_HEADS, LRU_HD, LRU_HD), LRU_HD ** -0.5)
    lru_bx = nrm((L, LRU_HEADS, LRU_HD), 0.01)
    a0 = unif((L, W), 0.9, 0.999) ** (1.0 / LRU_C)
    lru_lambda = jnp.log(a0) - jnp.log1p(-a0)
    merge_gate_w = nrm((L, D, N_BRANCH * D), D ** -0.5)
    merge_gate_b = nrm((L, N_BRANCH * D), 0.01)
    branch_w = nrm((L, N_BRANCH, W, D), W ** -0.5)
    w_out = nrm((L, D, D), D ** -0.5)
    norm2_g = 1.0 + nrm((L, D), 0.02)
    router_group_w = nrm((L, D, N_GROUPS), D ** -0.5)
    router_group_b = nrm((L, N_GROUPS), 0.01)
    router_expert_w = nrm((L, D, N_EXPERTS), D ** -0.5)
    router_expert_b = nrm((L, N_EXPERTS), 0.01)
    expert_w1 = nrm((L, N_EXPERTS, D, D_EXPERT), D ** -0.5)
    expert_w3 = nrm((L, N_EXPERTS, D, D_EXPERT), D ** -0.5)
    expert_w2 = nrm((L, N_EXPERTS, D_EXPERT, D), D_EXPERT ** -0.5)
    final_norm_g = 1.0 + nrm((D,), 0.02)
    return {
        "x": x, "norm1_g": norm1_g, "w_in": w_in, "conv_a_w": conv_a_w,
        "pool_w": pool_w, "pool_b": pool_b, "pool_scale": pool_scale,
        "s5_lambda_re": s5_lambda_re, "s5_lambda_im": s5_lambda_im, "s5_log_step": s5_log_step,
        "s5_b_re": s5_b_re, "s5_b_im": s5_b_im, "s5_c_re": s5_c_re, "s5_c_im": s5_c_im,
        "s5_d": s5_d, "s5_glu_w": s5_glu_w, "s5_glu_b": s5_glu_b,
        "lru_conv_w": lru_conv_w, "lru_conv_b": lru_conv_b, "lru_wa": lru_wa, "lru_ba": lru_ba,
        "lru_wx": lru_wx, "lru_bx": lru_bx, "lru_lambda": lru_lambda,
        "merge_gate_w": merge_gate_w, "merge_gate_b": merge_gate_b, "branch_w": branch_w, "w_out": w_out,
        "norm2_g": norm2_g, "router_group_w": router_group_w, "router_group_b": router_group_b,
        "router_expert_w": router_expert_w, "router_expert_b": router_expert_b,
        "expert_w1": expert_w1, "expert_w3": expert_w3, "expert_w2": expert_w2,
        "final_norm_g": final_norm_g,
    }

def reference(x, norm1_g, w_in, conv_a_w, pool_w, pool_b, pool_scale,
              s5_lambda_re, s5_lambda_im, s5_log_step, s5_b_re, s5_b_im, s5_c_re, s5_c_im,
              s5_d, s5_glu_w, s5_glu_b, lru_conv_w, lru_conv_b, lru_wa, lru_ba, lru_wx, lru_bx, lru_lambda,
              merge_gate_w, merge_gate_b, branch_w, w_out, norm2_g,
              router_group_w, router_group_b, router_expert_w, router_expert_b,
              expert_w1, expert_w3, expert_w2, final_norm_g):
    h = x
    for l in range(DEPTH):
        xn = rms_norm(h, norm1_g[l])
        h = h + hybrid_mixer(xn, w_in[l], conv_a_w[l], pool_w[l], pool_b[l], pool_scale[l],
                             s5_lambda_re[l], s5_lambda_im[l], s5_log_step[l], s5_b_re[l], s5_b_im[l],
                             s5_c_re[l], s5_c_im[l], s5_d[l], s5_glu_w[l], s5_glu_b[l],
                             lru_conv_w[l], lru_conv_b[l], lru_wa[l], lru_ba[l], lru_wx[l], lru_bx[l], lru_lambda[l],
                             merge_gate_w[l], merge_gate_b[l], branch_w[l], w_out[l])
        xn = rms_norm(h, norm2_g[l])
        h = h + hier_moe(xn, router_group_w[l], router_group_b[l], router_expert_w[l], router_expert_b[l],
                         expert_w1[l], expert_w3[l], expert_w2[l])
    return rms_norm(h, final_norm_g)


_drawn_inputs = setup_inputs


def setup_inputs(seed=0):
    import zlib

    import numpy as np

    out = dict(_drawn_inputs(seed))
    spreads = {}
    factors = {'pool_b': 4.077,
     'pool_scale': 3.086,
     's5_lambda_re': 64.0,
     's5_glu_b': 64.0,
     'lru_ba': 57.208,
     'lru_bx': 61.257,
     'merge_gate_b': 6.692,
     'router_group_b': 13.586,
     'router_expert_b': 14.796,
     'final_norm_g': 7.197,
     's5_lambda_im': 3.225,
     's5_log_step': 3.409,
     's5_b_re': 4.188,
     's5_b_im': 3.875,
     's5_c_re': 4.076,
     's5_c_im': 3.955,
     's5_glu_w': 4.44,
     'lru_conv_b': 3.62,
     'norm2_g': 3.028}
    for name, (base, spread) in spreads.items():
        noise = np.random.default_rng([zlib.crc32(name.encode()), seed]).standard_normal(out[name].shape)
        drawn = base * np.exp(spread * noise) if base else spread * noise
        out[name] = __import__('jax').numpy.asarray(drawn.astype(out[name].dtype))
    for name, factor in factors.items():
        out[name] = (out[name] * factor).astype(out[name].dtype)
    return out
```

```python
import math
from contextlib import ExitStack

import concourse.bass as bass
from concourse import mybir

F32 = mybir.dt.float32
F32R = mybir.dt.float32r
I32 = mybir.dt.int32
U32 = mybir.dt.uint32
ALU = mybir.AluOpType
ACT = mybir.ActivationFunctionType
AX = mybir.AxisListType
ds = bass.ds

P = 128
T = 2048
D = 1024
KD = D // P
TT = T // P
W = 256
NF = 14
NBR = 4
G, EPG = 4, 8
E = G * EPG
DE = 512
FE = DE // P
R = G + E
NB = T * 2 // P + E
EPS = 1e-6
GELU_C = 0.044715
GELU_S = math.sqrt(2.0 / math.pi)
MAGIC = 12582912.0


class Ring:

    def __init__(self, full, free, banks, uses):
        self.full, self.free, self.banks, self.uses = full, free, banks, list(uses)
        assert len(self.uses) % len(banks) == 0
        self.per = len(self.uses)

    def bank(self, use):
        return self.banks[self.uses.index(use) % len(self.banks)]

    def turn(self, use):
        return self.uses.index(use) + 1


class Steps:

    def __init__(self, eng, sem, per=0):
        self.eng, self.sem, self.per, self.n, self.base = eng, sem, per, 0, 0

    def trip(self, base):
        self.base, self.n = base, 0

    def mark(self, inst):
        inst.then_inc(self.sem, 1)
        self.n += 1

    def settle(self):
        self.eng.wait_ge(self.sem, self.base + self.n)

    def link(self, inst):
        self.mark(inst)
        self.settle()


def rsqrt_steps(dve, s, mean_sq, half, y, t):
    s.link(dve.tensor_scalar(y.bitcast(I32), mean_sq.bitcast(I32), -0.5, 1597463007.0, ALU.mult, ALU.add))
    s.link(dve.tensor_scalar(half, mean_sq, -0.5, None, ALU.mult))
    for _ in range(4):
        s.link(dve.tensor_tensor(t, y, y, ALU.mult))
        s.link(dve.tensor_tensor(t, t, half, ALU.mult))
        s.link(dve.scalar_tensor_tensor(y, t, 1.5, y, ALU.add, ALU.mult))


def horner(dve, s, out, x, coefs):
    s.link(dve.tensor_scalar(out, x, coefs[-1], None, ALU.mult))
    for c in coefs[-2::-1]:
        s.link(dve.scalar_tensor_tensor(out, out, c, x, ALU.add, ALU.mult))


def exp_exact(dve, s, out, x, n, f, pw):
    s.link(dve.tensor_scalar(f, x, -87.0, 88.0, ALU.max, ALU.min))
    s.link(dve.tensor_scalar(n, f, 1.0 / math.log(2.0), MAGIC, ALU.mult, ALU.add))
    s.link(dve.tensor_scalar(n, n, -MAGIC, None, ALU.add))
    s.link(dve.scalar_tensor_tensor(f, n, -0.693359375, f, ALU.mult, ALU.add))
    s.link(dve.scalar_tensor_tensor(f, n, 2.12194440e-4, f, ALU.mult, ALU.add))
    s.link(dve.tensor_scalar(pw, n, 127.0, 8388608.0, ALU.add, ALU.mult))
    horner(dve, s, out, f, [1.0 / math.factorial(k) for k in range(1, 9)])
    s.link(dve.scalar_tensor_tensor(out, out, 1.0, pw.bitcast(F32), ALU.add, ALU.mult))


def mix_branches(nc, io, dram):
    CT = 512
    CH = T // CT
    TC = CT // P
    NS = 8
    MAXW = 16
    FIRST_F = [8, 9, 10, 11]
    SLOT_F = [12, 13, 6, 7, 2, 0, 4, 3, 1, 5]
    DVE_STEPS = 108
    POOL_STEPS = 48

    with ExitStack() as ctx:
        def sb(name, shape, dt=F32):
            return ctx.enter_context(nc.sbuf_tensor(name, shape, dt))

        def sem(name):
            return ctx.enter_context(nc.semaphore(name))

        ps = [ctx.enter_context(nc.psum_tensor(f"mixps{i}", [P, CT], F32)) for i in range(8)]
        g_uses = [("t", t, h) for t in range(TC) for h in range(2)] + [("f", f) for f in FIRST_F]
        b_uses = []
        for n, f in enumerate(SLOT_F):
            (b_uses if f in (4, 5) else g_uses).append(("f", f))
            if n == 1:
                g_uses += [("r", 0), ("i", 0), ("r", 1), ("i", 1)]
            if n == 5:
                b_uses += [("pool", 0), ("pool", 1)]
        g_uses += [("glu", 0), ("glu", 1)]
        gr = Ring(sem("act_tile_full"), sem("act_tile_free"), ps[0:2], g_uses)
        br = Ring(sem("dve_tile_full"), sem("dve_tile_free"), ps[2:4], b_uses)
        sre, sim_, yps = ps[4], ps[5], ps[6]

        NW = 7
        win = sb("win", [P, NW, KD, P])
        g1 = sb("g1", [P, D])
        ident = sb("ident", [P, P])
        lamre, lamim = sb("lamre", [P, NS]), sb("lamim", [P, NS])
        ex = sb("ex", [P, NS + 2])
        lst = sb("lst", [P, 2 * NS])
        exo = sb("exo", [P, NS + 2])
        BT = [sb(f"BT{i}", [P, 2, P]) for i in range(2)]
        CTr = [sb(f"CTr{i}", [P, 2, P]) for i in range(2)]
        bd = sb("bd", [P, 3, 2, P])
        glw = sb("glw", [P, 2, W])
        cwa = sb("cwa", [P, 3, 2])
        cwl = sb("cwl", [P, 4, 2])
        vec = sb("vec", [P, 8, 2])
        LCB, PB, PSC, SD, GB, BA, BX, LAM = range(8)
        m4sp = sb("m4sp", [P, 2])
        invw, wcol = sb("invw", [P, 2]), sb("wcol", [P, 2])
        corr = sb("corr", [P, 2, MAXW])
        io16 = sb("io16", [P, MAXW], I32)
        tcos, tsin = sb("tcos", [P, NS, CT]), sb("tsin", [P, NS, CT])
        rdec = sb("rdec", [P, NS])
        pari = sb("pari", [P, NS + 2], I32)
        gpar = sb("gpar", [P, 2], I32)
        gmask = sb("gmask", [P, 2])

        xin = sb("xin", [P, TC, D])
        ssq, rst, rtmp, rhalf = sb("ssq", [P, TC]), sb("rst", [P, TC]), sb("rtmp", [P, TC]), sb("rhalf", [P, TC])
        msq = sb("msq", [P, TC])
        xT = sb("xT", [P, KD, CT])
        b_nat = [xT[:, i, 0:NS * 16].rearrange("p (s h) -> p s h", h=16) for i in range(2)]
        c_nat = [xT[:, 2 + i, 0:P].rearrange("p (u h) -> p u h", u=2) for i in range(2)]
        par = xT[:, 4, 0:24 * NS].rearrange("p (i s) -> p i s", s=NS)
        bgcg = sb("bgcg", [P, 4, CT])
        va = sb("va", [P, 2, CT + 2])
        pu = sb("pu", [P, 2, CT + MAXW - 1])
        pw_ = [sb(f"pw{i}", [P, CT + MAXW - 1]) for i in range(2)]
        su = sb("su", [P, 2, CT])
        lx = sb("lx", [P, 2, CT + 3])
        xc = sb("xc", [P, 2, CT])
        lg = sb("lg", [P, 2, CT])
        lru = sb("lru", [P, 2, 4, CT])
        hcar = sb("hcar", [P, 2])
        m = sb("m", [P, 8, CT])
        hst = sb("hst", [P, 2, 2, CT])
        scar = sb("scar", [P, 2, NS])
        ys = sb("ys", [P, NBR, 2, CT])
        yg, yq = su, sb("yq", [P, 2, CT])
        lq = yq

        par_in, bd_zero, bd_in = sem("params_in"), sem("diag_zero"), sem("diag_in")
        win_in = [sem(f"win_in{i}") for i in range(NW)]
        F_ORDER = FIRST_F + SLOT_F
        assert NF % NW == 0
        consts, idz = sem("consts"), sem("ident_zero")
        pre, pre_t, pre_tt, pre_a = sem("prep_steps"), sem("bc_ready"), sem("bc_turned"), sem("bc_copied")
        unit_rot, tabs = sem("unit_rotation"), sem("tables_steps")
        x_in = [sem(f"x_in{i}") for i in range(TC)]
        sq_done, xh_full, xT_out = sem("square_sum"), sem("xhat_full"), sem("xT_out")
        proj = sem("proj_evacuated")
        dstep, astep, pstep = sem("dve_step"), sem("act_step"), sem("pool_step")
        pooled, xc_full = sem("pooled_full"), sem("xc_full")
        lru_a, lru_q, lru_m, gl_u, gl_t = sem("lru_acts"), sem("lru_q"), sem("lru_root"), sem("gate_poly"), sem("gate_tanh")
        s_full, s_free, rot_in, scan_d, rot_m, h_full = (sem("bu_full"), sem("bu_free"), sem("bu_products"), sem("scans_in"),
                                                        sem("state_products"), sem("state_full"))
        y_full, y_free, y_pre, y_sq, y_u, y_t, yg_full, glu_t = (sem("y_full"), sem("y_free"), sem("y_pre"), sem("y_sq"),
                                                               sem("y_poly"), sem("y_tanh"), sem("y_gelu"), sem("glu_tanh"))
        ys_full, ys_out = sem("ys_full"), [sem(f"ys_out{i}") for i in range(NBR)]
        passed = sem("mix_passed")
        block = ctx.enter_context(nc.Block())

        GPER, BPER = gr.per, br.per
        PROJ = [("f", f) for f in (FIRST_F + SLOT_F) if f not in (4, 5)]
        NPROJ = len(PROJ)

        @block.sync
        def _(sp):
            n = [0]

            def load(dst, src):
                sp.dma_start(dst, src, allow_slow_non_contiguous=True).then_inc(par_in, 16)
                n[0] += 16

            for t in range(TC):
                sp.dma_start(xin[:, t], io["x"][0, t * P:(t + 1) * P, :]).then_inc(x_in[t], 16)
            load(g1[:], io["norm1_g"][0:1].partition_broadcast(P))
            load(lst[:], io["s5_log_step"][0:1].partition_broadcast(P))
            for q in range(2):
                rows = slice(64 * q, 64 * q + 64)
                load(lamre[rows, :], io["s5_lambda_re"][0].rearrange("(s q) p -> q p s", q=2)[q])
                load(lamim[rows, :], io["s5_lambda_im"][0].rearrange("(s q) p -> q p s", q=2)[q])
                load(b_nat[0][rows], io["s5_b_re"][0].rearrange("(s q) p h -> q p s h", q=2)[q])
                load(b_nat[1][rows], io["s5_b_im"][0].rearrange("(s q) p h -> q p s h", q=2)[q])
            for i, nm in enumerate(("s5_c_re", "s5_c_im")):
                for u in range(2):
                    load(c_nat[i][:, u], io[nm][0, 8 * u:8 * u + 8].rearrange("g h p -> (g h) p"))
            load(glw[:], io["s5_glu_w"][0].rearrange("(k p) n -> p k n", p=P))
            load(cwa[:], io["conv_a_w"][0].rearrange("k (j p) -> p k j", p=P))
            load(cwl[:], io["lru_conv_w"][0].rearrange("k (j p) -> p k j", p=P))
            for i, nm in enumerate(("lru_conv_b", "pool_b", "pool_scale", "s5_d", "s5_glu_b", "lru_ba", "lru_bx", "lru_lambda")):
                v = io[nm][0]
                if len(v.shape) == 2:
                    v = v.rearrange("a b -> (a b)")
                load(vec[:, i, :], v.rearrange("(j p) -> p j", p=P))
            sp.wait_ge(bd_zero, 1)
            for i, nm in enumerate(("pool_w", "lru_wa", "lru_wx")):
                for g in range(4):
                    q = 64 * (g % 2)
                    sp.dma_start(bd[q:q + 64, i, g // 2, q:q + 64], io[nm][0, g]).then_inc(bd_in, 16)

            def load_win(i):
                f = F_ORDER[i]
                sp.dma_start(win[:, i % NW], io["w_in"][0, :, f * P:(f + 1) * P].rearrange("(k p) n -> p k n", p=P))\
                  .then_inc(win_in[i % NW], 16)

            for i in range(NW):
                load_win(i)
            io["n_params"] = n[0]
            for i in range(NBR):
                sp.sem_inc(ys_out[i], 16)
            sp.sem_inc(xT_out, 16)
            with sp.Fori(0, CH) as c:
                nxt = (c + 1) % CH
                gb = sp.snap(c * GPER)
                bb = sp.snap(c * BPER)

                def used(i):
                    f = F_ORDER[i]
                    if f in (4, 5):
                        sp.wait_ge(br.full, bb + br.turn(("f", f)))
                    else:
                        sp.wait_ge(gr.full, gb + gr.turn(("f", f)))

                for t in range(TC):
                    sp.wait_ge(gr.full, gb + gr.turn(("t", t, 1)))
                    sp.dma_start(xin[:, t], io["x"][0, ds(nxt * CT + t * P, P), :]).then_inc(x_in[t], 16)
                sp.wait_ge(gr.free, gb + gr.turn(("t", TC - 1, 1)) + 2)
                sp.dma_start(dram["xT"][:, :, ds(c * CT, CT)].rearrange("k p t -> p k t"), xT[:]).then_inc(xT_out, 16)
                for i in range(NF):
                    used(i)
                    load_win((i + NW) % NF)
                for i, b in enumerate((3, 1, 0, 2)):
                    sp.wait_ge(ys_full, c * 8 + 2 * i + 2)
                    sp.dma_start(dram["ys"][b, :, :, ds(c * CT, CT)].rearrange("j p t -> p j t"), ys[:, b]).then_inc(ys_out[b], 16)
            for i in range(NW):
                sp.wait_ge(win_in[i], 16 * (1 + CH * NF // NW))
            sp.wait_ge(xT_out, 16 * (CH + 1))
            for i in range(NBR):
                sp.wait_ge(ys_out[i], 16 * (CH + 1))
            for t in range(TC):
                sp.wait_ge(x_in[t], 16 * (CH + 1))

        n_params = io["n_params"]

        @block.gpsimd
        def _(pool):
            pool.memset(bd[:], 0.0).then_inc(bd_zero, 1)
            pool.memset(ident[:], 0.0).then_inc(idz, 1)
            pool.wait_ge(idz, 1)
            pool.affine_select(out=ident[:], in_=ident[:], compare_op=ALU.not_equal, fill=1.0, base=0,
                               pattern=[[-1, P]], channel_multiplier=1).then_inc(consts, 1)
            pool.iota(gpar[:, 0:1], [[0, 1]], base=0, channel_multiplier=1).then_inc(consts, 1)
            pool.iota(io16[:], [[1, MAXW]], base=1, channel_multiplier=0).then_inc(consts, 1)
            pool.wait_ge(unit_rot, 2)
            ts = Steps(pool, tabs)
            k = 1
            while k < CT:
                t1 = ys[:, 0:2].rearrange("p a b t -> p (a b t)")[:, 0:NS * k].rearrange("p (s t) -> p s t", s=NS)
                t2 = ys[:, 2:4].rearrange("p a b t -> p (a b t)")[:, 0:NS * k].rearrange("p (s t) -> p s t", s=NS)
                zc = tcos[:, :, k - 1:k].to_broadcast([P, NS, k])
                zs = tsin[:, :, k - 1:k].to_broadcast([P, NS, k])
                ts.mark(pool.tensor_tensor(t1, tcos[:, :, 0:k], zc, ALU.mult))
                ts.link(pool.tensor_tensor(t2, tsin[:, :, 0:k], zs, ALU.mult))
                ts.link(pool.tensor_tensor(tcos[:, :, k:2 * k], t1, t2, ALU.subtract))
                ts.mark(pool.tensor_tensor(t1, tsin[:, :, 0:k], zc, ALU.mult))
                ts.link(pool.tensor_tensor(t2, tcos[:, :, 0:k], zs, ALU.mult))
                ts.link(pool.tensor_tensor(tsin[:, :, k:2 * k], t1, t2, ALU.add))
                k *= 2
            io["n_tabs"] = ts.n
            with pool.Fori(0, CH) as c:
                for s in range(NS):
                    pool.wait_ge(rot_in, c * NS + s + 1)
                    pool.tensor_tensor(m[:, 0], m[:, 0], m[:, 1], ALU.add).then_inc(scan_d, 1)
                    pool.tensor_tensor(m[:, 2], m[:, 2], m[:, 3], ALU.subtract).then_inc(scan_d, 1)
                    pool.wait_ge(rot_m, c * NS + s + 1)
                    if s >= 2:
                        pool.wait_ge(y_full, c * NS + s - 1)
                    pool.tensor_tensor(hst[:, s % 2, 0], m[:, 4], m[:, 5], ALU.subtract).then_inc(pstep, 1)
                    pool.tensor_tensor(hst[:, s % 2, 1], m[:, 6], m[:, 7], ALU.add).then_inc(pstep, 1)
                    pool.wait_ge(pstep, c * 2 * NS + 2 * s + 2)
                    pool.sem_inc(passed, 1)
                    pool.tensor_copy(scar[:, 0:1, s], hst[:, s % 2, 0, CT - 1:CT]).then_inc(h_full, 1)
                    pool.tensor_copy(scar[:, 1:2, s], hst[:, s % 2, 1, CT - 1:CT]).then_inc(h_full, 1)

        n_tabs = io["n_tabs"]

        @block.scalar
        def _(act):
            act.sem_inc(gr.free, 2)
            act.wait_ge(pre_tt, 1)
            for i in range(2):
                for u in range(2):
                    act.activation(BT[i][:, u], ps[i][:, u * P:(u + 1) * P], ACT.Copy).then_inc(pre_a, 1)
                    act.activation(CTr[i][:, u], ps[2 + i][:, u * P:(u + 1) * P], ACT.Copy,
                                   scale=(1.0 if i == 0 else -1.0)).then_inc(pre_a, 1)
            with act.Fori(0, CH) as c:
                gb = act.snap(c * GPER)
                for t in range(TC):
                    act.wait_ge(x_in[t], c * 16 + 16)
                    act.activation(lru[:, t // 2, 2 * (t % 2):2 * (t % 2) + 2, :].rearrange("p a b -> p (a b)"), xin[:, t], ACT.Square,
                                   accum_out=ssq[:, t:t + 1]).then_inc(sq_done, 1)
                act.wait_ge(xT_out, 16 * c + 16)
                for t in range(TC):
                    for h in range(2):
                        act.wait_ge(gr.full, gb + gr.turn(("t", t, h)))
                        act.activation(xT[:, 4 * h:4 * h + 4, t * P:(t + 1) * P],
                                       gr.bank(("t", t, h))[:].rearrange("p (k t) -> p k t", k=4), ACT.Copy).then_inc(gr.free, 1)

                def evac(dst, f):
                    act.wait_ge(gr.full, gb + gr.turn(("f", f)))
                    act.activation(dst, gr.bank(("f", f))[:], ACT.Copy).then_inc(gr.free, 1)

                DST = {0: bgcg[:, 0], 1: bgcg[:, 1], 2: bgcg[:, 2], 3: bgcg[:, 3],
                       6: pu[:, 0, MAXW - 1:], 7: pu[:, 1, MAXW - 1:], 8: su[:, 0], 9: su[:, 1],
                       10: lx[:, 0, 3:], 11: lx[:, 1, 3:], 12: lg[:, 0], 13: lg[:, 1]}
                for f in FIRST_F:
                    evac(DST[f], f)
                for n, f in enumerate(SLOT_F):
                    if f in (4, 5):
                        continue
                    if f in (12, 13):
                        act.wait_ge(gr.full, gb + gr.turn(("f", f)))
                        act.activation(lq[:, f - 12], gr.bank(("f", f))[:], ACT.Square).then_inc(lru_a, 1)
                    evac(DST[f], f)
                    if n == 1:
                        for j in range(2):
                            for i, nm in enumerate(("r", "i")):
                                act.wait_ge(gr.full, gb + gr.turn((nm, j)))
                                act.activation(lru[:, j, i], gr.bank((nm, j))[:], ACT.Tanh, scale=0.5,
                                               bias=vec[:, BA + i, j:j + 1]).then_inc(gr.free, 1)
                            act.wait_ge(gr.free, gb + gr.turn(("i", j)) + 2)
                            act.activation(lru[:, j, 2], lru[:, j, 0], ACT.Exp, scale=m4sp[:, j:j + 1],
                                           bias=m4sp[:, j:j + 1]).then_inc(astep, 1)
                            act.wait_ge(astep, c * 2 + j + 1)
                            act.activation(lru[:, j, 0], lru[:, j, 0], ACT.Tanh, scale=m4sp[:, j:j + 1],
                                           bias=m4sp[:, j:j + 1]).then_inc(lru_a, 1)
                            act.activation(lru[:, j, 3], lru[:, j, 2], ACT.Square).then_inc(lru_a, 1)
                    if n == 3:
                        for j in range(2):
                            act.wait_ge(gl_u, c * 2 + j + 1)
                            act.activation(lq[:, j], lq[:, j], ACT.Tanh, scale=GELU_S).then_inc(gl_t, 1)
                    if n == 5:
                        for j in range(2):
                            act.wait_ge(lru_q, c * 2 + j + 1)
                            act.activation(lru[:, j, 3], lru[:, j, 3], ACT.Sqrt, scale=-0.25).then_inc(lru_m, 1)
                for j in range(2):
                    act.wait_ge(y_pre, c * 2 + j + 1)
                    act.activation(yq[:, j], yg[:, j], ACT.Square).then_inc(y_sq, 1)
                for j in range(2):
                    act.wait_ge(y_u, c * 2 + j + 1)
                    act.activation(yq[:, j], yq[:, j], ACT.Tanh, scale=GELU_S).then_inc(y_t, 1)
                for j in range(2):
                    act.wait_ge(gr.full, gb + gr.turn(("glu", j)))
                    act.activation(yq[:, j], gr.bank(("glu", j))[:], ACT.Tanh, scale=0.25,
                                   bias=vec[:, GB, j:j + 1]).then_inc(gr.free, 1)

        @block.tensor
        def _(pe):
            pe.wait_ge(consts, 3)
            pe.wait_ge(pre_t, 1)
            for i in range(2):
                for u in range(2):
                    pe.transpose(ps[i][:, u * P:(u + 1) * P], m[:, i, u * P:(u + 1) * P], ident[:])
                    last = pe.transpose(ps[2 + i][:, u * P:(u + 1) * P], m[:, 2 + i, u * P:(u + 1) * P], ident[:])
            last.then_inc(pre_tt, 1)
            pe.wait_ge(pre_a, 8)
            pe.wait_ge(par_in, n_params)
            pe.wait_ge(bd_in, 16 * 12)
            with pe.Fori(0, CH) as c:
                gb = pe.snap(c * GPER)
                bb = pe.snap(c * BPER)
                sb_ = pe.snap(c * NS)

                def project(f):
                    ring, base = (br, bb) if f in (4, 5) else (gr, gb)
                    i = F_ORDER.index(f)
                    pe.wait_ge(win_in[i % NW], 16 * (NF // NW) * c + 16 * (i // NW + 1))
                    pe.wait_ge(ring.free, base + ring.turn(("f", f)))
                    for k in range(KD):
                        last = pe.matmul(ring.bank(("f", f))[:], win[:, i % NW, k], xT[:, k, :],
                                         start=(k == 0), stop=(k == KD - 1))
                    last.then_inc(ring.full, 1)

                for t in range(TC):
                    pe.wait_ge(xh_full, c * TC + t + 1)
                    for h in range(2):
                        pe.wait_ge(gr.free, gb + gr.turn(("t", t, h)))
                        for k in range(4):
                            last = pe.transpose(gr.bank(("t", t, h))[:, k * P:(k + 1) * P],
                                                xin[:, t, (4 * h + k) * P:(4 * h + k + 1) * P], ident[:])
                        last.then_inc(gr.full, 1)
                pe.wait_ge(gr.free, gb + 2 * TC + 2)
                project(8)
                project(9)
                project(10)
                project(11)
                pe.wait_ge(gr.free, gb + gr.turn(("f", 9)) + 2)
                for n, f in enumerate(SLOT_F):
                    if n < NS:
                        s, u, q = n, n // 4, 32 * (n % 4)
                        pe.wait_ge(s_free, sb_ + s + 1)
                        pe.matmul(sre[:], BT[0][q:q + 32, u, :], su[q:q + 32, u, :], start=True, stop=True)
                        pe.matmul(sim_[:], BT[1][q:q + 32, u, :], su[q:q + 32, u, :], start=True, stop=True).then_inc(s_full, 1)
                    project(f)
                    if n == 1:
                        for j in range(2):
                            pe.wait_ge(xc_full, c * 2 + j + 1)
                            for i, nm in enumerate(("r", "i")):
                                pe.wait_ge(gr.free, gb + gr.turn((nm, j)))
                                pe.matmul(gr.bank((nm, j))[:], bd[:, 1 + i, j], xc[:, j], start=True, stop=True).then_inc(gr.full, 1)
                    if n == 5:
                        for j in range(2):
                            pe.wait_ge(pooled, c * 2 + j + 1)
                            pe.wait_ge(br.free, bb + br.turn(("pool", j)))
                            pe.matmul(br.bank(("pool", j))[:], bd[:, 0, j], ys[:, 1, j], start=True, stop=True).then_inc(br.full, 1)
                    if n >= 2:
                        s = n - 2
                        u, q = s // 4, 32 * (s % 4)
                        if s % 4 == 0:
                            pe.wait_ge(y_free, c * 2 + u + 1)
                        pe.wait_ge(h_full, 2 * sb_ + 2 * s + 2)
                        pe.matmul(yps[q:q + 32, :], CTr[0][:, u, q:q + 32], hst[:, s % 2, 0], start=True, stop=False)
                        last = pe.matmul(yps[q:q + 32, :], CTr[1][:, u, q:q + 32], hst[:, s % 2, 1], start=False, stop=True)
                        last.then_inc(y_full, 1)
                pe.wait_ge(yg_full, c * 2 + 2)
                for j in range(2):
                    pe.wait_ge(gr.free, gb + gr.turn(("glu", j)))
                    for k in range(2):
                        last = pe.matmul(gr.bank(("glu", j))[:], glw[:, k, j * P:(j + 1) * P], yg[:, k],
                                         start=(k == 0), stop=(k == 1))
                    last.then_inc(gr.full, 1)

        @block.vector
        def _(dve):
            s = Steps(dve, pre)
            for b in range(2):
                dve.sem_inc(br.free, 1)
            dve.sem_inc(s_free, 1)
            dve.sem_inc(y_free, 1)
            for z in (va[:, :, 0:2], pu[:, :, 0:MAXW - 1], lx[:, :, 0:3], hcar[:], scar[:], m[:, 0:4, :]):
                s.mark(dve.memset(z, 0.0))
            for j in range(2):
                for q in range(2):
                    w = float(2 ** (2 * j + q + 1))
                    s.mark(dve.memset(wcol[64 * q:64 * q + 64, j:j + 1], w))
                    s.mark(dve.memset(invw[64 * q:64 * q + 64, j:j + 1], 1.0 / w))
            dve.wait_ge(consts, 3)
            dve.wait_ge(par_in, n_params)
            s.settle()
            pt = lambda i: par[:, i, :]
            for q in range(2):
                s.mark(dve.tensor_copy(ex[64 * q:64 * q + 64, 0:NS],
                                       lst[64 * q:64 * q + 64, :].rearrange("p (s q) -> p q s", q=2)[:, q]))
            for i in (BA, BX, GB):
                s.mark(dve.tensor_scalar(vec[:, i, :], vec[:, i, :], 0.5, None, ALU.mult))
            for j in range(2):
                cj = corr[:, j, :]
                s.link(dve.tensor_copy(cj, io16[:]))
                s.link(dve.tensor_scalar(cj, cj, wcol[:, j:j + 1], None, ALU.min))
                s.link(dve.reciprocal(cj, cj))
                s.link(dve.tensor_scalar(cj, cj, wcol[:, j:j + 1], None, ALU.mult))
            s.link(dve.tensor_scalar(gpar[:, 1:2], gpar[:, 0:1], 4, 1, ALU.logical_shift_right, ALU.bitwise_and))
            s.link(dve.tensor_copy(gmask[:, 1:2], gpar[:, 1:2]))
            s.link(dve.tensor_scalar(gmask[:, 0:1], gmask[:, 1:2], -1.0, 1.0, ALU.mult, ALU.add))
            neg, mabs = par[:, 0, 0:2], ex[:, NS:NS + 2]
            s.link(dve.tensor_scalar(neg, vec[:, LAM, :], -1.0, None, ALU.mult))
            s.link(dve.tensor_tensor(mabs, neg, vec[:, LAM, :], ALU.min))
            nn, ff = par[:, 1:3, :].rearrange("p a b -> p (a b)")[:, 0:NS + 2], par[:, 3:5, :].rearrange("p a b -> p (a b)")[:, 0:NS + 2]
            exp_exact(dve, s, exo[:], ex[:], nn, ff, pari[:])
            e_, z, z2, po = exo[:, NS:NS + 2], par[:, 5, 0:2], par[:, 6, 0:2], par[:, 7, 0:2]
            s.link(dve.tensor_scalar(z, e_, 2.0, None, ALU.add))
            s.link(dve.reciprocal(z, z))
            s.link(dve.tensor_tensor(z, z, e_, ALU.mult))
            s.link(dve.tensor_tensor(z2, z, z, ALU.mult))
            horner(dve, s, po, z2, [1.0 / k for k in range(3, 17, 2)])
            s.link(dve.scalar_tensor_tensor(po, po, 1.0, z, ALU.add, ALU.mult))
            s.link(dve.tensor_scalar(neg, neg, 0.0, None, ALU.max))
            s.link(dve.scalar_tensor_tensor(po, po, 2.0, neg, ALU.mult, ALU.add))
            s.link(dve.tensor_scalar(m4sp[:], po, -4.0, None, ALU.mult))
            LR, X, TH, Q, V, V2, SN, CS, ER, CM1, ST, CO, AR, AI, DEN, CRE, CIM, T1, T2 = range(0, 19)
            step = exo[:, 0:NS]
            s.link(dve.tensor_scalar(pt(LR), lamre[:], -1e-4, None, ALU.min))
            s.link(dve.tensor_tensor(pt(X), pt(LR), step, ALU.mult))
            s.link(dve.tensor_tensor(pt(TH), lamim[:], step, ALU.mult))
            s.link(dve.tensor_scalar(pt(Q), pt(TH), 1.0 / (2 * math.pi), MAGIC, ALU.mult, ALU.add))
            s.link(dve.tensor_scalar(pt(Q), pt(Q), -MAGIC, None, ALU.add))
            s.link(dve.tensor_scalar(pt(V), pt(TH), 0.5, None, ALU.mult))
            pi1 = 3.140625
            pi2 = 9.670257568359375e-4
            pi3 = math.pi - pi1 - pi2
            for pc in (pi1, pi2, pi3):
                s.link(dve.scalar_tensor_tensor(pt(V), pt(Q), -pc, pt(V), ALU.mult, ALU.add))
            s.link(dve.tensor_tensor(pt(V2), pt(V), pt(V), ALU.mult))
            horner(dve, s, pt(SN), pt(V2), [(-1.0) ** k / math.factorial(2 * k + 1) for k in range(1, 8)])
            s.link(dve.scalar_tensor_tensor(pt(SN), pt(SN), 1.0, pt(V), ALU.add, ALU.mult))
            horner(dve, s, pt(CS), pt(V2), [(-1.0) ** k / math.factorial(2 * k) for k in range(1, 9)])
            s.link(dve.tensor_scalar(pt(CS), pt(CS), 1.0, None, ALU.add))
            s.link(dve.tensor_tensor(pt(CM1), pt(SN), pt(SN), ALU.mult))
            s.link(dve.tensor_scalar(pt(CM1), pt(CM1), -2.0, None, ALU.mult))
            s.link(dve.tensor_tensor(pt(ST), pt(SN), pt(CS), ALU.mult))
            s.link(dve.tensor_scalar(pt(ST), pt(ST), 2.0, None, ALU.mult))
            s.link(dve.tensor_scalar(pt(CO), pt(CM1), 1.0, None, ALU.add))
            dve.tensor_copy(tcos[:, :, 0:1], pt(CO).unsqueeze(2)).then_inc(unit_rot, 1)
            dve.tensor_copy(tsin[:, :, 0:1], pt(ST).unsqueeze(2)).then_inc(unit_rot, 1)
            s.link(dve.tensor_scalar(pt(T1), pt(X), -88.0, 1.0 / 128, ALU.max, ALU.mult))
            horner(dve, s, pt(ER), pt(T1), [1.0 / math.factorial(k) for k in range(1, 11)])
            for _ in range(7):
                s.link(dve.scalar_tensor_tensor(pt(ER), pt(ER), 2.0, pt(ER), ALU.add, ALU.mult))
            s.link(dve.tensor_scalar(rdec[:], pt(ER), 1.0, None, ALU.add))
            s.link(dve.tensor_tensor(pt(AR), pt(ER), pt(CO), ALU.mult))
            s.link(dve.tensor_tensor(pt(AR), pt(AR), pt(CM1), ALU.add))
            s.link(dve.tensor_tensor(pt(AI), rdec[:], pt(ST), ALU.mult))
            s.link(dve.tensor_tensor(pt(T1), pt(LR), pt(LR), ALU.mult))
            s.link(dve.tensor_tensor(pt(DEN), lamim[:], lamim[:], ALU.mult))
            s.link(dve.tensor_tensor(pt(DEN), pt(DEN), pt(T1), ALU.add))
            s.link(dve.reciprocal(pt(DEN), pt(DEN)))
            s.link(dve.tensor_tensor(pt(T1), pt(AR), pt(LR), ALU.mult))
            s.link(dve.tensor_tensor(pt(T2), pt(AI), lamim[:], ALU.mult))
            s.link(dve.tensor_tensor(pt(CRE), pt(T1), pt(T2), ALU.add))
            s.link(dve.tensor_tensor(pt(CRE), pt(CRE), pt(DEN), ALU.mult))
            s.link(dve.tensor_tensor(pt(T1), pt(AI), pt(LR), ALU.mult))
            s.link(dve.tensor_tensor(pt(T2), pt(AR), lamim[:], ALU.mult))
            s.link(dve.tensor_tensor(pt(CIM), pt(T1), pt(T2), ALU.subtract))
            s.link(dve.tensor_tensor(pt(CIM), pt(CIM), pt(DEN), ALU.mult))
            cre = pt(CRE).unsqueeze(2).to_broadcast([P, NS, 16])
            cim = pt(CIM).unsqueeze(2).to_broadcast([P, NS, 16])
            tb = [m[:, 4 + i, 0:NS * 16].rearrange("p (s h) -> p s h", h=16) for i in range(4)]
            s.mark(dve.tensor_tensor(tb[0], b_nat[0], cre, ALU.mult))
            s.mark(dve.tensor_tensor(tb[1], b_nat[1], cim, ALU.mult))
            s.mark(dve.tensor_tensor(tb[2], b_nat[1], cre, ALU.mult))
            s.link(dve.tensor_tensor(tb[3], b_nat[0], cim, ALU.mult))
            for q in range(2):
                rows = slice(64 * q, 64 * q + 64)
                for i, op in enumerate((ALU.subtract, ALU.add)):
                    dst = m[rows, i, 0:2 * P].rearrange("p (s h) -> p s h", h=32)[:, :, 16 * q:16 * q + 16]
                    s.link(dve.tensor_tensor(dst, tb[2 * i][rows], tb[2 * i + 1][rows], op))
            for i in range(2):
                for q in range(2):
                    dst = m[:, 2 + i, 0:2 * P].rearrange("p (u w) -> p u w", w=P)[:, :, 64 * q:64 * q + 64]
                    s.link(dve.tensor_scalar(dst, c_nat[i], gmask[:, q:q + 1], None, ALU.mult))
            dve.sem_inc(pre_t, 1)
            dve.wait_ge(pre_tt, 1)
            dve.wait_ge(tabs, n_tabs)
            dve.sem_inc(passed, 1)

            s = Steps(dve, dstep, DVE_STEPS)
            with dve.Fori(0, CH) as c:
                s.trip(dve.snap(c * DVE_STEPS))
                gb = dve.snap(c * GPER)
                bb = dve.snap(c * BPER)
                cs = dve.snap(c * NS)
                c2 = dve.snap(c * 2)
                dve.wait_ge(sq_done, c * TC + TC)
                s.link(dve.tensor_scalar(msq[:], ssq[:], 1.0 / D, EPS, ALU.mult, ALU.add))
                rsqrt_steps(dve, s, msq[:], rhalf[:], rst[:], rtmp[:])
                for t in range(TC):
                    dve.scalar_tensor_tensor(xin[:, t], xin[:, t], rst[:, t:t + 1], g1[:], ALU.mult, ALU.mult).then_inc(xh_full, 1)

                def stood(f):
                    dve.wait_ge(gr.free, gb + gr.turn(("f", f)) + 2)

                for j in range(2):
                    stood(10 + j)
                    s.link(dve.tensor_scalar(xc[:, j], lx[:, j, 3:3 + CT], cwl[:, 3, j:j + 1], vec[:, LCB, j:j + 1], ALU.mult, ALU.add))
                    for k in (2, 1, 0):
                        i = dve.scalar_tensor_tensor(xc[:, j], lx[:, j, k:k + CT], cwl[:, k, j:j + 1], xc[:, j], ALU.mult, ALU.add)
                        if k:
                            s.link(i)
                    i.then_inc(xc_full, 1)
                dve.wait_ge(xc_full, c2 + 2)
                s.mark(dve.tensor_copy(lx[:, :, 0:3], lx[:, :, CT:CT + 3]))

                def s5_in(n):
                    dve.wait_ge(s_full, cs + n + 1)
                    dve.tensor_tensor(m[:, 0], sre[:], tcos[:, n], ALU.mult)
                    s.mark(dve.tensor_tensor(m[:, 1], sim_[:], tsin[:, n], ALU.mult))
                    dve.tensor_tensor(m[:, 2], sim_[:], tcos[:, n], ALU.mult)
                    s.link(dve.tensor_tensor(m[:, 3], sre[:], tsin[:, n], ALU.mult))
                    dve.sem_inc(s_free, 1)
                    dve.sem_inc(rot_in, 1)

                def s5_scan(n):
                    dve.wait_ge(scan_d, 2 * cs + 2 * n + 2)
                    r = rdec[:, n:n + 1].to_broadcast([P, CT])
                    s.mark(dve.tensor_tensor_scan(m[:, 1], r, m[:, 0], scar[:, 0, n:n + 1], ALU.mult, ALU.add))
                    s.link(dve.tensor_tensor_scan(m[:, 3], r, m[:, 2], scar[:, 1, n:n + 1], ALU.mult, ALU.add))
                    dve.wait_ge(h_full, 2 * cs + 2 * n) if n else None
                    dve.tensor_tensor(m[:, 4], m[:, 1], tcos[:, n], ALU.mult)
                    s.mark(dve.tensor_tensor(m[:, 5], m[:, 3], tsin[:, n], ALU.mult))
                    dve.tensor_tensor(m[:, 6], m[:, 3], tcos[:, n], ALU.mult)
                    s.link(dve.tensor_tensor(m[:, 7], m[:, 1], tsin[:, n], ALU.mult))
                    dve.sem_inc(rot_m, 1)

                def lru_gate_poly():
                    for j in range(2):
                        stood(12 + j)
                        s.link(dve.tensor_scalar(lq[:, j], lq[:, j], GELU_C, 1.0, ALU.mult, ALU.add))
                        dve.tensor_tensor(lq[:, j], lq[:, j], lg[:, j], ALU.mult).then_inc(gl_u, 1)

                def lru_q_():
                    for j in range(2):
                        dve.wait_ge(lru_a, c * 6 + 2 + 2 * j + 2)
                        dve.scalar_tensor_tensor(lru[:, j, 3], lru[:, j, 3], 1.0, lru[:, j, 0], ALU.add, ALU.mult).then_inc(lru_q, 1)

                def lru_out():
                    dve.wait_ge(ys_out[3], 16 * c + 16)
                    for j in range(2):
                        dve.wait_ge(lru_m, c2 + j + 1)
                        s.link(dve.scalar_tensor_tensor(lru[:, j, 1], lru[:, j, 1], 1.0, xc[:, j], ALU.add, ALU.mult))
                        s.link(dve.tensor_tensor(lru[:, j, 1], lru[:, j, 1], lru[:, j, 3], ALU.mult))
                        s.link(dve.tensor_tensor_scan(lru[:, j, 0], lru[:, j, 2], lru[:, j, 1], hcar[:, j:j + 1], ALU.mult, ALU.add))
                        s.mark(dve.tensor_copy(hcar[:, j:j + 1], lru[:, j, 0, CT - 1:CT]))
                        dve.wait_ge(gl_t, c2 + j + 1)
                        s.link(dve.scalar_tensor_tensor(lg[:, j], lq[:, j], 1.0, lg[:, j], ALU.add, ALU.mult))
                        dve.scalar_tensor_tensor(ys[:, 3, j], lru[:, j, 0], 0.5, lg[:, j], ALU.mult, ALU.mult).then_inc(ys_full, 1)

                def pool_mix():
                    dve.wait_ge(ys_out[1], 16 * c + 16)
                    H = MAXW - 1
                    N = CT + H
                    for j in range(2):
                        stood(6 + j)
                        u = pu[:, j]
                        a, b = pw_[0], pw_[1]
                        if j == 0:
                            s.mark(dve.tensor_tensor(b[0:64, H:N], u[0:64, H:N], u[0:64, H - 1:N - 1], ALU.add))
                            s.link(dve.tensor_tensor(a[64:P, 1:N], u[64:P, 1:N], u[64:P, 0:N - 1], ALU.add))
                            s.link(dve.tensor_tensor(b[64:P, H:N], a[64:P, H:N], a[64:P, H - 2:N - 2], ALU.add))
                        else:
                            s.link(dve.tensor_tensor(a[:, 1:N], u[:, 1:N], u[:, 0:N - 1], ALU.add))
                            s.link(dve.tensor_tensor(b[:, 3:N], a[:, 3:N], a[:, 1:N - 2], ALU.add))
                            s.link(dve.tensor_tensor(a[:, 7:N], b[:, 7:N], b[:, 3:N - 4], ALU.add))
                            s.mark(dve.tensor_copy(b[0:64, H:N], a[0:64, H:N]))
                            s.link(dve.tensor_tensor(b[64:P, H:N], a[64:P, H:N], a[64:P, H - 8:N - 8], ALU.add))
                        s.link(dve.tensor_tensor(b[:, H:H + MAXW], b[:, H:H + MAXW], corr[:, j], ALU.mult))
                        dve.scalar_tensor_tensor(ys[:, 1, j], b[:, H:N], invw[:, j:j + 1], u[:, H:N], ALU.mult, ALU.subtract).then_inc(pooled, 1)
                        dve.wait_ge(pooled, c2 + j + 1)
                    s.mark(dve.tensor_copy(pu[:, :, 0:H], pu[:, :, CT:N]))
                    s.mark(dve.memset(corr[:], 1.0))

                def pool_out():
                    for j in range(2):
                        dve.wait_ge(br.full, bb + br.turn(("pool", j)))
                        s.link(dve.tensor_scalar(ys[:, 1, j], br.bank(("pool", j))[:], vec[:, PB, j:j + 1], vec[:, PSC, j:j + 1], ALU.add, ALU.mult))
                        dve.sem_inc(br.free, 1)
                        dve.sem_inc(ys_full, 1)

                def conv_a(j):
                    stood(2 + j)
                    dve.wait_ge(br.full, bb + br.turn(("f", 4 + j)))
                    dve.tensor_tensor(va[:, j, 2:2 + CT], br.bank(("f", 4 + j))[:], bgcg[:, 2 + j], ALU.mult).then_inc(br.free, 1)
                    dve.wait_ge(br.free, bb + br.turn(("f", 4 + j)) + 2)
                    y = pw_[j][:, 0:CT]
                    s.link(dve.tensor_scalar(y, va[:, j, 2:2 + CT], cwa[:, 2, j:j + 1], None, ALU.mult))
                    for k in (1, 0):
                        s.link(dve.scalar_tensor_tensor(y, va[:, j, k:k + CT], cwa[:, k, j:j + 1], y, ALU.mult, ALU.add))
                    stood(j)
                    if j == 0:
                        dve.wait_ge(ys_out[0], 16 * c + 16)
                    dve.tensor_tensor(ys[:, 0, j], y, bgcg[:, j], ALU.mult).then_inc(ys_full, 1)
                    s.mark(dve.tensor_copy(va[:, j, 0:2], va[:, j, CT:CT + 2]))

                def y_in(u):
                    dve.wait_ge(y_full, cs + 4 * u + 4)
                    dve.scalar_tensor_tensor(yg[:, u], su[:, u], vec[:, SD, u:u + 1], yps[:], ALU.mult, ALU.add).then_inc(y_free, 1)
                    dve.wait_ge(y_free, c2 + u + 2)
                    dve.sem_inc(y_pre, 1)

                for n in range(10):
                    if n >= 1 and n <= NS:
                        s5_scan(n - 1)
                    if n < NS:
                        s5_in(n)
                    if n == 1:
                        lru_gate_poly()
                    if n == 2:
                        lru_q_()
                    if n == 4:
                        pool_mix()
                    if n == 6:
                        y_in(0)
                        lru_out()
                        pool_out()
                    if n == 7:
                        conv_a(0)
                    if n == 9:
                        y_in(1)
                for j in range(2):
                    dve.wait_ge(y_sq, c2 + j + 1)
                    s.link(dve.tensor_scalar(yq[:, j], yq[:, j], GELU_C, 1.0, ALU.mult, ALU.add))
                    dve.tensor_tensor(yq[:, j], yq[:, j], yg[:, j], ALU.mult).then_inc(y_u, 1)
                conv_a(1)
                for j in range(2):
                    dve.wait_ge(y_t, c2 + j + 1)
                    dve.scalar_tensor_tensor(yg[:, j], yq[:, j], 1.0, yg[:, j], ALU.add, ALU.mult).then_inc(yg_full, 1)
                dve.wait_ge(ys_out[2], 16 * c + 16)
                for j in range(2):
                    dve.wait_ge(gr.free, gb + gr.turn(("glu", j)) + 2)
                    dve.wait_ge(yg_full, c2 + 2)
                    s.link(dve.scalar_tensor_tensor(yq[:, j], yq[:, j], 1.0, yg[:, j], ALU.add, ALU.mult))
                    dve.tensor_scalar(ys[:, 2, j], yq[:, j], 0.25, None, ALU.mult).then_inc(ys_full, 1)
                assert s.n == DVE_STEPS, s.n


def merge_branches(nc, io, dram, logits):
    TM = 512
    TRIPS = T // TM
    MT = TM // P
    RSQ = 14
    NORM_STEPS = 1 + RSQ
    STEP_DVE = NBR - 1
    TRIP_DVE = KD * STEP_DVE + MT * NORM_STEPS
    WK = KD + 2
    PIECE = 4
    PIECES = (KD + 2 * NBR) // PIECE
    SU = NBR
    assert PIECES == MT == 4
    with ExitStack() as ctx:
        def sb(name, shape, dt=F32):
            return ctx.enter_context(nc.sbuf_tensor(name, shape, dt))

        def sem(name):
            return ctx.enter_context(nc.semaphore(name))

        ps = [ctx.enter_context(nc.psum_tensor(f"mrgps{i}", [P, 512], F32)) for i in range(5)]
        act_hi, act_lo = sb("act_hi", [P, KD + 2 * NBR, TM], F32R), sb("act_lo", [P, KD + 2 * NBR, TM], F32R)
        act_raw = sb("act_raw", [P, 2, PIECE * TM])
        merged = sb("merged", [P, KD, TM])
        wout = sb("wout", [P, KD, D])
        w_raw = sb("w_raw", [P, NBR, WK, P])
        w_hi, w_lo = sb("w_hi", [P, 2, WK, P], F32R), sb("w_lo", [P, 2, WK, P], F32R)
        gt, tmp = sb("gt", [P, TM]), sb("tmp", [P, TM])
        xr, xn = sb("xr", [P, 2, D]), sb("xn", [P, 2, D])
        xnT = sb("xnT", [P, KD, P])
        sqj = sb("sqj", [P, D])
        g2 = sb("g2", [P, D])
        rw = sb("rw", [P, KD, R])
        rb = sb("rb", [P, R])
        mb = sb("mb", [P, NBR, KD])
        ident = sb("m_ident", [P, P])
        ssq, msq, rst, rh, rt = (sb(f"m_st{i}", [P, 2]) for i in range(5))

        GPER = BPER = KD * SU + 2 * MT
        g_full, g_free, b_full, b_free = sem("gate_full"), sem("gate_free"), sem("prod_full"), sem("prod_free")
        gbank, bbank, rps = ps[0:2], ps[2:4], ps[4]
        r_full, r_free = sem("router_full"), sem("router_free")
        par_in, idz, idn = sem("m_params_in"), sem("m_ident_zero"), sem("m_ident")
        w_in, w_hi_set, w_split = [sem(f"mw_in{k}") for k in range(NBR)], sem("w_hi_set"), sem("w_split")
        act_in, act_hi_set, act_split = [sem(f"acts_in{i}") for i in range(2)], sem("act_hi_set"), sem("act_split")
        wout_in = sem("wout_in")
        x_in, h_out, n_out = ([sem(f"{n}{i}") for i in range(2)] for n in ("xr_in", "h_out", "n_out"))
        h_done, sq_done, n_full = sem("h_done"), sem("h_squared"), sem("xn_full")
        half_b, dstep, passed = sem("half_bias"), sem("m_dve_step"), sem("m_passed")
        block = ctx.enter_context(nc.Block())

        params = ((mb[:], io["merge_gate_b"][0].rearrange("(k d p) -> p k d", k=NBR, p=P)),
                  (g2[:], io["norm2_g"][0:1].partition_broadcast(P)),
                  (rw[:, :, 0:G], io["router_group_w"][0].rearrange("(k p) n -> p k n", p=P)),
                  (rw[:, :, G:R], io["router_expert_w"][0].rearrange("(k p) n -> p k n", p=P)),
                  (rb[:, 0:G], io["router_group_b"][0:1].partition_broadcast(P)),
                  (rb[:, G:R], io["router_expert_b"][0:1].partition_broadcast(P)))

        @block.sync
        def _(sp):
            def load_piece(m, c):
                cols = ds(m * TM, TM)
                if c < PIECES // 2:
                    src = dram["xT"][PIECE * c:PIECE * (c + 1), :, cols].rearrange("k p t -> p k t")
                else:
                    b = 2 * (c - PIECES // 2)
                    src = dram["ys"][b:b + 2, :, :, cols].rearrange("b j p t -> p (b j) t")
                sp.dma_start(act_raw[:, c % 2].rearrange("p (k t) -> p k t", t=TM), src).then_inc(act_in[c % 2], 16)

            def load_weights(k, d):
                sp.dma_start(w_raw[:, k, 0:KD], io["merge_gate_w"][0, :, ds(k * D + d * P, P)].rearrange("(k p) n -> p k n", p=P))\
                  .then_inc(w_in[k], 16)
                sp.dma_start(w_raw[:, k, KD:WK], io["branch_w"][0, k, :, ds(d * P, P)].rearrange("(k p) n -> p k n", p=P))\
                  .then_inc(w_in[k], 16)

            load_piece(0, 0)
            load_weights(0, 0)
            load_piece(0, 1)
            for k in range(1, NBR):
                load_weights(k, 0)
            for c in range(2, PIECES):
                sp.wait_ge(act_split, c - 1)
                load_piece(0, c)
            for dst, src in params:
                sp.dma_start(dst, src, allow_slow_non_contiguous=True).then_inc(par_in, 16)
            sp.dma_start(wout[:], io["w_out"][0].rearrange("(k p) n -> p k n", p=P)).then_inc(wout_in, 16)
            for i in range(2):
                sp.sem_inc(h_out[i], 16)
                sp.sem_inc(n_out[i], 16)
            with sp.Fori(0, TRIPS) as m:
                with sp.Fori(0, KD) as d:
                    for k in range(NBR):
                        sp.wait_ge(w_split, (m * KD + d) * SU + (k + 1))
                        load_weights(k, (d + 1) % KD)
                m8 = sp.snap(m * MT)

                def load_x(t):
                    sp.wait_ge(h_out[t % 2], 16 * (MT // 2) * m + 16 * (t // 2) + 16)
                    sp.dma_start(xr[:, t % 2], io["x"][0, ds(m * TM + t * P, P), :]).then_inc(x_in[t % 2], 16)

                load_x(0)
                load_x(1)
                for c in range(2):
                    sp.wait_ge(act_split, m * PIECES + (PIECES + c - 1))
                    load_piece((m + 1) % TRIPS, c)
                for t in range(MT):
                    if t + 2 < PIECES:
                        sp.wait_ge(act_split, m * PIECES + (PIECES + t + 1))
                        load_piece((m + 1) % TRIPS, t + 2)
                    sp.wait_ge(h_done, m8 + t + 1)
                    sp.dma_start(dram["h"][ds(m * TM + t * P, P), :], xr[:, t % 2]).then_inc(h_out[t % 2], 16)
                    sp.wait_ge(n_full, m8 + t + 1)
                    sp.dma_start(dram["xn"][ds(m * TM + t * P, P), :], xn[:, t % 2]).then_inc(n_out[t % 2], 16)
                    if t + 2 < MT:
                        load_x(t + 2)
            for i in range(2):
                sp.wait_ge(h_out[i], 16 + 16 * TRIPS * MT // 2)
                sp.wait_ge(n_out[i], 16 + 16 * TRIPS * MT // 2)
            for k in range(NBR):
                sp.wait_ge(w_in[k], 32 * (1 + TRIPS * KD))

        @block.gpsimd
        def _(pool):
            pool.memset(ident[:], 0.0).then_inc(idz, 1)
            pool.wait_ge(idz, 1)
            pool.affine_select(out=ident[:], in_=ident[:], compare_op=ALU.not_equal, fill=1.0, base=0,
                               pattern=[[-1, P]], channel_multiplier=1).then_inc(idn, 1)

        @block.scalar
        def _(act):
            act.sem_inc(g_free, 2)

            def piece_high(n, c):
                act.wait_ge(act_in[c % 2], n * 16)
                act.sem_inc(passed, 1)
                act.activation(act_hi[:, PIECE * c:PIECE * (c + 1)].rearrange("p k t -> p (k t)"), act_raw[:, c % 2],
                               ACT.Copy).then_inc(act_hi_set, 1)

            def weights_high(n, k):
                act.wait_ge(w_in[k], n * 32)
                act.sem_inc(passed, 1)
                act.activation(w_hi[:, k % 2].rearrange("p k n -> p (k n)"), w_raw[:, k].rearrange("p k n -> p (k n)"),
                               ACT.Copy).then_inc(w_hi_set, 1)

            piece_high(1, 0)
            weights_high(1, 0)
            for c in range(1, PIECES):
                piece_high(c // 2 + 1, c)
            act.wait_ge(half_b, 1)
            with act.Fori(0, TRIPS) as m:
                with act.Fori(0, KD) as d:
                    gb = act.snap(m * GPER + d * SU)
                    md = act.snap(m * KD + d)
                    for k in range(NBR):
                        act.wait_ge(b_free, gb + k + 2)
                        weights_high(md + (1 if k + 1 < NBR else 2), (k + 1) % NBR)
                        act.wait_ge(g_full, gb + k + 1)
                        act.sem_inc(passed, 1)
                        act.activation(gt[:], gbank[k % 2][:], ACT.Tanh, scale=0.5, bias=mb[:, k, ds(d, 1)]).then_inc(g_free, 1)
                gb = act.snap(m * GPER + KD * SU)
                m8 = act.snap(m * MT)

                def square(t):
                    act.wait_ge(h_done, m8 + t + 1)
                    act.wait_ge(sq_done, m8 + t + 1)
                    act.activation(sqj[:], xr[:, t % 2], ACT.Square, accum_out=ssq[:, t % 2:t % 2 + 1]).then_inc(sq_done, 1)

                def turn(t):
                    act.wait_ge(r_full, m8 + t + 1)
                    for h in range(2):
                        act.wait_ge(g_full, gb + 2 * t + h + 1)
                        act.activation(xnT[:, 4 * h:4 * h + 4, :].rearrange("p k t -> p (k t)"), gbank[h][:],
                                       ACT.Copy).then_inc(g_free, 1)

                act.wait_ge(b_free, gb + 2)
                piece_high(m * 2 + 3, 0)
                square(0)
                for t in range(1, MT):
                    piece_high(m * 2 + (t // 2 + 3), t)
                    square(t)
                    turn(t - 1)
                turn(MT - 1)

        @block.tensor
        def _(pe):
            pe.sem_inc(r_full, 1)
            pe.wait_ge(idn, 1)
            with pe.Fori(0, TRIPS) as m:
                pe.wait_ge(act_split, m * PIECES + KD // PIECE)
                pe.sem_inc(passed, 1)
                with pe.Fori(0, KD) as d:
                    base = pe.snap(m * GPER + d * SU)
                    first = pe.snap((m * KD + d) * SU)
                    pieces = pe.snap(m * PIECES + PIECES)

                    def product(bank, k, w_tiles, a_tile):
                        for kk in w_tiles:
                            a = a_tile + kk - w_tiles[0]
                            for w, x in ((w_hi, act_hi), (w_hi, act_lo), (w_lo, act_hi)):
                                last = pe.matmul(bank[:], w[:, k % 2, kk], x[:, a], start=(kk == w_tiles[0] and x is act_hi and w is w_hi),
                                                 stop=(kk == w_tiles[-1] and w is w_lo))
                        return last

                    for k in range(NBR):
                        pe.wait_ge(w_split, first + k + 1)
                        pe.wait_ge(g_free, base + k + 1)
                        product(gbank[k % 2], k, range(KD), 0).then_inc(g_full, 1)
                        if k == 0:
                            pe.wait_ge(act_split, pieces)
                        pe.wait_ge(b_free, base + k + 1)
                        product(bbank[k % 2], k, range(KD, WK), KD + 2 * k).then_inc(b_full, 1)
                base = pe.snap(m * GPER + KD * SU)
                m8 = pe.snap(m * MT)

                def project(t):
                    for h in range(2):
                        pe.wait_ge(b_free, base + 2 * t + h + 1)
                        for kk in range(KD):
                            last = pe.matmul(bbank[h][:], merged[:, kk, t * P:(t + 1) * P], wout[:, kk, h * 512:(h + 1) * 512],
                                             start=(kk == 0), stop=(kk == KD - 1))
                        last.then_inc(b_full, 1)

                def turn(t):
                    pe.wait_ge(n_full, m8 + t + 1)
                    for h in range(2):
                        pe.wait_ge(g_free, base + 2 * t + h + 1)
                        for kk in range(4):
                            last = pe.transpose(gbank[h][:, kk * P:(kk + 1) * P], xn[:, t % 2, (4 * h + kk) * P:(4 * h + kk + 1) * P], ident[:])
                        last.then_inc(g_full, 1)

                def rout(t):
                    pe.wait_ge(g_free, base + 2 * t + 4)
                    pe.wait_ge(r_free, m8 + t + 1)
                    for kk in range(KD):
                        last = pe.matmul(rps[:, 0:R], xnT[:, kk], rw[:, kk], start=(kk == 0), stop=(kk == KD - 1))
                    last.then_inc(r_full, 1)

                pe.wait_ge(wout_in, 16)
                pe.wait_ge(par_in, 16 * len(params))
                pe.wait_ge(dstep, m * TRIP_DVE + KD * STEP_DVE)
                project(0)
                for t in range(1, MT):
                    project(t)
                    if t >= 2:
                        rout(t - 2)
                    turn(t - 1)
                rout(MT - 2)
                turn(MT - 1)
                rout(MT - 1)

        @block.vector
        def _(dve):
            dve.sem_inc(b_free, 2)
            dve.sem_inc(r_free, 1)
            dve.sem_inc(sq_done, 1)

            def piece_low(n, c):
                dve.wait_ge(act_hi_set, n)
                hi = act_hi[:, PIECE * c:PIECE * (c + 1)].rearrange("p k t -> p (k t)")
                dve.tensor_tensor(act_lo[:, PIECE * c:PIECE * (c + 1)].rearrange("p k t -> p (k t)"), act_raw[:, c % 2],
                                  hi.bitcast(F32), ALU.subtract).then_inc(act_split, 1)

            def weights_low(n, k):
                dve.wait_ge(w_hi_set, n)
                hi, lo = (w[:, k % 2].rearrange("p k n -> p (k n)") for w in (w_hi, w_lo))
                dve.tensor_tensor(lo, w_raw[:, k].rearrange("p k n -> p (k n)"), hi.bitcast(F32), ALU.subtract).then_inc(w_split, 1)

            piece_low(1, 0)
            weights_low(1, 0)
            for c in range(1, PIECES):
                piece_low(c + 1, c)
            dve.wait_ge(par_in, 16 * len(params))
            dve.tensor_scalar(mb[:], mb[:], 0.5, None, ALU.mult).then_inc(half_b, 1)
            s = Steps(dve, dstep)
            with dve.Fori(0, TRIPS) as m:
                with dve.Fori(0, KD) as d:
                    gb = dve.snap(m * GPER + d * SU)
                    s.trip(dve.snap(m * TRIP_DVE + d * STEP_DVE))
                    first = dve.snap((m * KD + d) * SU)
                    acc = merged[:, ds(d, 1), :].rearrange("p a t -> p (a t)")
                    for k in range(NBR):
                        weights_low(first + k + 2, (k + 1) % NBR)
                        dve.wait_ge(b_full, gb + k + 1)
                        dve.wait_ge(g_free, gb + k + 3)
                        if k == 0:
                            dve.scalar_tensor_tensor(acc, gt[:], 1.0, bbank[k % 2][:], ALU.add, ALU.mult).then_inc(b_free, 1)
                        else:
                            dve.scalar_tensor_tensor(tmp[:], gt[:], 1.0, bbank[k % 2][:], ALU.add, ALU.mult).then_inc(b_free, 1)
                            dve.wait_ge(b_free, gb + k + 3)
                            s.link(dve.tensor_tensor(acc, acc, tmp[:], ALU.add))
                gb = dve.snap(m * GPER + KD * SU)
                m8 = dve.snap(m * MT)
                s.trip(dve.snap(m * TRIP_DVE + KD * STEP_DVE))

                def residual(t):
                    dve.wait_ge(x_in[t % 2], 16 * (MT // 2) * m + 16 * (t // 2) + 16)
                    for h in range(2):
                        half = xr[:, t % 2, h * 512:(h + 1) * 512]
                        dve.wait_ge(b_full, gb + 2 * t + h + 1)
                        dve.scalar_tensor_tensor(half, bbank[h][:], 0.5, half, ALU.mult, ALU.add).then_inc(b_free, 1)
                    dve.wait_ge(b_free, gb + 2 * t + 4)
                    dve.sem_inc(h_done, 1)

                def norm(t):
                    p = t % 2
                    one = slice(p, p + 1)
                    dve.wait_ge(sq_done, m8 + t + 2)
                    s.link(dve.tensor_scalar(msq[:, one], ssq[:, one], 1.0 / D, EPS, ALU.mult, ALU.add))
                    rsqrt_steps(dve, s, msq[:, one], rh[:, one], rst[:, one], rt[:, one])
                    if t >= 2:
                        dve.wait_ge(g_full, gb + 2 * (t - 2) + 2)
                    dve.wait_ge(n_out[p], 16 * (MT // 2) * m + 16 * (t // 2) + 16)
                    dve.scalar_tensor_tensor(xn[:, p], xr[:, p], rst[:, one], g2[:], ALU.mult, ALU.mult).then_inc(n_full, 1)

                def logit(t):
                    dve.wait_ge(r_full, m8 + t + 2)
                    dve.tensor_tensor(logits[:, ds(m8 + t, 1), :].rearrange("p a r -> p (a r)"), rps[:, 0:R], rb[:], ALU.add).then_inc(r_free, 1)

                pieces = dve.snap(m * PIECES + PIECES)
                piece_low(pieces + 1, 0)
                residual(0)
                for t in range(1, MT):
                    piece_low(pieces + (t + 1), t)
                    residual(t)
                    norm(t - 1)
                    if t >= 3:
                        logit(t - 3)
                norm(MT - 1)
                for t in range(MT - 3, MT):
                    logit(t)
                assert s.n == MT * NORM_STEPS, s.n


def route(nc, logits, table, pos, wts, ends):
    with ExitStack() as ctx:
        def sb(name, shape, dt=F32):
            return ctx.enter_context(nc.sbuf_tensor(name, shape, dt))

        def sem(name):
            return ctx.enter_context(nc.semaphore(name))

        rank_ps, tot_ps, tab_ps = (ctx.enter_context(nc.psum_tensor(f"rtps{i}", [P, 512], F32)) for i in range(3))
        NBT = NB + 1
        gmax, gsum, gval = (sb(f"rt_g{i}", [P, TT]) for i in range(3))
        gd, geq = sb("gd", [P, TT, G]), sb("geq", [P, TT, G])
        gi, m1, m2, dd = (sb(f"rt_m{i}", [P, TT]) for i in range(4))
        em, eq = sb("em", [P, TT, E]), sb("eq", [P, TT, E])
        oh = [sb(f"oh{i}", [P, TT, E]) for i in range(2)]
        hot = sb("hot", [P, TT, E])
        io_g, io_e, io_s, io_b, io_tok, io_blk = (sb("io_g", [P, G]), sb("io_e", [P, E]), sb("io_s", [P, P]), sb("io_b", [P, NBT]),
                                                  sb("io_tok", [P, TT]), sb("io_blk", [P, TT]))
        tri, ones = sb("tri", [P, P]), sb("ones", [P, P])
        cum, tot = sb("cum", [P, TT, E]), sb("tot", [P, TT, E])
        cnt, nb, nbi, nbe, e1 = (sb(f"rt_c{i}", [P, E]) for i in range(5))
        big = sb("big", [P, E, TT])
        off = sb("off", [P, TT, E])
        posf = sb("posf", [P, TT, 2])
        posb, poss = sb("posb", [P, TT, 2], I32), sb("poss", [P, TT, 2], I32)
        blkf, slotf = sb("blkf", [P, TT, 2]), sb("slotf", [P, TT, 2])
        V, U = sb("V", [P, TT, 2, P]), sb("U", [P, TT, 2, NBT])
        consts, ones_set, step = sem("rt_consts"), sem("rt_ones"), sem("rt_steps")
        d_ready, e_done, d2_ready, e2_done = sem("group_diff"), sem("group_exp"), sem("expert_diff"), sem("expert_exp")
        hot_ready, ranks, uv_ready, tab_ready = sem("hot_ready"), sem("ranks"), sem("uv_ready"), sem("table_ready")
        block = ctx.enter_context(nc.Block())

        @block.gpsimd
        def _(pool):
            kw = dict(allow_small_or_imprecise_dtypes=True)
            pool.iota(io_g[:], [[1, G]], base=0, channel_multiplier=0, **kw).then_inc(consts, 1)
            pool.iota(io_e[:], [[1, E]], base=0, channel_multiplier=0, **kw).then_inc(consts, 1)
            pool.iota(io_s[:], [[1, P]], base=0, channel_multiplier=0, **kw).then_inc(consts, 1)
            pool.iota(io_b[:], [[1, NBT]], base=0, channel_multiplier=0, **kw).then_inc(consts, 1)
            pool.iota(io_tok[:], [[P, TT]], base=0, channel_multiplier=1, **kw).then_inc(consts, 1)
            pool.iota(io_blk[:], [[P, TT]], base=0, channel_multiplier=0, **kw).then_inc(consts, 1)
            pool.memset(ones[:], 1.0).then_inc(consts, 1)
            pool.wait_ge(consts, 7)
            pool.affine_select(out=tri[:], in_=ones[:], compare_op=ALU.is_gt, fill=0.0, base=0,
                               pattern=[[1, P]], channel_multiplier=-1).then_inc(consts, 1)

        @block.scalar
        def _(act):
            act.wait_ge(d_ready, 1)
            act.activation(geq[:], gd[:], ACT.Exp).then_inc(e_done, 1)
            act.wait_ge(d2_ready, 1)
            act.activation(dd[:], dd[:], ACT.Exp).then_inc(e2_done, 1)

        @block.tensor
        def _(pe):
            pe.wait_ge(consts, 8)
            pe.wait_ge(hot_ready, 1)
            h = hot[:].rearrange("p t e -> p (t e)")
            pe.matmul(rank_ps[:], tri[:], h, start=True, stop=True)
            pe.matmul(tot_ps[:], ones[:], h, start=True, stop=True).then_inc(ranks, 1)
            pe.wait_ge(uv_ready, 1)
            for i in range(TT):
                for k in range(2):
                    last = pe.matmul(tab_ps[:, 0:NBT], V[:, i, k], U[:, i, k], start=(i + k == 0), stop=(i == TT - 1 and k == 1))
            last.then_inc(tab_ready, 1)

        @block.vector
        def _(dve):
            s = Steps(dve, step)
            TTc = dve.tensor_tensor
            bc = lambda ap, n: ap.unsqueeze(2).to_broadcast([P, TT, n])
            row = lambda ap, n: ap.unsqueeze(1).to_broadcast([P, TT, n])
            lgG, lgE = logits[:, :, 0:G], logits[:, :, G:R]

            def first_hot(dst, vals, best, iota_row, n, tmpv, idx):
                s.link(TTc(tmpv, vals, bc(best, n), ALU.is_equal))
                s.link(dve.scalar_tensor_tensor(tmpv, tmpv, -64.0, row(iota_row, n), ALU.mult, ALU.add))
                s.link(dve.tensor_reduce(idx, tmpv, AX.X, ALU.min))
                s.link(dve.tensor_scalar(idx, idx, 64.0, None, ALU.add))
                s.link(TTc(dst, row(iota_row, n), bc(idx, n), ALU.is_equal))

            s.link(dve.tensor_reduce(gmax[:], lgG, AX.X, ALU.max))
            TTc(gd[:], lgG, bc(gmax[:], G), ALU.subtract).then_inc(d_ready, 1)
            dve.wait_ge(e_done, 1)
            s.link(dve.tensor_reduce(gsum[:], geq[:], AX.X, ALU.add))
            s.link(dve.reciprocal(gval[:], gsum[:]))
            dve.wait_ge(consts, 8)
            first_hot(gd[:], lgG, gmax[:], io_g[:], G, geq[:], gi[:])
            s.link(dve.tensor_scalar(gd[:], gd[:], -1.0, 1e30, ALU.add, ALU.mult))
            for g in range(G):
                s.mark(TTc(em[:, :, EPG * g:EPG * (g + 1)], lgE[:, :, EPG * g:EPG * (g + 1)],
                           gd[:, :, g:g + 1].to_broadcast([P, TT, EPG]), ALU.add))
            s.settle()
            s.link(dve.tensor_reduce(m1[:], em[:], AX.X, ALU.max))
            first_hot(oh[0][:], em[:], m1[:], io_e[:], E, eq[:], gi[:])
            s.link(dve.scalar_tensor_tensor(em[:], oh[0][:], -3e38, em[:], ALU.mult, ALU.add))
            s.link(dve.tensor_reduce(m2[:], em[:], AX.X, ALU.max))
            TTc(dd[:], m2[:], m1[:], ALU.subtract).then_inc(d2_ready, 1)
            first_hot(oh[1][:], em[:], m2[:], io_e[:], E, eq[:], gi[:])
            TTc(hot[:], oh[0][:], oh[1][:], ALU.add).then_inc(hot_ready, 1)
            dve.wait_ge(e2_done, 1)
            s.link(dve.tensor_scalar(gsum[:], dd[:], 1.0, None, ALU.add))
            s.link(dve.reciprocal(gsum[:], gsum[:]))
            s.link(TTc(gsum[:], gsum[:], gval[:], ALU.mult))
            s.mark(dve.tensor_copy(wts[:, :, 0], gsum[:]))
            s.mark(TTc(wts[:, :, 1], gsum[:], dd[:], ALU.mult))
            dve.wait_ge(ranks, 1)
            s.link(dve.tensor_copy(tot[:].rearrange("p t e -> p (t e)"), tot_ps[:]))
            s.link(dve.memset(cum[:, 0], 0.0))
            for i in range(1, TT):
                s.link(TTc(cum[:, i], cum[:, i - 1], tot[:, i - 1], ALU.add))
            s.link(TTc(cnt[:], cum[:, TT - 1], tot[:, TT - 1], ALU.add))
            s.link(TTc(big[:], cnt[:].unsqueeze(2).to_broadcast([P, E, TT]), io_blk[:].unsqueeze(1).to_broadcast([P, E, TT]), ALU.is_gt))
            s.link(dve.tensor_reduce(nb[:], big[:], AX.X, ALU.add))
            s.link(dve.tensor_scalar(nb[:], nb[:], 1.0, None, ALU.max))
            s.link(dve.memset(e1[:], 1.0))
            s.link(dve.tensor_tensor_scan(nbi[:], e1[:], nb[:], 0.0, ALU.mult, ALU.add))
            s.link(TTc(nbe[:], nbi[:], nb[:], ALU.subtract))
            s.mark(dve.memset(ends[:, 0:1], 0))
            s.mark(dve.tensor_copy(ends[:, 1:E + 1], nbi[:]))
            s.link(dve.tensor_scalar(nbe[:], nbe[:], float(P), None, ALU.mult))
            s.link(TTc(off[:].rearrange("p t e -> p (t e)"), rank_ps[:], cum[:].rearrange("p t e -> p (t e)"), ALU.add))
            s.link(TTc(off[:], off[:], row(nbe[:], E), ALU.add))
            for k in range(2):
                s.link(TTc(eq[:], oh[k][:], off[:], ALU.mult))
                s.link(dve.tensor_reduce(posf[:, :, k], eq[:], AX.X, ALU.add))
            s.link(dve.tensor_copy(pos[:], posf[:]))
            s.mark(dve.tensor_scalar(posb[:], pos[:], 7, None, ALU.logical_shift_right))
            s.link(dve.tensor_scalar(poss[:], pos[:], P - 1, None, ALU.bitwise_and))
            s.mark(dve.tensor_copy(blkf[:], posb[:]))
            s.link(dve.tensor_copy(slotf[:], poss[:]))
            for k in range(2):
                s.mark(TTc(V[:, :, k], row(io_s[:], P), bc(slotf[:, :, k], P), ALU.is_equal))
                s.link(TTc(U[:, :, k], row(io_b[:], NBT), bc(blkf[:, :, k], NBT), ALU.is_equal))
                s.link(TTc(U[:, :, k], U[:, :, k], bc(io_tok[:], NBT), ALU.mult))
            dve.sem_inc(uv_ready, 1)
            dve.wait_ge(tab_ready, 1)
            s.link(dve.tensor_copy(table[:], tab_ps[:, 0:NBT]))


def run_experts(nc, io, dram, table, ends):
    with ExitStack() as ctx:
        def sb(name, shape, dt=F32):
            return ctx.enter_context(nc.sbuf_tensor(name, shape, dt))

        def sem(name):
            return ctx.enter_context(nc.semaphore(name))

        ps = [ctx.enter_context(nc.psum_tensor(f"exps{i}", [P, 512], F32)) for i in range(6)]
        tbank, hbank, ybank = ps[0:2], ps[2:4], ps[4:6]
        w1, w3 = sb("w1", [P, 2, KD, DE]), sb("w3", [P, 2, KD, DE])
        w2 = sb("w2", [P, 2, FE, D])
        xg, xgT = sb("xg", [P, D]), sb("xgT", [P, KD, P])
        idx = sb("idx", [P, 1], I32)
        th = sb("th", [P, 2, 2 * P])
        gg = sb("gg", [P, 2, 2 * P])
        hT = sb("hT", [P, FE, P])
        ysb = sb("ysb", [P, 2, 512])
        ident = sb("x_ident", [P, P])
        zeros = sb("zeros", [P, D])
        zeros_set, zeros_out = sem("zeros_set"), sem("zeros_out")
        w_in = [sem(f"w_in{i}") for i in range(2)]
        idz, idn = sem("x_ident_zero"), sem("x_ident_set")
        idx_set, gathered, turned = sem("idx_set"), sem("gathered"), sem("x_turned")
        xT_full, h_ps, tanh_d, gate_d, h_full = sem("xgT_full"), sem("h_psum"), sem("h_tanh"), sem("h_gated"), sem("hT_full")
        y_ps, y_free, y_out = sem("y_psum"), sem("y_read"), [sem(f"y_out{i}") for i in range(2)]
        passed = sem("x_passed")
        block = ctx.enter_context(nc.Block())

        def bounds(eng, e):
            return (eng.value_load(ends[0:1, ds(e, 1)], min_val=0, max_val=NB),
                    eng.value_load(ends[0:1, ds(e + 1, 1)], min_val=1, max_val=NB))

        @block.sync
        def _(sp):
            def load(e, p):
                sp.dma_start(w1[:, p], io["expert_w1"][0, ds(e, 1)].rearrange("o (k p) n -> p (o k) n", p=P)).then_inc(w_in[p], 16)
                sp.dma_start(w3[:, p], io["expert_w3"][0, ds(e, 1)].rearrange("o (k p) n -> p (o k) n", p=P)).then_inc(w_in[p], 16)
                sp.dma_start(w2[:, p], io["expert_w2"][0, ds(e, 1)].rearrange("o (k p) n -> p (o k) n", p=P)).then_inc(w_in[p], 16)

            load(0, 0)
            load(1, 1)
            with sp.Fori(0, E // 2 - 1) as q:
                for p in range(2):
                    end = sp.value_load(ends[0:1, ds(q * 2 + (p + 1), 1)], min_val=1, max_val=NB)
                    sp.wait_ge(y_ps, end * 2)
                    load(q * 2 + (p + 2), p)
            total = sp.value_load(ends[0:1, E:E + 1], min_val=1, max_val=NB - 1)
            sp.wait_ge(zeros_set, 1)
            with sp.Fori(total, NB) as g:
                sp.dma_start(dram["y"][ds(g * P, P), :], zeros[:]).then_inc(zeros_out, 16)
            with sp.Fori(0, total) as g:
                sp.sem_inc(zeros_out, 16)
            sp.wait_ge(zeros_out, NB * 16)

        @block.gpsimd
        def _(pool):
            pool.memset(ident[:], 0.0).then_inc(idz, 1)
            pool.wait_ge(idz, 1)
            pool.affine_select(out=ident[:], in_=ident[:], compare_op=ALU.not_equal, fill=1.0, base=0,
                               pattern=[[-1, P]], channel_multiplier=1).then_inc(idn, 1)
            pool.memset(zeros[:], 0.0).then_inc(zeros_set, 1)
            total = pool.value_load(ends[0:1, E:E + 1], min_val=1, max_val=NB)
            with pool.Fori(0, total + 1) as g:
                pool.wait_ge(turned, g + 1)
                pool.sem_inc(passed, 1)
                pool.tensor_copy(idx[:], table[:, ds(g, 1)]).then_inc(idx_set, 1)
                pool.wait_ge(idx_set, g + 1)
                pool.sem_inc(passed, 1)
                pool.indirect_dma_start(xg[:], None, dram["xn"], bass.IndirectOffsetOnAxis(idx[:], 0)).then_inc(gathered, 16)

        @block.tensor
        def _(pe):
            def turn(g):
                pe.wait_ge(gathered, g * 16 + 16)
                for h in range(2):
                    for k in range(4):
                        last = pe.transpose(tbank[h][:, k * P:(k + 1) * P], xg[:, (4 * h + k) * P:(4 * h + k + 1) * P], ident[:])
                last.then_inc(turned, 1)

            pe.sem_inc(turned, 1)
            pe.wait_ge(idn, 1)
            turn(0)
            with pe.Fori(0, E // 2) as q:
                for p in range(2):
                    b0, b1 = bounds(pe, q * 2 + p)
                    pe.wait_ge(w_in[p], q * 48 + 48)
                    pe.sem_inc(passed, 1)
                    with pe.Fori(b0, b1) as g:
                        pe.wait_ge(xT_full, g * 2 + 2)
                        for j in range(2):
                            pe.wait_ge(h_full, g * 2 + (j + 1))
                            for wi, w in enumerate((w1, w3)):
                                for f in range(2):
                                    c0 = (2 * j + f) * P
                                    for k in range(KD):
                                        last = pe.matmul(hbank[j][:, (2 * wi + f) * P:(2 * wi + f + 1) * P], w[:, p, k, c0:c0 + P],
                                                         xgT[:, k], start=(k == 0), stop=(k == KD - 1))
                            last.then_inc(h_ps, 1)
                        turn(g + 1)
                        for f in range(FE):
                            if f % 2 == 0:
                                pe.wait_ge(h_full, g * 2 + (f // 2 + 3))
                            for n in range(2):
                                if f == 0:
                                    pe.wait_ge(y_free, g * 2 + (n + 1))
                                last = pe.matmul(ybank[n][:], hT[:, f], w2[:, p, f, n * 512:(n + 1) * 512], start=(f == 0), stop=(f == FE - 1))
                                if f == FE - 1:
                                    last.then_inc(y_ps, 1)

        @block.scalar
        def _(act):
            act.sem_inc(y_free, 2)
            for n in range(2):
                act.sem_inc(y_out[n], 16)

            def copy_xT(g):
                act.wait_ge(turned, g + 2)
                for h in range(2):
                    act.activation(xgT[:, 4 * h:4 * h + 4].rearrange("p k t -> p (k t)"), tbank[h][:], ACT.Copy).then_inc(xT_full, 1)

            copy_xT(0)
            total = act.value_load(ends[0:1, E:E + 1], min_val=1, max_val=NB)
            with act.Fori(0, total) as g:
                for j in range(2):
                    act.wait_ge(h_ps, g * 2 + (j + 1))
                    act.activation(th[:, j], hbank[j][:, 0:2 * P], ACT.Tanh, scale=0.5).then_inc(tanh_d, 1)
                copy_xT(g + 1)
                for n in range(2):
                    act.wait_ge(y_ps, g * 2 + (n + 1))
                    act.wait_ge(y_out[n], g * 16 + 16)
                    act.activation(ysb[:, n], ybank[n][:], ACT.Copy, scale=0.5).then_inc(y_free, 1)
                    act.wait_ge(y_free, g * 2 + (n + 3))
                    act.dma_start(dram["y"][ds(g * P, P), n * 512:(n + 1) * 512], ysb[:, n]).then_inc(y_out[n], 16)
            for n in range(2):
                act.wait_ge(y_out[n], total * 16 + 16)
            act.sem_inc(passed, 1)

        @block.vector
        def _(dve):
            dve.sem_inc(h_full, 2)
            total = dve.value_load(ends[0:1, E:E + 1], min_val=1, max_val=NB)
            with dve.Fori(0, total) as g:
                for j in range(2):
                    dve.wait_ge(tanh_d, g * 2 + (j + 1))
                    dve.scalar_tensor_tensor(gg[:, j], th[:, j], 1.0, hbank[j][:, 0:2 * P], ALU.add, ALU.mult).then_inc(gate_d, 1)
                    dve.wait_ge(gate_d, g * 2 + (j + 1))
                    dve.tensor_tensor(hT[:, 2 * j:2 * j + 2].rearrange("p f t -> p (f t)"), gg[:, j], hbank[j][:, 2 * P:4 * P],
                                      ALU.mult).then_inc(h_full, 1)


def combine(nc, io, dram, pos, wts, out):
    PER = 1 + 14
    with ExitStack() as ctx:
        def sb(name, shape, dt=F32):
            return ctx.enter_context(nc.sbuf_tensor(name, shape, dt))

        def sem(name):
            return ctx.enter_context(nc.semaphore(name))

        B = 4
        y = [sb(f"cy{k}", [P, B, D]) for k in range(2)]
        h = sb("ch", [P, B, D])
        o = sb("co", [P, B, D])
        sqj = sb("csq", [P, 2, D])
        fg = sb("fg", [P, D])
        ssq, msq, rst, rh, rt = (sb(f"c_st{i}", [P, B]) for i in range(5))
        idx = sb("cidx", [P, 2, TT], I32)
        y_in = [[sem(f"cy_in{k}{b}") for b in range(B)] for k in range(2)]
        h_in, o_out = ([sem(f"{n}{b}") for b in range(B)] for n in ("ch_in", "co_out"))
        fg_in, acc, sq, done, step = sem("fg_in"), sem("c_sums"), sem("c_squares"), sem("c_done"), sem("c_steps")
        idx_set = sem("c_idx")
        block = ctx.enter_context(nc.Block())

        @block.sync
        def _(sp):
            sp.dma_start(fg[:], io["final_norm_g"].rearrange("(a n) -> a n", a=1).partition_broadcast(P)).then_inc(fg_in, 16)
            for i in range(TT):
                b = i % B
                if i >= B:
                    sp.wait_ge(done, i - B + 1)
                sp.dma_start(h[:, b], dram["h"][i * P:(i + 1) * P, :]).then_inc(h_in[b], 16)

        @block.gpsimd
        def _(pool):
            for k in range(2):
                pool.tensor_copy(idx[:, k], pos[:, :, k]).then_inc(idx_set, 1)
            pool.wait_ge(idx_set, 2)
            for i in range(TT):
                b = i % B
                if i >= B:
                    pool.wait_ge(acc, 2 * (i - B) + 2)
                for k in range(2):
                    pool.indirect_dma_start(y[k][:, b], None, dram["y"], bass.IndirectOffsetOnAxis(idx[:, k, i:i + 1], 0)).then_inc(y_in[k][b], 16)

        @block.scalar
        def _(act):
            for i in range(TT):
                b = i % B
                act.wait_ge(acc, 2 * i + 2)
                if i >= 2:
                    act.wait_ge(sq, i - 1)
                act.activation(sqj[:, i % 2], h[:, b], ACT.Square, accum_out=ssq[:, b:b + 1]).then_inc(sq, 1)
                if i >= 1:
                    act.wait_ge(done, i)
                    act.dma_start(out[0, (i - 1) * P:i * P, :], o[:, (i - 1) % B]).then_inc(o_out[(i - 1) % B], 16)
            act.wait_ge(done, TT)
            act.dma_start(out[0, (TT - 1) * P:TT * P, :], o[:, (TT - 1) % B]).then_inc(o_out[(TT - 1) % B], 16)
            for b in range(B):
                act.wait_ge(o_out[b], 16 * TT // B)

        @block.vector
        def _(dve):
            s = Steps(dve, step)
            dve.wait_ge(fg_in, 16)

            def add(i):
                b, turn = i % B, i // B + 1
                dve.wait_ge(h_in[b], 16 * turn)
                for k in range(2):
                    dve.wait_ge(y_in[k][b], 16 * turn)
                    dve.scalar_tensor_tensor(h[:, b], y[k][:, b], wts[:, i, k:k + 1], h[:, b], ALU.mult, ALU.add).then_inc(acc, 1)
                    dve.wait_ge(acc, 2 * i + k + 1)

            def norm(i):
                b = i % B
                one = slice(b, b + 1)
                dve.wait_ge(sq, i + 1)
                s.link(dve.tensor_scalar(msq[:, one], ssq[:, one], 1.0 / D, EPS, ALU.mult, ALU.add))
                rsqrt_steps(dve, s, msq[:, one], rh[:, one], rst[:, one], rt[:, one])
                if i >= B:
                    dve.wait_ge(o_out[b], 16 * (i // B))
                dve.scalar_tensor_tensor(o[:, b], h[:, b], rst[:, one], fg[:], ALU.mult, ALU.mult).then_inc(done, 1)

            add(0)
            for i in range(1, TT):
                add(i)
                norm(i - 1)
            norm(TT - 1)


def trunk(nc, io, out):
    dram = {
        "xT": nc.dram_tensor("xn1_feature_major", [KD, P, T], F32, kind="Internal").ap(),
        "ys": nc.dram_tensor("branches", [NBR, 2, P, T], F32, kind="Internal").ap(),
        "h": nc.dram_tensor("residual", [T, D], F32, kind="Internal").ap(),
        "xn": nc.dram_tensor("xn2", [T, D], F32, kind="Internal").ap(),
        "y": nc.dram_tensor("expert_rows", [NB * P, D], F32, kind="Internal").ap(),
    }
    with ExitStack() as ctx:
        wts = ctx.enter_context(nc.sbuf_tensor("wts", [P, TT, 2], F32))
        pos = ctx.enter_context(nc.sbuf_tensor("pos", [P, TT, 2], I32))
        table = ctx.enter_context(nc.sbuf_tensor("table", [P, NB + 1], I32))
        ends = ctx.enter_context(nc.sbuf_tensor("ends", [P, E + 1], I32))
        mix_branches(nc, io, dram)
        with nc.sbuf_tensor("logits", [P, TT, R], F32) as logits:
            merge_branches(nc, io, dram, logits)
            route(nc, logits, table, pos, wts, ends)
        run_experts(nc, io, dram, table, ends)
        combine(nc, io, dram, pos, wts, out)


_INS = ["x", "norm1_g", "w_in", "conv_a_w", "pool_w", "pool_b", "pool_scale", "s5_lambda_re", "s5_lambda_im", "s5_log_step",
        "s5_b_re", "s5_b_im", "s5_c_re", "s5_c_im", "s5_d", "s5_glu_w", "s5_glu_b", "lru_conv_w", "lru_conv_b", "lru_wa", "lru_ba",
        "lru_wx", "lru_bx", "lru_lambda", "merge_gate_w", "merge_gate_b", "branch_w", "w_out", "norm2_g", "router_group_w",
        "router_group_b", "router_expert_w", "router_expert_b", "expert_w1", "expert_w3", "expert_w2", "final_norm_g"]


def kernel(**inputs):
    import numpy as _np
    import concourse.bacc as _bacc
    from concourse import mybir as _mybir
    from concourse.bass_utils import run_bass_kernel_spmd as _run

    nc = _bacc.Bacc("TRN2", target_bir_lowering=False, num_devices=1)
    arrays, io = {}, {}
    for name in _INS:
        a = _np.ascontiguousarray(inputs[name])
        arrays[f"in_{name}_dram"] = a
        io[name] = nc.dram_tensor(f"in_{name}_dram", a.shape, _mybir.dt.from_np(a.dtype), kind="ExternalInput").ap()
    out = nc.dram_tensor("out_dram", (1, T, D), F32, kind="ExternalOutput").ap()
    trunk(nc, io, out)
    r = _run(nc, [arrays], core_ids=[0])
    return r.results[0]["out_dram"]
```

```python
import math
from contextlib import ExitStack

import concourse.bass as bass
from concourse import mybir

F32 = mybir.dt.float32
F32R = mybir.dt.float32r
I32 = mybir.dt.int32
U32 = mybir.dt.uint32
ALU = mybir.AluOpType
ACT = mybir.ActivationFunctionType
AX = mybir.AxisListType
ds = bass.ds

P = 128
T = 2048
D = 1024
KD = D // P
TT = T // P
W = 256
NF = 14
NBR = 4
G, EPG = 4, 8
E = G * EPG
DE = 512
FE = DE // P
R = G + E
NB = T * 2 // P + E
EPS = 1e-6
GELU_C = 0.044715
GELU_S = math.sqrt(2.0 / math.pi)
MAGIC = 12582912.0


class Ring:

    def __init__(self, full, free, banks, uses):
        self.full, self.free, self.banks, self.uses = full, free, banks, list(uses)
        assert len(self.uses) % len(banks) == 0
        self.per = len(self.uses)

    def bank(self, use):
        return self.banks[self.uses.index(use) % len(self.banks)]

    def turn(self, use):
        return self.uses.index(use) + 1


class Steps:

    def __init__(self, eng, sem, per=0):
        self.eng, self.sem, self.per, self.n, self.base = eng, sem, per, 0, 0

    def trip(self, base):
        self.base, self.n = base, 0

    def mark(self, inst):
        inst.then_inc(self.sem, 1)
        self.n += 1

    def settle(self):
        self.eng.wait_ge(self.sem, self.base + self.n)

    def link(self, inst):
        self.mark(inst)
        self.settle()


def rsqrt_steps(dve, s, mean_sq, half, y, t):
    s.link(dve.tensor_scalar(y.bitcast(I32), mean_sq.bitcast(I32), -0.5, 1597463007.0, ALU.mult, ALU.add))
    s.link(dve.tensor_scalar(half, mean_sq, -0.5, None, ALU.mult))
    for _ in range(4):
        s.link(dve.tensor_tensor(t, y, y, ALU.mult))
        s.link(dve.tensor_tensor(t, t, half, ALU.mult))
        s.link(dve.scalar_tensor_tensor(y, t, 1.5, y, ALU.add, ALU.mult))


def horner(dve, s, out, x, coefs):
    s.link(dve.tensor_scalar(out, x, coefs[-1], None, ALU.mult))
    for c in coefs[-2::-1]:
        s.link(dve.scalar_tensor_tensor(out, out, c, x, ALU.add, ALU.mult))


def exp_exact(dve, s, out, x, n, f, pw):
    s.link(dve.tensor_scalar(f, x, -87.0, 88.0, ALU.max, ALU.min))
    s.link(dve.tensor_scalar(n, f, 1.0 / math.log(2.0), MAGIC, ALU.mult, ALU.add))
    s.link(dve.tensor_scalar(n, n, -MAGIC, None, ALU.add))
    s.link(dve.scalar_tensor_tensor(f, n, -0.693359375, f, ALU.mult, ALU.add))
    s.link(dve.scalar_tensor_tensor(f, n, 2.12194440e-4, f, ALU.mult, ALU.add))
    s.link(dve.tensor_scalar(pw, n, 127.0, 8388608.0, ALU.add, ALU.mult))
    horner(dve, s, out, f, [1.0 / math.factorial(k) for k in range(1, 9)])
    s.link(dve.scalar_tensor_tensor(out, out, 1.0, pw.bitcast(F32), ALU.add, ALU.mult))


def mix_branches(nc, io, dram):
    CT = 512
    CH = T // CT
    TC = CT // P
    NS = 8
    MAXW = 16
    FIRST_F = [8, 9, 10, 11]
    SLOT_F = [12, 13, 6, 7, 2, 0, 4, 3, 1, 5]
    DVE_STEPS = 108
    POOL_STEPS = 48

    with ExitStack() as ctx:
        def sb(name, shape, dt=F32):
            return ctx.enter_context(nc.sbuf_tensor(name, shape, dt))

        def sem(name):
            return ctx.enter_context(nc.semaphore(name))

        ps = [ctx.enter_context(nc.psum_tensor(f"mixps{i}", [P, CT], F32)) for i in range(8)]
        g_uses = [("t", t, h) for t in range(TC) for h in range(2)] + [("f", f) for f in FIRST_F]
        b_uses = []
        for n, f in enumerate(SLOT_F):
            (b_uses if f in (4, 5) else g_uses).append(("f", f))
            if n == 1:
                g_uses += [("r", 0), ("i", 0), ("r", 1), ("i", 1)]
            if n == 5:
                b_uses += [("pool", 0), ("pool", 1)]
        g_uses += [("glu", 0), ("glu", 1)]
        gr = Ring(sem("act_tile_full"), sem("act_tile_free"), ps[0:2], g_uses)
        br = Ring(sem("dve_tile_full"), sem("dve_tile_free"), ps[2:4], b_uses)
        sre, sim_, yps = ps[4], ps[5], ps[6]

        NW = 7
        win = sb("win", [P, NW, KD, P])
        g1 = sb("g1", [P, D])
        ident = sb("ident", [P, P])
        lamre, lamim = sb("lamre", [P, NS]), sb("lamim", [P, NS])
        ex = sb("ex", [P, NS + 2])
        lst = sb("lst", [P, 2 * NS])
        exo = sb("exo", [P, NS + 2])
        BT = [sb(f"BT{i}", [P, 2, P]) for i in range(2)]
        CTr = [sb(f"CTr{i}", [P, 2, P]) for i in range(2)]
        bd = sb("bd", [P, 3, 2, P])
        glw = sb("glw", [P, 2, W])
        cwa = sb("cwa", [P, 3, 2])
        cwl = sb("cwl", [P, 4, 2])
        vec = sb("vec", [P, 8, 2])
        LCB, PB, PSC, SD, GB, BA, BX, LAM = range(8)
        m4sp = sb("m4sp", [P, 2])
        invw, wcol = sb("invw", [P, 2]), sb("wcol", [P, 2])
        corr = sb("corr", [P, 2, MAXW])
        io16 = sb("io16", [P, MAXW], I32)
        tcos, tsin = sb("tcos", [P, NS, CT]), sb("tsin", [P, NS, CT])
        rdec = sb("rdec", [P, NS])
        pari = sb("pari", [P, NS + 2], I32)
        gpar = sb("gpar", [P, 2], I32)
        gmask = sb("gmask", [P, 2])

        xin = sb("xin", [P, TC, D])
        ssq, rst, rtmp, rhalf = sb("ssq", [P, TC]), sb("rst", [P, TC]), sb("rtmp", [P, TC]), sb("rhalf", [P, TC])
        msq = sb("msq", [P, TC])
        xT = sb("xT", [P, KD, CT])
        b_nat = [xT[:, i, 0:NS * 16].rearrange("p (s h) -> p s h", h=16) for i in range(2)]
        c_nat = [xT[:, 2 + i, 0:P].rearrange("p (u h) -> p u h", u=2) for i in range(2)]
        par = xT[:, 4, 0:24 * NS].rearrange("p (i s) -> p i s", s=NS)
        bgcg = sb("bgcg", [P, 4, CT])
        va = sb("va", [P, 2, CT + 2])
        pu = sb("pu", [P, 2, CT + MAXW - 1])
        pw_ = [sb(f"pw{i}", [P, CT + MAXW - 1]) for i in range(2)]
        su = sb("su", [P, 2, CT])
        lx = sb("lx", [P, 2, CT + 3])
        xc = sb("xc", [P, 2, CT])
        lg = sb("lg", [P, 2, CT])
        lru = sb("lru", [P, 2, 4, CT])
        hcar = sb("hcar", [P, 2])
        m = sb("m", [P, 8, CT])
        hst = sb("hst", [P, 2, 2, CT])
        scar = sb("scar", [P, 2, NS])
        ys = sb("ys", [P, NBR, 2, CT])
        yg, yq = su, sb("yq", [P, 2, CT])
        lq = yq

        par_in, bd_zero, bd_in = sem("params_in"), sem("diag_zero"), sem("diag_in")
        win_in = [sem(f"win_in{i}") for i in range(NW)]
        F_ORDER = FIRST_F + SLOT_F
        assert NF % NW == 0
        consts, idz = sem("consts"), sem("ident_zero")
        pre, pre_t, pre_tt, pre_a = sem("prep_steps"), sem("bc_ready"), sem("bc_turned"), sem("bc_copied")
        unit_rot, tabs = sem("unit_rotation"), sem("tables_steps")
        x_in = [sem(f"x_in{i}") for i in range(TC)]
        sq_done, xh_full, xT_out = sem("square_sum"), sem("xhat_full"), sem("xT_out")
        proj = sem("proj_evacuated")
        dstep, astep, pstep = sem("dve_step"), sem("act_step"), sem("pool_step")
        pooled, xc_full = sem("pooled_full"), sem("xc_full")
        lru_a, lru_q, lru_m, gl_u, gl_t = sem("lru_acts"), sem("lru_q"), sem("lru_root"), sem("gate_poly"), sem("gate_tanh")
        s_full, s_free, rot_in, scan_d, rot_m, h_full = (sem("bu_full"), sem("bu_free"), sem("bu_products"), sem("scans_in"),
                                                        sem("state_products"), sem("state_full"))
        y_full, y_free, y_pre, y_sq, y_u, y_t, yg_full, glu_t = (sem("y_full"), sem("y_free"), sem("y_pre"), sem("y_sq"),
                                                               sem("y_poly"), sem("y_tanh"), sem("y_gelu"), sem("glu_tanh"))
        ys_full, ys_out = sem("ys_full"), [sem(f"ys_out{i}") for i in range(NBR)]
        passed = sem("mix_passed")
        block = ctx.enter_context(nc.Block())

        GPER, BPER = gr.per, br.per
        PROJ = [("f", f) for f in (FIRST_F + SLOT_F) if f not in (4, 5)]
        NPROJ = len(PROJ)

        @block.sync
        def _(sp):
            n = [0]

            def load(dst, src):
                sp.dma_start(dst, src, allow_slow_non_contiguous=True).then_inc(par_in, 16)
                n[0] += 16

            for t in range(TC):
                sp.dma_start(xin[:, t], io["x"][0, t * P:(t + 1) * P, :]).then_inc(x_in[t], 16)
            load(g1[:], io["norm1_g"][0:1].partition_broadcast(P))
            load(lst[:], io["s5_log_step"][0:1].partition_broadcast(P))
            for q in range(2):
                rows = slice(64 * q, 64 * q + 64)
                load(lamre[rows, :], io["s5_lambda_re"][0].rearrange("(s q) p -> q p s", q=2)[q])
                load(lamim[rows, :], io["s5_lambda_im"][0].rearrange("(s q) p -> q p s", q=2)[q])
                load(b_nat[0][rows], io["s5_b_re"][0].rearrange("(s q) p h -> q p s h", q=2)[q])
                load(b_nat[1][rows], io["s5_b_im"][0].rearrange("(s q) p h -> q p s h", q=2)[q])
            for i, nm in enumerate(("s5_c_re", "s5_c_im")):
                for u in range(2):
                    load(c_nat[i][:, u], io[nm][0, 8 * u:8 * u + 8].rearrange("g h p -> (g h) p"))
            load(glw[:], io["s5_glu_w"][0].rearrange("(k p) n -> p k n", p=P))
            load(cwa[:], io["conv_a_w"][0].rearrange("k (j p) -> p k j", p=P))
            load(cwl[:], io["lru_conv_w"][0].rearrange("k (j p) -> p k j", p=P))
            for i, nm in enumerate(("lru_conv_b", "pool_b", "pool_scale", "s5_d", "s5_glu_b", "lru_ba", "lru_bx", "lru_lambda")):
                v = io[nm][0]
                if len(v.shape) == 2:
                    v = v.rearrange("a b -> (a b)")
                load(vec[:, i, :], v.rearrange("(j p) -> p j", p=P))
            sp.wait_ge(bd_zero, 1)
            for i, nm in enumerate(("pool_w", "lru_wa", "lru_wx")):
                for g in range(4):
                    q = 64 * (g % 2)
                    sp.dma_start(bd[q:q + 64, i, g // 2, q:q + 64], io[nm][0, g]).then_inc(bd_in, 16)

            def load_win(i):
                f = F_ORDER[i]
                sp.dma_start(win[:, i % NW], io["w_in"][0, :, f * P:(f + 1) * P].rearrange("(k p) n -> p k n", p=P))\
                  .then_inc(win_in[i % NW], 16)

            for i in range(NW):
                load_win(i)
            io["n_params"] = n[0]
            for i in range(NBR):
                sp.sem_inc(ys_out[i], 16)
            sp.sem_inc(xT_out, 16)
            with sp.Fori(0, CH) as c:
                nxt = (c + 1) % CH
                gb = sp.snap(c * GPER)
                bb = sp.snap(c * BPER)

                def used(i):
                    f = F_ORDER[i]
                    if f in (4, 5):
                        sp.wait_ge(br.full, bb + br.turn(("f", f)))
                    else:
                        sp.wait_ge(gr.full, gb + gr.turn(("f", f)))

                for t in range(TC):
                    sp.wait_ge(gr.full, gb + gr.turn(("t", t, 1)))
                    sp.dma_start(xin[:, t], io["x"][0, ds(nxt * CT + t * P, P), :]).then_inc(x_in[t], 16)
                sp.wait_ge(gr.free, gb + gr.turn(("t", TC - 1, 1)) + 2)
                sp.dma_start(dram["xT"][:, :, ds(c * CT, CT)].rearrange("k p t -> p k t"), xT[:]).then_inc(xT_out, 16)
                for i in range(NF):
                    used(i)
                    load_win((i + NW) % NF)
                for i, b in enumerate((3, 1, 0, 2)):
                    sp.wait_ge(ys_full, c * 8 + 2 * i + 2)
                    sp.dma_start(dram["ys"][b, :, :, ds(c * CT, CT)].rearrange("j p t -> p j t"), ys[:, b]).then_inc(ys_out[b], 16)
            for i in range(NW):
                sp.wait_ge(win_in[i], 16 * (1 + CH * NF // NW))
            sp.wait_ge(xT_out, 16 * (CH + 1))
            for i in range(NBR):
                sp.wait_ge(ys_out[i], 16 * (CH + 1))
            for t in range(TC):
                sp.wait_ge(x_in[t], 16 * (CH + 1))

        n_params = io["n_params"]

        @block.gpsimd
        def _(pool):
            pool.memset(bd[:], 0.0).then_inc(bd_zero, 1)
            pool.memset(ident[:], 0.0).then_inc(idz, 1)
            pool.wait_ge(idz, 1)
            pool.affine_select(out=ident[:], in_=ident[:], compare_op=ALU.not_equal, fill=1.0, base=0,
                               pattern=[[-1, P]], channel_multiplier=1).then_inc(consts, 1)
            pool.iota(gpar[:, 0:1], [[0, 1]], base=0, channel_multiplier=1).then_inc(consts, 1)
            pool.iota(io16[:], [[1, MAXW]], base=1, channel_multiplier=0).then_inc(consts, 1)
            pool.wait_ge(unit_rot, 2)
            ts = Steps(pool, tabs)
            k = 1
            while k < CT:
                t1 = ys[:, 0:2].rearrange("p a b t -> p (a b t)")[:, 0:NS * k].rearrange("p (s t) -> p s t", s=NS)
                t2 = ys[:, 2:4].rearrange("p a b t -> p (a b t)")[:, 0:NS * k].rearrange("p (s t) -> p s t", s=NS)
                zc = tcos[:, :, k - 1:k].to_broadcast([P, NS, k])
                zs = tsin[:, :, k - 1:k].to_broadcast([P, NS, k])
                ts.mark(pool.tensor_tensor(t1, tcos[:, :, 0:k], zc, ALU.mult))
                ts.link(pool.tensor_tensor(t2, tsin[:, :, 0:k], zs, ALU.mult))
                ts.link(pool.tensor_tensor(tcos[:, :, k:2 * k], t1, t2, ALU.subtract))
                ts.mark(pool.tensor_tensor(t1, tsin[:, :, 0:k], zc, ALU.mult))
                ts.link(pool.tensor_tensor(t2, tcos[:, :, 0:k], zs, ALU.mult))
                ts.link(pool.tensor_tensor(tsin[:, :, k:2 * k], t1, t2, ALU.add))
                k *= 2
            io["n_tabs"] = ts.n
            with pool.Fori(0, CH) as c:
                for s in range(NS):
                    pool.wait_ge(rot_in, c * NS + s + 1)
                    pool.tensor_tensor(m[:, 0], m[:, 0], m[:, 1], ALU.add).then_inc(scan_d, 1)
                    pool.tensor_tensor(m[:, 2], m[:, 2], m[:, 3], ALU.subtract).then_inc(scan_d, 1)
                    pool.wait_ge(rot_m, c * NS + s + 1)
                    if s >= 2:
                        pool.wait_ge(y_full, c * NS + s - 1)
                    pool.tensor_tensor(hst[:, s % 2, 0], m[:, 4], m[:, 5], ALU.subtract).then_inc(pstep, 1)
                    pool.tensor_tensor(hst[:, s % 2, 1], m[:, 6], m[:, 7], ALU.add).then_inc(pstep, 1)
                    pool.wait_ge(pstep, c * 2 * NS + 2 * s + 2)
                    pool.sem_inc(passed, 1)
                    pool.tensor_copy(scar[:, 0:1, s], hst[:, s % 2, 0, CT - 1:CT]).then_inc(h_full, 1)
                    pool.tensor_copy(scar[:, 1:2, s], hst[:, s % 2, 1, CT - 1:CT]).then_inc(h_full, 1)

        n_tabs = io["n_tabs"]

        @block.scalar
        def _(act):
            act.sem_inc(gr.free, 2)
            act.wait_ge(pre_tt, 1)
            for i in range(2):
                for u in range(2):
                    act.activation(BT[i][:, u], ps[i][:, u * P:(u + 1) * P], ACT.Copy).then_inc(pre_a, 1)
                    act.activation(CTr[i][:, u], ps[2 + i][:, u * P:(u + 1) * P], ACT.Copy,
                                   scale=(1.0 if i == 0 else -1.0)).then_inc(pre_a, 1)
            with act.Fori(0, CH) as c:
                gb = act.snap(c * GPER)
                for t in range(TC):
                    act.wait_ge(x_in[t], c * 16 + 16)
                    act.activation(lru[:, t // 2, 2 * (t % 2):2 * (t % 2) + 2, :].rearrange("p a b -> p (a b)"), xin[:, t], ACT.Square,
                                   accum_out=ssq[:, t:t + 1]).then_inc(sq_done, 1)
                act.wait_ge(xT_out, 16 * c + 16)
                for t in range(TC):
                    for h in range(2):
                        act.wait_ge(gr.full, gb + gr.turn(("t", t, h)))
                        act.activation(xT[:, 4 * h:4 * h + 4, t * P:(t + 1) * P],
                                       gr.bank(("t", t, h))[:].rearrange("p (k t) -> p k t", k=4), ACT.Copy).then_inc(gr.free, 1)

                def evac(dst, f):
                    act.wait_ge(gr.full, gb + gr.turn(("f", f)))
                    act.activation(dst, gr.bank(("f", f))[:], ACT.Copy).then_inc(gr.free, 1)

                DST = {0: bgcg[:, 0], 1: bgcg[:, 1], 2: bgcg[:, 2], 3: bgcg[:, 3],
                       6: pu[:, 0, MAXW - 1:], 7: pu[:, 1, MAXW - 1:], 8: su[:, 0], 9: su[:, 1],
                       10: lx[:, 0, 3:], 11: lx[:, 1, 3:], 12: lg[:, 0], 13: lg[:, 1]}
                for f in FIRST_F:
                    evac(DST[f], f)
                for n, f in enumerate(SLOT_F):
                    if f in (4, 5):
                        continue
                    if f in (12, 13):
                        act.wait_ge(gr.full, gb + gr.turn(("f", f)))
                        act.activation(lq[:, f - 12], gr.bank(("f", f))[:], ACT.Square).then_inc(lru_a, 1)
                    evac(DST[f], f)
                    if n == 1:
                        for j in range(2):
                            for i, nm in enumerate(("r", "i")):
                                act.wait_ge(gr.full, gb + gr.turn((nm, j)))
                                act.activation(lru[:, j, i], gr.bank((nm, j))[:], ACT.Tanh, scale=0.5,
                                               bias=vec[:, BA + i, j:j + 1]).then_inc(gr.free, 1)
                            act.wait_ge(gr.free, gb + gr.turn(("i", j)) + 2)
                            act.activation(lru[:, j, 2], lru[:, j, 0], ACT.Exp, scale=m4sp[:, j:j + 1],
                                           bias=m4sp[:, j:j + 1]).then_inc(astep, 1)
                            act.wait_ge(astep, c * 2 + j + 1)
                            act.activation(lru[:, j, 0], lru[:, j, 0], ACT.Tanh, scale=m4sp[:, j:j + 1],
                                           bias=m4sp[:, j:j + 1]).then_inc(lru_a, 1)
                            act.activation(lru[:, j, 3], lru[:, j, 2], ACT.Square).then_inc(lru_a, 1)
                    if n == 3:
                        for j in range(2):
                            act.wait_ge(gl_u, c * 2 + j + 1)
                            act.activation(lq[:, j], lq[:, j], ACT.Tanh, scale=GELU_S).then_inc(gl_t, 1)
                    if n == 5:
                        for j in range(2):
                            act.wait_ge(lru_q, c * 2 + j + 1)
                            act.activation(lru[:, j, 3], lru[:, j, 3], ACT.Sqrt, scale=-0.25).then_inc(lru_m, 1)
                for j in range(2):
                    act.wait_ge(y_pre, c * 2 + j + 1)
                    act.activation(yq[:, j], yg[:, j], ACT.Square).then_inc(y_sq, 1)
                for j in range(2):
                    act.wait_ge(y_u, c * 2 + j + 1)
                    act.activation(yq[:, j], yq[:, j], ACT.Tanh, scale=GELU_S).then_inc(y_t, 1)
                for j in range(2):
                    act.wait_ge(gr.full, gb + gr.turn(("glu", j)))
                    act.activation(yq[:, j], gr.bank(("glu", j))[:], ACT.Tanh, scale=0.25,
                                   bias=vec[:, GB, j:j + 1]).then_inc(gr.free, 1)

        @block.tensor
        def _(pe):
            pe.wait_ge(consts, 3)
            pe.wait_ge(pre_t, 1)
            for i in range(2):
                for u in range(2):
                    pe.transpose(ps[i][:, u * P:(u + 1) * P], m[:, i, u * P:(u + 1) * P], ident[:])
                    last = pe.transpose(ps[2 + i][:, u * P:(u + 1) * P], m[:, 2 + i, u * P:(u + 1) * P], ident[:])
            last.then_inc(pre_tt, 1)
            pe.wait_ge(pre_a, 8)
            pe.wait_ge(par_in, n_params)
            pe.wait_ge(bd_in, 16 * 12)
            with pe.Fori(0, CH) as c:
                gb = pe.snap(c * GPER)
                bb = pe.snap(c * BPER)
                sb_ = pe.snap(c * NS)

                def project(f):
                    ring, base = (br, bb) if f in (4, 5) else (gr, gb)
                    i = F_ORDER.index(f)
                    pe.wait_ge(win_in[i % NW], 16 * (NF // NW) * c + 16 * (i // NW + 1))
                    pe.wait_ge(ring.free, base + ring.turn(("f", f)))
                    for k in range(KD):
                        last = pe.matmul(ring.bank(("f", f))[:], win[:, i % NW, k], xT[:, k, :],
                                         start=(k == 0), stop=(k == KD - 1))
                    last.then_inc(ring.full, 1)

                for t in range(TC):
                    pe.wait_ge(xh_full, c * TC + t + 1)
                    for h in range(2):
                        pe.wait_ge(gr.free, gb + gr.turn(("t", t, h)))
                        for k in range(4):
                            last = pe.transpose(gr.bank(("t", t, h))[:, k * P:(k + 1) * P],
                                                xin[:, t, (4 * h + k) * P:(4 * h + k + 1) * P], ident[:])
                        last.then_inc(gr.full, 1)
                pe.wait_ge(gr.free, gb + 2 * TC + 2)
                project(8)
                project(9)
                project(10)
                project(11)
                pe.wait_ge(gr.free, gb + gr.turn(("f", 9)) + 2)
                for n, f in enumerate(SLOT_F):
                    if n < NS:
                        s, u, q = n, n // 4, 32 * (n % 4)
                        pe.wait_ge(s_free, sb_ + s + 1)
                        pe.matmul(sre[:], BT[0][q:q + 32, u, :], su[q:q + 32, u, :], start=True, stop=True)
                        pe.matmul(sim_[:], BT[1][q:q + 32, u, :], su[q:q + 32, u, :], start=True, stop=True).then_inc(s_full, 1)
                    project(f)
                    if n == 1:
                        for j in range(2):
                            pe.wait_ge(xc_full, c * 2 + j + 1)
                            for i, nm in enumerate(("r", "i")):
                                pe.wait_ge(gr.free, gb + gr.turn((nm, j)))
                                pe.matmul(gr.bank((nm, j))[:], bd[:, 1 + i, j], xc[:, j], start=True, stop=True).then_inc(gr.full, 1)
                    if n == 5:
                        for j in range(2):
                            pe.wait_ge(pooled, c * 2 + j + 1)
                            pe.wait_ge(br.free, bb + br.turn(("pool", j)))
                            pe.matmul(br.bank(("pool", j))[:], bd[:, 0, j], ys[:, 1, j], start=True, stop=True).then_inc(br.full, 1)
                    if n >= 2:
                        s = n - 2
                        u, q = s // 4, 32 * (s % 4)
                        if s % 4 == 0:
                            pe.wait_ge(y_free, c * 2 + u + 1)
                        pe.wait_ge(h_full, 2 * sb_ + 2 * s + 2)
                        pe.matmul(yps[q:q + 32, :], CTr[0][:, u, q:q + 32], hst[:, s % 2, 0], start=True, stop=False)
                        last = pe.matmul(yps[q:q + 32, :], CTr[1][:, u, q:q + 32], hst[:, s % 2, 1], start=False, stop=True)
                        last.then_inc(y_full, 1)
                pe.wait_ge(yg_full, c * 2 + 2)
                for j in range(2):
                    pe.wait_ge(gr.free, gb + gr.turn(("glu", j)))
                    for k in range(2):
                        last = pe.matmul(gr.bank(("glu", j))[:], glw[:, k, j * P:(j + 1) * P], yg[:, k],
                                         start=(k == 0), stop=(k == 1))
                    last.then_inc(gr.full, 1)

        @block.vector
        def _(dve):
            s = Steps(dve, pre)
            for b in range(2):
                dve.sem_inc(br.free, 1)
            dve.sem_inc(s_free, 1)
            dve.sem_inc(y_free, 1)
            for z in (va[:, :, 0:2], pu[:, :, 0:MAXW - 1], lx[:, :, 0:3], hcar[:], scar[:], m[:, 0:4, :]):
                s.mark(dve.memset(z, 0.0))
            for j in range(2):
                for q in range(2):
                    w = float(2 ** (2 * j + q + 1))
                    s.mark(dve.memset(wcol[64 * q:64 * q + 64, j:j + 1], w))
                    s.mark(dve.memset(invw[64 * q:64 * q + 64, j:j + 1], 1.0 / w))
            dve.wait_ge(consts, 3)
            dve.wait_ge(par_in, n_params)
            s.settle()
            pt = lambda i: par[:, i, :]
            for q in range(2):
                s.mark(dve.tensor_copy(ex[64 * q:64 * q + 64, 0:NS],
                                       lst[64 * q:64 * q + 64, :].rearrange("p (s q) -> p q s", q=2)[:, q]))
            for i in (BA, BX, GB):
                s.mark(dve.tensor_scalar(vec[:, i, :], vec[:, i, :], 0.5, None, ALU.mult))
            for j in range(2):
                cj = corr[:, j, :]
                s.link(dve.tensor_copy(cj, io16[:]))
                s.link(dve.tensor_scalar(cj, cj, wcol[:, j:j + 1], None, ALU.min))
                s.link(dve.reciprocal(cj, cj))
                s.link(dve.tensor_scalar(cj, cj, wcol[:, j:j + 1], None, ALU.mult))
            s.link(dve.tensor_scalar(gpar[:, 1:2], gpar[:, 0:1], 4, 1, ALU.logical_shift_right, ALU.bitwise_and))
            s.link(dve.tensor_copy(gmask[:, 1:2], gpar[:, 1:2]))
            s.link(dve.tensor_scalar(gmask[:, 0:1], gmask[:, 1:2], -1.0, 1.0, ALU.mult, ALU.add))
            neg, mabs = par[:, 0, 0:2], ex[:, NS:NS + 2]
            s.link(dve.tensor_scalar(neg, vec[:, LAM, :], -1.0, None, ALU.mult))
            s.link(dve.tensor_tensor(mabs, neg, vec[:, LAM, :], ALU.min))
            nn, ff = par[:, 1:3, :].rearrange("p a b -> p (a b)")[:, 0:NS + 2], par[:, 3:5, :].rearrange("p a b -> p (a b)")[:, 0:NS + 2]
            exp_exact(dve, s, exo[:], ex[:], nn, ff, pari[:])
            e_, z, z2, po = exo[:, NS:NS + 2], par[:, 5, 0:2], par[:, 6, 0:2], par[:, 7, 0:2]
            s.link(dve.tensor_scalar(z, e_, 2.0, None, ALU.add))
            s.link(dve.reciprocal(z, z))
            s.link(dve.tensor_tensor(z, z, e_, ALU.mult))
            s.link(dve.tensor_tensor(z2, z, z, ALU.mult))
            horner(dve, s, po, z2, [1.0 / k for k in range(3, 17, 2)])
            s.link(dve.scalar_tensor_tensor(po, po, 1.0, z, ALU.add, ALU.mult))
            s.link(dve.tensor_scalar(neg, neg, 0.0, None, ALU.max))
            s.link(dve.scalar_tensor_tensor(po, po, 2.0, neg, ALU.mult, ALU.add))
            s.link(dve.tensor_scalar(m4sp[:], po, -4.0, None, ALU.mult))
            LR, X, TH, Q, V, V2, SN, CS, ER, CM1, ST, CO, AR, AI, DEN, CRE, CIM, T1, T2 = range(0, 19)
            step = exo[:, 0:NS]
            s.link(dve.tensor_scalar(pt(LR), lamre[:], -1e-4, None, ALU.min))
            s.link(dve.tensor_tensor(pt(X), pt(LR), step, ALU.mult))
            s.link(dve.tensor_tensor(pt(TH), lamim[:], step, ALU.mult))
            s.link(dve.tensor_scalar(pt(Q), pt(TH), 1.0 / (2 * math.pi), MAGIC, ALU.mult, ALU.add))
            s.link(dve.tensor_scalar(pt(Q), pt(Q), -MAGIC, None, ALU.add))
            s.link(dve.tensor_scalar(pt(V), pt(TH), 0.5, None, ALU.mult))
            pi1 = 3.140625
            pi2 = 9.670257568359375e-4
            pi3 = math.pi - pi1 - pi2
            for pc in (pi1, pi2, pi3):
                s.link(dve.scalar_tensor_tensor(pt(V), pt(Q), -pc, pt(V), ALU.mult, ALU.add))
            s.link(dve.tensor_tensor(pt(V2), pt(V), pt(V), ALU.mult))
            horner(dve, s, pt(SN), pt(V2), [(-1.0) ** k / math.factorial(2 * k + 1) for k in range(1, 8)])
            s.link(dve.scalar_tensor_tensor(pt(SN), pt(SN), 1.0, pt(V), ALU.add, ALU.mult))
            horner(dve, s, pt(CS), pt(V2), [(-1.0) ** k / math.factorial(2 * k) for k in range(1, 9)])
            s.link(dve.tensor_scalar(pt(CS), pt(CS), 1.0, None, ALU.add))
            s.link(dve.tensor_tensor(pt(CM1), pt(SN), pt(SN), ALU.mult))
            s.link(dve.tensor_scalar(pt(CM1), pt(CM1), -2.0, None, ALU.mult))
            s.link(dve.tensor_tensor(pt(ST), pt(SN), pt(CS), ALU.mult))
            s.link(dve.tensor_scalar(pt(ST), pt(ST), 2.0, None, ALU.mult))
            s.link(dve.tensor_scalar(pt(CO), pt(CM1), 1.0, None, ALU.add))
            dve.tensor_copy(tcos[:, :, 0:1], pt(CO).unsqueeze(2)).then_inc(unit_rot, 1)
            dve.tensor_copy(tsin[:, :, 0:1], pt(ST).unsqueeze(2)).then_inc(unit_rot, 1)
            s.link(dve.tensor_scalar(pt(T1), pt(X), -88.0, 1.0 / 128, ALU.max, ALU.mult))
            horner(dve, s, pt(ER), pt(T1), [1.0 / math.factorial(k) for k in range(1, 11)])
            for _ in range(7):
                s.link(dve.scalar_tensor_tensor(pt(ER), pt(ER), 2.0, pt(ER), ALU.add, ALU.mult))
            s.link(dve.tensor_scalar(rdec[:], pt(ER), 1.0, None, ALU.add))
            s.link(dve.tensor_tensor(pt(AR), pt(ER), pt(CO), ALU.mult))
            s.link(dve.tensor_tensor(pt(AR), pt(AR), pt(CM1), ALU.add))
            s.link(dve.tensor_tensor(pt(AI), rdec[:], pt(ST), ALU.mult))
            s.link(dve.tensor_tensor(pt(T1), pt(LR), pt(LR), ALU.mult))
            s.link(dve.tensor_tensor(pt(DEN), lamim[:], lamim[:], ALU.mult))
            s.link(dve.tensor_tensor(pt(DEN), pt(DEN), pt(T1), ALU.add))
            s.link(dve.reciprocal(pt(DEN), pt(DEN)))
            s.link(dve.tensor_tensor(pt(T1), pt(AR), pt(LR), ALU.mult))
            s.link(dve.tensor_tensor(pt(T2), pt(AI), lamim[:], ALU.mult))
            s.link(dve.tensor_tensor(pt(CRE), pt(T1), pt(T2), ALU.add))
            s.link(dve.tensor_tensor(pt(CRE), pt(CRE), pt(DEN), ALU.mult))
            s.link(dve.tensor_tensor(pt(T1), pt(AI), pt(LR), ALU.mult))
            s.link(dve.tensor_tensor(pt(T2), pt(AR), lamim[:], ALU.mult))
            s.link(dve.tensor_tensor(pt(CIM), pt(T1), pt(T2), ALU.subtract))
            s.link(dve.tensor_tensor(pt(CIM), pt(CIM), pt(DEN), ALU.mult))
            cre = pt(CRE).unsqueeze(2).to_broadcast([P, NS, 16])
            cim = pt(CIM).unsqueeze(2).to_broadcast([P, NS, 16])
            tb = [m[:, 4 + i, 0:NS * 16].rearrange("p (s h) -> p s h", h=16) for i in range(4)]
            s.mark(dve.tensor_tensor(tb[0], b_nat[0], cre, ALU.mult))
            s.mark(dve.tensor_tensor(tb[1], b_nat[1], cim, ALU.mult))
            s.mark(dve.tensor_tensor(tb[2], b_nat[1], cre, ALU.mult))
            s.link(dve.tensor_tensor(tb[3], b_nat[0], cim, ALU.mult))
            for q in range(2):
                rows = slice(64 * q, 64 * q + 64)
                for i, op in enumerate((ALU.subtract, ALU.add)):
                    dst = m[rows, i, 0:2 * P].rearrange("p (s h) -> p s h", h=32)[:, :, 16 * q:16 * q + 16]
                    s.link(dve.tensor_tensor(dst, tb[2 * i][rows], tb[2 * i + 1][rows], op))
            for i in range(2):
                for q in range(2):
                    dst = m[:, 2 + i, 0:2 * P].rearrange("p (u w) -> p u w", w=P)[:, :, 64 * q:64 * q + 64]
                    s.link(dve.tensor_scalar(dst, c_nat[i], gmask[:, q:q + 1], None, ALU.mult))
            dve.sem_inc(pre_t, 1)
            dve.wait_ge(pre_tt, 1)
            dve.sem_inc(passed, 1)

            s = Steps(dve, dstep, DVE_STEPS)
            with dve.Fori(0, CH) as c:
                s.trip(dve.snap(c * DVE_STEPS))
                gb = dve.snap(c * GPER)
                bb = dve.snap(c * BPER)
                cs = dve.snap(c * NS)
                c2 = dve.snap(c * 2)
                dve.wait_ge(sq_done, c * TC + TC)
                s.link(dve.tensor_scalar(msq[:], ssq[:], 1.0 / D, EPS, ALU.mult, ALU.add))
                rsqrt_steps(dve, s, msq[:], rhalf[:], rst[:], rtmp[:])
                for t in range(TC):
                    dve.scalar_tensor_tensor(xin[:, t], xin[:, t], rst[:, t:t + 1], g1[:], ALU.mult, ALU.mult).then_inc(xh_full, 1)

                def stood(f):
                    dve.wait_ge(gr.free, gb + gr.turn(("f", f)) + 2)

                for j in range(2):
                    stood(10 + j)
                    s.link(dve.tensor_scalar(xc[:, j], lx[:, j, 3:3 + CT], cwl[:, 3, j:j + 1], vec[:, LCB, j:j + 1], ALU.mult, ALU.add))
                    for k in (2, 1, 0):
                        i = dve.scalar_tensor_tensor(xc[:, j], lx[:, j, k:k + CT], cwl[:, k, j:j + 1], xc[:, j], ALU.mult, ALU.add)
                        if k:
                            s.link(i)
                    i.then_inc(xc_full, 1)
                dve.wait_ge(xc_full, c2 + 2)
                s.mark(dve.tensor_copy(lx[:, :, 0:3], lx[:, :, CT:CT + 3]))

                def s5_in(n):
                    dve.wait_ge(s_full, cs + n + 1)
                    dve.tensor_tensor(m[:, 0], sre[:], tcos[:, n], ALU.mult)
                    s.mark(dve.tensor_tensor(m[:, 1], sim_[:], tsin[:, n], ALU.mult))
                    dve.tensor_tensor(m[:, 2], sim_[:], tcos[:, n], ALU.mult)
                    s.link(dve.tensor_tensor(m[:, 3], sre[:], tsin[:, n], ALU.mult))
                    dve.sem_inc(s_free, 1)
                    dve.sem_inc(rot_in, 1)

                def s5_scan(n):
                    dve.wait_ge(scan_d, 2 * cs + 2 * n + 2)
                    r = rdec[:, n:n + 1].to_broadcast([P, CT])
                    s.mark(dve.tensor_tensor_scan(m[:, 1], r, m[:, 0], scar[:, 0, n:n + 1], ALU.mult, ALU.add))
                    s.link(dve.tensor_tensor_scan(m[:, 3], r, m[:, 2], scar[:, 1, n:n + 1], ALU.mult, ALU.add))
                    dve.wait_ge(h_full, 2 * cs + 2 * n) if n else None
                    dve.tensor_tensor(m[:, 4], m[:, 1], tcos[:, n], ALU.mult)
                    s.mark(dve.tensor_tensor(m[:, 5], m[:, 3], tsin[:, n], ALU.mult))
                    dve.tensor_tensor(m[:, 6], m[:, 3], tcos[:, n], ALU.mult)
                    s.link(dve.tensor_tensor(m[:, 7], m[:, 1], tsin[:, n], ALU.mult))
                    dve.sem_inc(rot_m, 1)

                def lru_gate_poly():
                    for j in range(2):
                        stood(12 + j)
                        s.link(dve.tensor_scalar(lq[:, j], lq[:, j], GELU_C, 1.0, ALU.mult, ALU.add))
                        dve.tensor_tensor(lq[:, j], lq[:, j], lg[:, j], ALU.mult).then_inc(gl_u, 1)

                def lru_q_():
                    for j in range(2):
                        dve.wait_ge(lru_a, c * 6 + 2 + 2 * j + 2)
                        dve.scalar_tensor_tensor(lru[:, j, 3], lru[:, j, 3], 1.0, lru[:, j, 0], ALU.add, ALU.mult).then_inc(lru_q, 1)

                def lru_out():
                    dve.wait_ge(ys_out[3], 16 * c + 16)
                    for j in range(2):
                        dve.wait_ge(lru_m, c2 + j + 1)
                        s.link(dve.scalar_tensor_tensor(lru[:, j, 1], lru[:, j, 1], 1.0, xc[:, j], ALU.add, ALU.mult))
                        s.link(dve.tensor_tensor(lru[:, j, 1], lru[:, j, 1], lru[:, j, 3], ALU.mult))
                        s.link(dve.tensor_tensor_scan(lru[:, j, 0], lru[:, j, 2], lru[:, j, 1], hcar[:, j:j + 1], ALU.mult, ALU.add))
                        s.mark(dve.tensor_copy(hcar[:, j:j + 1], lru[:, j, 0, CT - 1:CT]))
                        dve.wait_ge(gl_t, c2 + j + 1)
                        s.link(dve.scalar_tensor_tensor(lg[:, j], lq[:, j], 1.0, lg[:, j], ALU.add, ALU.mult))
                        dve.scalar_tensor_tensor(ys[:, 3, j], lru[:, j, 0], 0.5, lg[:, j], ALU.mult, ALU.mult).then_inc(ys_full, 1)

                def pool_mix():
                    dve.wait_ge(ys_out[1], 16 * c + 16)
                    H = MAXW - 1
                    N = CT + H
                    for j in range(2):
                        stood(6 + j)
                        u = pu[:, j]
                        a, b = pw_[0], pw_[1]
                        if j == 0:
                            s.mark(dve.tensor_tensor(b[0:64, H:N], u[0:64, H:N], u[0:64, H - 1:N - 1], ALU.add))
                            s.link(dve.tensor_tensor(a[64:P, 1:N], u[64:P, 1:N], u[64:P, 0:N - 1], ALU.add))
                            s.link(dve.tensor_tensor(b[64:P, H:N], a[64:P, H:N], a[64:P, H - 2:N - 2], ALU.add))
                        else:
                            s.link(dve.tensor_tensor(a[:, 1:N], u[:, 1:N], u[:, 0:N - 1], ALU.add))
                            s.link(dve.tensor_tensor(b[:, 3:N], a[:, 3:N], a[:, 1:N - 2], ALU.add))
                            s.link(dve.tensor_tensor(a[:, 7:N], b[:, 7:N], b[:, 3:N - 4], ALU.add))
                            s.mark(dve.tensor_copy(b[0:64, H:N], a[0:64, H:N]))
                            s.link(dve.tensor_tensor(b[64:P, H:N], a[64:P, H:N], a[64:P, H - 8:N - 8], ALU.add))
                        s.link(dve.tensor_tensor(b[:, H:H + MAXW], b[:, H:H + MAXW], corr[:, j], ALU.mult))
                        dve.scalar_tensor_tensor(ys[:, 1, j], b[:, H:N], invw[:, j:j + 1], u[:, H:N], ALU.mult, ALU.subtract).then_inc(pooled, 1)
                        dve.wait_ge(pooled, c2 + j + 1)
                    s.mark(dve.tensor_copy(pu[:, :, 0:H], pu[:, :, CT:N]))
                    s.mark(dve.memset(corr[:], 1.0))

                def pool_out():
                    for j in range(2):
                        dve.wait_ge(br.full, bb + br.turn(("pool", j)))
                        s.link(dve.tensor_scalar(ys[:, 1, j], br.bank(("pool", j))[:], vec[:, PB, j:j + 1], vec[:, PSC, j:j + 1], ALU.add, ALU.mult))
                        dve.sem_inc(br.free, 1)
                        dve.sem_inc(ys_full, 1)

                def conv_a(j):
                    stood(2 + j)
                    dve.wait_ge(br.full, bb + br.turn(("f", 4 + j)))
                    dve.tensor_tensor(va[:, j, 2:2 + CT], br.bank(("f", 4 + j))[:], bgcg[:, 2 + j], ALU.mult).then_inc(br.free, 1)
                    dve.wait_ge(br.free, bb + br.turn(("f", 4 + j)) + 2)
                    y = pw_[j][:, 0:CT]
                    s.link(dve.tensor_scalar(y, va[:, j, 2:2 + CT], cwa[:, 2, j:j + 1], None, ALU.mult))
                    for k in (1, 0):
                        s.link(dve.scalar_tensor_tensor(y, va[:, j, k:k + CT], cwa[:, k, j:j + 1], y, ALU.mult, ALU.add))
                    stood(j)
                    if j == 0:
                        dve.wait_ge(ys_out[0], 16 * c + 16)
                    dve.tensor_tensor(ys[:, 0, j], y, bgcg[:, j], ALU.mult).then_inc(ys_full, 1)
                    s.mark(dve.tensor_copy(va[:, j, 0:2], va[:, j, CT:CT + 2]))

                def y_in(u):
                    dve.wait_ge(y_full, cs + 4 * u + 4)
                    dve.scalar_tensor_tensor(yg[:, u], su[:, u], vec[:, SD, u:u + 1], yps[:], ALU.mult, ALU.add).then_inc(y_free, 1)
                    dve.wait_ge(y_free, c2 + u + 2)
                    dve.sem_inc(y_pre, 1)

                for n in range(10):
                    if n >= 1 and n <= NS:
                        s5_scan(n - 1)
                    if n == 0:
                        dve.wait_ge(tabs, n_tabs)
                    if n < NS:
                        s5_in(n)
                    if n == 1:
                        lru_gate_poly()
                    if n == 2:
                        lru_q_()
                    if n == 4:
                        pool_mix()
                    if n == 6:
                        y_in(0)
                        lru_out()
                        pool_out()
                    if n == 7:
                        conv_a(0)
                    if n == 9:
                        y_in(1)
                for j in range(2):
                    dve.wait_ge(y_sq, c2 + j + 1)
                    s.link(dve.tensor_scalar(yq[:, j], yq[:, j], GELU_C, 1.0, ALU.mult, ALU.add))
                    dve.tensor_tensor(yq[:, j], yq[:, j], yg[:, j], ALU.mult).then_inc(y_u, 1)
                conv_a(1)
                for j in range(2):
                    dve.wait_ge(y_t, c2 + j + 1)
                    dve.scalar_tensor_tensor(yg[:, j], yq[:, j], 1.0, yg[:, j], ALU.add, ALU.mult).then_inc(yg_full, 1)
                dve.wait_ge(ys_out[2], 16 * c + 16)
                for j in range(2):
                    dve.wait_ge(gr.free, gb + gr.turn(("glu", j)) + 2)
                    dve.wait_ge(yg_full, c2 + 2)
                    s.link(dve.scalar_tensor_tensor(yq[:, j], yq[:, j], 1.0, yg[:, j], ALU.add, ALU.mult))
                    dve.tensor_scalar(ys[:, 2, j], yq[:, j], 0.25, None, ALU.mult).then_inc(ys_full, 1)
                assert s.n == DVE_STEPS, s.n


def merge_branches(nc, io, dram, logits):
    TM = 512
    TRIPS = T // TM
    MT = TM // P
    RSQ = 14
    NORM_STEPS = 1 + RSQ
    STEP_DVE = NBR - 1
    TRIP_DVE = KD * STEP_DVE + MT * NORM_STEPS
    WK = KD + 2
    PIECE = 4
    PIECES = (KD + 2 * NBR) // PIECE
    SU = NBR
    assert PIECES == MT == 4
    with ExitStack() as ctx:
        def sb(name, shape, dt=F32):
            return ctx.enter_context(nc.sbuf_tensor(name, shape, dt))

        def sem(name):
            return ctx.enter_context(nc.semaphore(name))

        ps = [ctx.enter_context(nc.psum_tensor(f"mrgps{i}", [P, 512], F32)) for i in range(5)]
        act_hi, act_lo = sb("act_hi", [P, KD + 2 * NBR, TM], F32R), sb("act_lo", [P, KD + 2 * NBR, TM], F32R)
        act_raw = sb("act_raw", [P, 2, PIECE * TM])
        merged = sb("merged", [P, KD, TM])
        wout = sb("wout", [P, KD, D])
        w_raw = sb("w_raw", [P, NBR, WK, P])
        w_hi, w_lo = sb("w_hi", [P, 2, WK, P], F32R), sb("w_lo", [P, 2, WK, P], F32R)
        gt, tmp = sb("gt", [P, TM]), sb("tmp", [P, TM])
        xr, xn = sb("xr", [P, 2, D]), sb("xn", [P, 2, D])
        xnT = sb("xnT", [P, KD, P])
        sqj = sb("sqj", [P, D])
        g2 = sb("g2", [P, D])
        rw = sb("rw", [P, KD, R])
        rb = sb("rb", [P, R])
        mb = sb("mb", [P, NBR, KD])
        ident = sb("m_ident", [P, P])
        ssq, msq, rst, rh, rt = (sb(f"m_st{i}", [P, 2]) for i in range(5))

        GPER = BPER = KD * SU + 2 * MT
        g_full, g_free, b_full, b_free = sem("gate_full"), sem("gate_free"), sem("prod_full"), sem("prod_free")
        gbank, bbank, rps = ps[0:2], ps[2:4], ps[4]
        r_full, r_free = sem("router_full"), sem("router_free")
        par_in, idz, idn = sem("m_params_in"), sem("m_ident_zero"), sem("m_ident")
        w_in, w_hi_set, w_split = [sem(f"mw_in{k}") for k in range(NBR)], sem("w_hi_set"), sem("w_split")
        act_in, act_hi_set, act_split = [sem(f"acts_in{i}") for i in range(2)], sem("act_hi_set"), sem("act_split")
        wout_in = sem("wout_in")
        x_in, h_out, n_out = ([sem(f"{n}{i}") for i in range(2)] for n in ("xr_in", "h_out", "n_out"))
        h_done, sq_done, n_full = sem("h_done"), sem("h_squared"), sem("xn_full")
        half_b, dstep, passed = sem("half_bias"), sem("m_dve_step"), sem("m_passed")
        block = ctx.enter_context(nc.Block())

        params = ((mb[:], io["merge_gate_b"][0].rearrange("(k d p) -> p k d", k=NBR, p=P)),
                  (g2[:], io["norm2_g"][0:1].partition_broadcast(P)),
                  (rw[:, :, 0:G], io["router_group_w"][0].rearrange("(k p) n -> p k n", p=P)),
                  (rw[:, :, G:R], io["router_expert_w"][0].rearrange("(k p) n -> p k n", p=P)),
                  (rb[:, 0:G], io["router_group_b"][0:1].partition_broadcast(P)),
                  (rb[:, G:R], io["router_expert_b"][0:1].partition_broadcast(P)))

        @block.sync
        def _(sp):
            def load_piece(m, c):
                cols = ds(m * TM, TM)
                if c < PIECES // 2:
                    src = dram["xT"][PIECE * c:PIECE * (c + 1), :, cols].rearrange("k p t -> p k t")
                else:
                    b = 2 * (c - PIECES // 2)
                    src = dram["ys"][b:b + 2, :, :, cols].rearrange("b j p t -> p (b j) t")
                sp.dma_start(act_raw[:, c % 2].rearrange("p (k t) -> p k t", t=TM), src).then_inc(act_in[c % 2], 16)

            def load_weights(k, d):
                sp.dma_start(w_raw[:, k, 0:KD], io["merge_gate_w"][0, :, ds(k * D + d * P, P)].rearrange("(k p) n -> p k n", p=P))\
                  .then_inc(w_in[k], 16)
                sp.dma_start(w_raw[:, k, KD:WK], io["branch_w"][0, k, :, ds(d * P, P)].rearrange("(k p) n -> p k n", p=P))\
                  .then_inc(w_in[k], 16)

            load_piece(0, 0)
            load_weights(0, 0)
            load_piece(0, 1)
            for k in range(1, NBR):
                load_weights(k, 0)
            for c in range(2, PIECES):
                sp.wait_ge(act_split, c - 1)
                load_piece(0, c)
            for dst, src in params:
                sp.dma_start(dst, src, allow_slow_non_contiguous=True).then_inc(par_in, 16)
            sp.dma_start(wout[:], io["w_out"][0].rearrange("(k p) n -> p k n", p=P)).then_inc(wout_in, 16)
            for i in range(2):
                sp.sem_inc(h_out[i], 16)
                sp.sem_inc(n_out[i], 16)
            with sp.Fori(0, TRIPS) as m:
                with sp.Fori(0, KD) as d:
                    for k in range(NBR):
                        sp.wait_ge(w_split, (m * KD + d) * SU + (k + 1))
                        load_weights(k, (d + 1) % KD)
                m8 = sp.snap(m * MT)

                def load_x(t):
                    sp.wait_ge(h_out[t % 2], 16 * (MT // 2) * m + 16 * (t // 2) + 16)
                    sp.dma_start(xr[:, t % 2], io["x"][0, ds(m * TM + t * P, P), :]).then_inc(x_in[t % 2], 16)

                load_x(0)
                load_x(1)
                for c in range(2):
                    sp.wait_ge(act_split, m * PIECES + (PIECES + c - 1))
                    load_piece((m + 1) % TRIPS, c)
                for t in range(MT):
                    if t + 2 < PIECES:
                        sp.wait_ge(act_split, m * PIECES + (PIECES + t + 1))
                        load_piece((m + 1) % TRIPS, t + 2)
                    sp.wait_ge(h_done, m8 + t + 1)
                    sp.dma_start(dram["h"][ds(m * TM + t * P, P), :], xr[:, t % 2]).then_inc(h_out[t % 2], 16)
                    sp.wait_ge(n_full, m8 + t + 1)
                    sp.dma_start(dram["xn"][ds(m * TM + t * P, P), :], xn[:, t % 2]).then_inc(n_out[t % 2], 16)
                    if t + 2 < MT:
                        load_x(t + 2)
            for i in range(2):
                sp.wait_ge(h_out[i], 16 + 16 * TRIPS * MT // 2)
                sp.wait_ge(n_out[i], 16 + 16 * TRIPS * MT // 2)
            for k in range(NBR):
                sp.wait_ge(w_in[k], 32 * (1 + TRIPS * KD))

        @block.gpsimd
        def _(pool):
            pool.memset(ident[:], 0.0).then_inc(idz, 1)
            pool.wait_ge(idz, 1)
            pool.affine_select(out=ident[:], in_=ident[:], compare_op=ALU.not_equal, fill=1.0, base=0,
                               pattern=[[-1, P]], channel_multiplier=1).then_inc(idn, 1)

        @block.scalar
        def _(act):
            act.sem_inc(g_free, 2)

            def piece_high(n, c):
                act.wait_ge(act_in[c % 2], n * 16)
                act.sem_inc(passed, 1)
                act.activation(act_hi[:, PIECE * c:PIECE * (c + 1)].rearrange("p k t -> p (k t)"), act_raw[:, c % 2],
                               ACT.Copy).then_inc(act_hi_set, 1)

            def weights_high(n, k):
                act.wait_ge(w_in[k], n * 32)
                act.sem_inc(passed, 1)
                act.activation(w_hi[:, k % 2].rearrange("p k n -> p (k n)"), w_raw[:, k].rearrange("p k n -> p (k n)"),
                               ACT.Copy).then_inc(w_hi_set, 1)

            piece_high(1, 0)
            weights_high(1, 0)
            for c in range(1, PIECES):
                piece_high(c // 2 + 1, c)
            act.wait_ge(half_b, 1)
            with act.Fori(0, TRIPS) as m:
                with act.Fori(0, KD) as d:
                    gb = act.snap(m * GPER + d * SU)
                    md = act.snap(m * KD + d)
                    for k in range(NBR):
                        act.wait_ge(b_free, gb + k + 2)
                        weights_high(md + (1 if k + 1 < NBR else 2), (k + 1) % NBR)
                        act.wait_ge(g_full, gb + k + 1)
                        act.sem_inc(passed, 1)
                        act.activation(gt[:], gbank[k % 2][:], ACT.Tanh, scale=0.5, bias=mb[:, k, ds(d, 1)]).then_inc(g_free, 1)
                gb = act.snap(m * GPER + KD * SU)
                m8 = act.snap(m * MT)

                def square(t):
                    act.wait_ge(h_done, m8 + t + 1)
                    act.wait_ge(sq_done, m8 + t + 1)
                    act.activation(sqj[:], xr[:, t % 2], ACT.Square, accum_out=ssq[:, t % 2:t % 2 + 1]).then_inc(sq_done, 1)

                def turn(t):
                    act.wait_ge(r_full, m8 + t + 1)
                    for h in range(2):
                        act.wait_ge(g_full, gb + 2 * t + h + 1)
                        act.activation(xnT[:, 4 * h:4 * h + 4, :].rearrange("p k t -> p (k t)"), gbank[h][:],
                                       ACT.Copy).then_inc(g_free, 1)

                act.wait_ge(b_free, gb + 2)
                piece_high(m * 2 + 3, 0)
                square(0)
                for t in range(1, MT):
                    piece_high(m * 2 + (t // 2 + 3), t)
                    square(t)
                    turn(t - 1)
                turn(MT - 1)

        @block.tensor
        def _(pe):
            pe.sem_inc(r_full, 1)
            pe.wait_ge(idn, 1)
            with pe.Fori(0, TRIPS) as m:
                pe.wait_ge(act_split, m * PIECES + KD // PIECE)
                pe.sem_inc(passed, 1)
                with pe.Fori(0, KD) as d:
                    base = pe.snap(m * GPER + d * SU)
                    first = pe.snap((m * KD + d) * SU)
                    pieces = pe.snap(m * PIECES + PIECES)

                    def product(bank, k, w_tiles, a_tile):
                        for kk in w_tiles:
                            a = a_tile + kk - w_tiles[0]
                            for w, x in ((w_hi, act_hi), (w_hi, act_lo), (w_lo, act_hi)):
                                last = pe.matmul(bank[:], w[:, k % 2, kk], x[:, a], start=(kk == w_tiles[0] and x is act_hi and w is w_hi),
                                                 stop=(kk == w_tiles[-1] and w is w_lo))
                        return last

                    for k in range(NBR):
                        pe.wait_ge(w_split, first + k + 1)
                        pe.wait_ge(g_free, base + k + 1)
                        product(gbank[k % 2], k, range(KD), 0).then_inc(g_full, 1)
                        if k == 0:
                            pe.wait_ge(act_split, pieces)
                        pe.wait_ge(b_free, base + k + 1)
                        product(bbank[k % 2], k, range(KD, WK), KD + 2 * k).then_inc(b_full, 1)
                base = pe.snap(m * GPER + KD * SU)
                m8 = pe.snap(m * MT)

                def project(t):
                    for h in range(2):
                        pe.wait_ge(b_free, base + 2 * t + h + 1)
                        for kk in range(KD):
                            last = pe.matmul(bbank[h][:], merged[:, kk, t * P:(t + 1) * P], wout[:, kk, h * 512:(h + 1) * 512],
                                             start=(kk == 0), stop=(kk == KD - 1))
                        last.then_inc(b_full, 1)

                def turn(t):
                    pe.wait_ge(n_full, m8 + t + 1)
                    for h in range(2):
                        pe.wait_ge(g_free, base + 2 * t + h + 1)
                        for kk in range(4):
                            last = pe.transpose(gbank[h][:, kk * P:(kk + 1) * P], xn[:, t % 2, (4 * h + kk) * P:(4 * h + kk + 1) * P], ident[:])
                        last.then_inc(g_full, 1)

                def rout(t):
                    pe.wait_ge(g_free, base + 2 * t + 4)
                    pe.wait_ge(r_free, m8 + t + 1)
                    for kk in range(KD):
                        last = pe.matmul(rps[:, 0:R], xnT[:, kk], rw[:, kk], start=(kk == 0), stop=(kk == KD - 1))
                    last.then_inc(r_full, 1)

                pe.wait_ge(wout_in, 16)
                pe.wait_ge(par_in, 16 * len(params))
                pe.wait_ge(dstep, m * TRIP_DVE + KD * STEP_DVE)
                project(0)
                for t in range(1, MT):
                    project(t)
                    if t >= 2:
                        rout(t - 2)
                    turn(t - 1)
                rout(MT - 2)
                turn(MT - 1)
                rout(MT - 1)

        @block.vector
        def _(dve):
            dve.sem_inc(b_free, 2)
            dve.sem_inc(r_free, 1)
            dve.sem_inc(sq_done, 1)

            def piece_low(n, c):
                dve.wait_ge(act_hi_set, n)
                hi = act_hi[:, PIECE * c:PIECE * (c + 1)].rearrange("p k t -> p (k t)")
                dve.tensor_tensor(act_lo[:, PIECE * c:PIECE * (c + 1)].rearrange("p k t -> p (k t)"), act_raw[:, c % 2],
                                  hi.bitcast(F32), ALU.subtract).then_inc(act_split, 1)

            def weights_low(n, k):
                dve.wait_ge(w_hi_set, n)
                hi, lo = (w[:, k % 2].rearrange("p k n -> p (k n)") for w in (w_hi, w_lo))
                dve.tensor_tensor(lo, w_raw[:, k].rearrange("p k n -> p (k n)"), hi.bitcast(F32), ALU.subtract).then_inc(w_split, 1)

            piece_low(1, 0)
            weights_low(1, 0)
            for c in range(1, PIECES):
                piece_low(c + 1, c)
            dve.wait_ge(par_in, 16 * len(params))
            dve.tensor_scalar(mb[:], mb[:], 0.5, None, ALU.mult).then_inc(half_b, 1)
            s = Steps(dve, dstep)
            with dve.Fori(0, TRIPS) as m:
                with dve.Fori(0, KD) as d:
                    gb = dve.snap(m * GPER + d * SU)
                    s.trip(dve.snap(m * TRIP_DVE + d * STEP_DVE))
                    first = dve.snap((m * KD + d) * SU)
                    acc = merged[:, ds(d, 1), :].rearrange("p a t -> p (a t)")
                    for k in range(NBR):
                        weights_low(first + k + 2, (k + 1) % NBR)
                        dve.wait_ge(b_full, gb + k + 1)
                        dve.wait_ge(g_free, gb + k + 3)
                        if k == 0:
                            dve.scalar_tensor_tensor(acc, gt[:], 1.0, bbank[k % 2][:], ALU.add, ALU.mult).then_inc(b_free, 1)
                        else:
                            dve.scalar_tensor_tensor(tmp[:], gt[:], 1.0, bbank[k % 2][:], ALU.add, ALU.mult).then_inc(b_free, 1)
                            dve.wait_ge(b_free, gb + k + 3)
                            s.link(dve.tensor_tensor(acc, acc, tmp[:], ALU.add))
                gb = dve.snap(m * GPER + KD * SU)
                m8 = dve.snap(m * MT)
                s.trip(dve.snap(m * TRIP_DVE + KD * STEP_DVE))

                def residual(t):
                    dve.wait_ge(x_in[t % 2], 16 * (MT // 2) * m + 16 * (t // 2) + 16)
                    for h in range(2):
                        half = xr[:, t % 2, h * 512:(h + 1) * 512]
                        dve.wait_ge(b_full, gb + 2 * t + h + 1)
                        dve.scalar_tensor_tensor(half, bbank[h][:], 0.5, half, ALU.mult, ALU.add).then_inc(b_free, 1)
                    dve.wait_ge(b_free, gb + 2 * t + 4)
                    dve.sem_inc(h_done, 1)

                def norm(t):
                    p = t % 2
                    one = slice(p, p + 1)
                    dve.wait_ge(sq_done, m8 + t + 2)
                    s.link(dve.tensor_scalar(msq[:, one], ssq[:, one], 1.0 / D, EPS, ALU.mult, ALU.add))
                    rsqrt_steps(dve, s, msq[:, one], rh[:, one], rst[:, one], rt[:, one])
                    if t >= 2:
                        dve.wait_ge(g_full, gb + 2 * (t - 2) + 2)
                    dve.wait_ge(n_out[p], 16 * (MT // 2) * m + 16 * (t // 2) + 16)
                    dve.scalar_tensor_tensor(xn[:, p], xr[:, p], rst[:, one], g2[:], ALU.mult, ALU.mult).then_inc(n_full, 1)

                def logit(t):
                    dve.wait_ge(r_full, m8 + t + 2)
                    dve.tensor_tensor(logits[:, ds(m8 + t, 1), :].rearrange("p a r -> p (a r)"), rps[:, 0:R], rb[:], ALU.add).then_inc(r_free, 1)

                pieces = dve.snap(m * PIECES + PIECES)
                piece_low(pieces + 1, 0)
                residual(0)
                for t in range(1, MT):
                    norm(t - 1)
                    piece_low(pieces + (t + 1), t)
                    residual(t)
                    if t >= 3:
                        logit(t - 3)
                norm(MT - 1)
                for t in range(MT - 3, MT):
                    logit(t)
                assert s.n == MT * NORM_STEPS, s.n


def route(nc, logits, table, pos, wts, ends, wt):
    with ExitStack() as ctx:
        def sb(name, shape, dt=F32):
            return ctx.enter_context(nc.sbuf_tensor(name, shape, dt))

        def sem(name):
            return ctx.enter_context(nc.semaphore(name))

        rank_ps, tot_ps, tab_ps = (ctx.enter_context(nc.psum_tensor(f"rtps{i}", [P, 512], F32)) for i in range(3))
        NBT = NB + 1
        gmax, gsum, gval = (sb(f"rt_g{i}", [P, TT]) for i in range(3))
        gd, geq = sb("gd", [P, TT, G]), sb("geq", [P, TT, G])
        gi, m1, m2, dd = (sb(f"rt_m{i}", [P, TT]) for i in range(4))
        em, eq = sb("em", [P, TT, E]), sb("eq", [P, TT, E])
        oh = [sb(f"oh{i}", [P, TT, E]) for i in range(2)]
        hot = sb("hot", [P, TT, E])
        io_g, io_e, io_s, io_b, io_tok, io_blk = (sb("io_g", [P, G]), sb("io_e", [P, E]), sb("io_s", [P, P]), sb("io_b", [P, NBT]),
                                                  sb("io_tok", [P, TT]), sb("io_blk", [P, TT]))
        tri, ones = sb("tri", [P, P]), sb("ones", [P, P])
        cum, tot = sb("cum", [P, TT, E]), sb("tot", [P, TT, E])
        cnt, nb, nbi, nbe, e1 = (sb(f"rt_c{i}", [P, E]) for i in range(5))
        big = sb("big", [P, E, TT])
        off = sb("off", [P, TT, E])
        posf = sb("posf", [P, TT, 2])
        posb, poss = sb("posb", [P, TT, 2], I32), sb("poss", [P, TT, 2], I32)
        blkf, slotf = sb("blkf", [P, TT, 2]), sb("slotf", [P, TT, 2])
        V, U = sb("V", [P, TT, 2, P]), sb("U", [P, TT, 2, NBT])
        consts, ones_set, step = sem("rt_consts"), sem("rt_ones"), sem("rt_steps")
        d_ready, e_done, d2_ready, e2_done = sem("group_diff"), sem("group_exp"), sem("expert_diff"), sem("expert_exp")
        hot_ready, ranks, uv_ready, tab_ready = sem("hot_ready"), sem("ranks"), sem("uv_ready"), sem("table_ready")
        block = ctx.enter_context(nc.Block())

        @block.gpsimd
        def _(pool):
            kw = dict(allow_small_or_imprecise_dtypes=True)
            pool.iota(io_g[:], [[1, G]], base=0, channel_multiplier=0, **kw).then_inc(consts, 1)
            pool.iota(io_e[:], [[1, E]], base=0, channel_multiplier=0, **kw).then_inc(consts, 1)
            pool.iota(io_s[:], [[1, P]], base=0, channel_multiplier=0, **kw).then_inc(consts, 1)
            pool.iota(io_b[:], [[1, NBT]], base=0, channel_multiplier=0, **kw).then_inc(consts, 1)
            pool.iota(io_tok[:], [[P, TT]], base=0, channel_multiplier=1, **kw).then_inc(consts, 1)
            pool.iota(io_blk[:], [[P, TT]], base=0, channel_multiplier=0, **kw).then_inc(consts, 1)
            pool.memset(ones[:], 1.0).then_inc(consts, 1)
            pool.wait_ge(consts, 7)
            pool.affine_select(out=tri[:], in_=ones[:], compare_op=ALU.is_gt, fill=0.0, base=0,
                               pattern=[[1, P]], channel_multiplier=-1).then_inc(consts, 1)
            for i in range(4):
                wt.write_low13(pool, 0, i)
            wt.write_low2(pool, 0)

        @block.sync
        def _(sp):
            for i in range(4):
                wt.load13(sp, 0, i)
            wt.load2(sp, 0)

        @block.scalar
        def _(act):
            act.wait_ge(d_ready, 1)
            act.activation(geq[:], gd[:], ACT.Exp).then_inc(e_done, 1)
            act.wait_ge(d2_ready, 1)
            act.activation(dd[:], dd[:], ACT.Exp).then_inc(e2_done, 1)
            for i in range(4):
                wt.write_high13(act, 0, i)
            wt.write_high2(act, 0)

        @block.tensor
        def _(pe):
            pe.wait_ge(consts, 8)
            pe.wait_ge(hot_ready, 1)
            h = hot[:].rearrange("p t e -> p (t e)")
            pe.matmul(rank_ps[:], tri[:], h, start=True, stop=True)
            pe.matmul(tot_ps[:], ones[:], h, start=True, stop=True).then_inc(ranks, 1)
            pe.wait_ge(uv_ready, 1)
            for i in range(TT):
                for k in range(2):
                    last = pe.matmul(tab_ps[:, 0:NBT], V[:, i, k], U[:, i, k], start=(i + k == 0), stop=(i == TT - 1 and k == 1))
            last.then_inc(tab_ready, 1)

        @block.vector
        def _(dve):
            s = Steps(dve, step)
            TTc = dve.tensor_tensor
            bc = lambda ap, n: ap.unsqueeze(2).to_broadcast([P, TT, n])
            row = lambda ap, n: ap.unsqueeze(1).to_broadcast([P, TT, n])
            lgG, lgE = logits[:, :, 0:G], logits[:, :, G:R]

            def first_hot(dst, vals, best, iota_row, n, tmpv, idx):
                s.link(TTc(tmpv, vals, bc(best, n), ALU.is_equal))
                s.link(dve.scalar_tensor_tensor(tmpv, tmpv, -64.0, row(iota_row, n), ALU.mult, ALU.add))
                s.link(dve.tensor_reduce(idx, tmpv, AX.X, ALU.min))
                s.link(dve.tensor_scalar(idx, idx, 64.0, None, ALU.add))
                s.link(TTc(dst, row(iota_row, n), bc(idx, n), ALU.is_equal))

            s.link(dve.tensor_reduce(gmax[:], lgG, AX.X, ALU.max))
            TTc(gd[:], lgG, bc(gmax[:], G), ALU.subtract).then_inc(d_ready, 1)
            dve.wait_ge(e_done, 1)
            s.link(dve.tensor_reduce(gsum[:], geq[:], AX.X, ALU.add))
            s.link(dve.reciprocal(gval[:], gsum[:]))
            dve.wait_ge(consts, 8)
            first_hot(gd[:], lgG, gmax[:], io_g[:], G, geq[:], gi[:])
            s.link(dve.tensor_scalar(gd[:], gd[:], -1.0, 1e30, ALU.add, ALU.mult))
            for g in range(G):
                s.mark(TTc(em[:, :, EPG * g:EPG * (g + 1)], lgE[:, :, EPG * g:EPG * (g + 1)],
                           gd[:, :, g:g + 1].to_broadcast([P, TT, EPG]), ALU.add))
            s.settle()
            s.link(dve.tensor_reduce(m1[:], em[:], AX.X, ALU.max))
            first_hot(oh[0][:], em[:], m1[:], io_e[:], E, eq[:], gi[:])
            s.link(dve.scalar_tensor_tensor(em[:], oh[0][:], -3e38, em[:], ALU.mult, ALU.add))
            s.link(dve.tensor_reduce(m2[:], em[:], AX.X, ALU.max))
            TTc(dd[:], m2[:], m1[:], ALU.subtract).then_inc(d2_ready, 1)
            first_hot(oh[1][:], em[:], m2[:], io_e[:], E, eq[:], gi[:])
            TTc(hot[:], oh[0][:], oh[1][:], ALU.add).then_inc(hot_ready, 1)
            dve.wait_ge(e2_done, 1)
            s.link(dve.tensor_scalar(gsum[:], dd[:], 1.0, None, ALU.add))
            s.link(dve.reciprocal(gsum[:], gsum[:]))
            s.link(TTc(gsum[:], gsum[:], gval[:], ALU.mult))
            s.mark(dve.tensor_copy(wts[:, :, 0], gsum[:]))
            s.mark(TTc(wts[:, :, 1], gsum[:], dd[:], ALU.mult))
            dve.wait_ge(ranks, 1)
            s.link(dve.tensor_copy(tot[:].rearrange("p t e -> p (t e)"), tot_ps[:]))
            s.link(dve.memset(cum[:, 0], 0.0))
            for i in range(1, TT):
                s.link(TTc(cum[:, i], cum[:, i - 1], tot[:, i - 1], ALU.add))
            s.link(TTc(cnt[:], cum[:, TT - 1], tot[:, TT - 1], ALU.add))
            s.link(TTc(big[:], cnt[:].unsqueeze(2).to_broadcast([P, E, TT]), io_blk[:].unsqueeze(1).to_broadcast([P, E, TT]), ALU.is_gt))
            s.link(dve.tensor_reduce(nb[:], big[:], AX.X, ALU.add))
            s.link(dve.tensor_scalar(nb[:], nb[:], 1.0, None, ALU.max))
            s.link(dve.memset(e1[:], 1.0))
            s.link(dve.tensor_tensor_scan(nbi[:], e1[:], nb[:], 0.0, ALU.mult, ALU.add))
            s.link(TTc(nbe[:], nbi[:], nb[:], ALU.subtract))
            s.mark(dve.memset(ends[:, 0:1], 0))
            s.mark(dve.tensor_copy(ends[:, 1:E + 1], nbi[:]))
            s.link(dve.tensor_scalar(nbe[:], nbe[:], float(P), None, ALU.mult))
            s.link(TTc(off[:].rearrange("p t e -> p (t e)"), rank_ps[:], cum[:].rearrange("p t e -> p (t e)"), ALU.add))
            s.link(TTc(off[:], off[:], row(nbe[:], E), ALU.add))
            for k in range(2):
                s.link(TTc(eq[:], oh[k][:], off[:], ALU.mult))
                s.link(dve.tensor_reduce(posf[:, :, k], eq[:], AX.X, ALU.add))
            s.link(dve.tensor_copy(pos[:], posf[:]))
            s.mark(dve.tensor_scalar(posb[:], pos[:], 7, None, ALU.logical_shift_right))
            s.link(dve.tensor_scalar(poss[:], pos[:], P - 1, None, ALU.bitwise_and))
            s.mark(dve.tensor_copy(blkf[:], posb[:]))
            s.link(dve.tensor_copy(slotf[:], poss[:]))
            for k in range(2):
                s.mark(TTc(V[:, :, k], row(io_s[:], P), bc(slotf[:, :, k], P), ALU.is_equal))
                s.link(TTc(U[:, :, k], row(io_b[:], NBT), bc(blkf[:, :, k], NBT), ALU.is_equal))
                s.link(TTc(U[:, :, k], U[:, :, k], bc(io_tok[:], NBT), ALU.mult))
            dve.sem_inc(uv_ready, 1)
            dve.wait_ge(tab_ready, 1)
            s.link(dve.tensor_copy(table[:], tab_ps[:, 0:NBT]))


class ExpertWeights:

    def __init__(self, ctx, nc, io):
        def sb(name, shape, dt):
            return ctx.enter_context(nc.sbuf_tensor(name, shape, dt))

        def sem(name):
            return ctx.enter_context(nc.semaphore(name))

        self.io = io
        self.raw13, self.hi13, self.lo13 = (sb(f"w13_{n}", [P, 4, KD * P * 2], dt) for n, dt in (("raw", F32), ("hi", F32R), ("lo", F32R)))
        self.raw2, self.hi2, self.lo2 = (sb(f"w2_{n}", [P, FE, D], dt) for n, dt in (("raw", F32), ("hi", F32R), ("lo", F32R)))
        self.in13, self.in2 = [sem(f"w13_in{i}") for i in range(4)], sem("w2_in")
        self.high13, self.split13, self.high2, self.split2 = sem("w13_high"), sem("w13_split"), sem("w2_high"), sem("w2_split")

    def load13(self, eng, e, i):
        j, name = i // 2, ("expert_w1", "expert_w3")[i % 2]
        src = self.io[name][0, ds(e, 1), :, j * 256:(j + 1) * 256].rearrange("o (k p) n -> p (o k) n", p=P)
        eng.dma_start(self.raw13[:, i].rearrange("p (k n) -> p k n", n=256), src).then_inc(self.in13[i], 16)

    def load2(self, eng, e):
        eng.dma_start(self.raw2[:], self.io["expert_w2"][0, ds(e, 1)].rearrange("o (k p) n -> p (o k) n", p=P)).then_inc(self.in2, 16)

    def write_high13(self, act, e, i):
        act.wait_ge(self.in13[i], e * 16 + 16)
        act.activation(self.hi13[:, i], self.raw13[:, i], ACT.Copy).then_inc(self.high13, 1)

    def write_high2(self, act, e):
        act.wait_ge(self.in2, e * 16 + 16)
        for f in range(FE):
            act.activation(self.hi2[:, f], self.raw2[:, f], ACT.Copy).then_inc(self.high2, 1)

    def write_low13(self, eng, e, i):
        eng.wait_ge(self.high13, e * 4 + (i + 1))
        eng.tensor_tensor(self.lo13[:, i], self.raw13[:, i], self.hi13[:, i].bitcast(F32), ALU.subtract).then_inc(self.split13, 1)

    def write_low2(self, eng, e):
        for f in range(FE):
            eng.wait_ge(self.high2, e * 4 + (f + 1))
            eng.tensor_tensor(self.lo2[:, f], self.raw2[:, f], self.hi2[:, f].bitcast(F32), ALU.subtract).then_inc(self.split2, 1)


def run_experts(nc, dram, table, ends, wt):
    HC = 256
    with ExitStack() as ctx:
        def sb(name, shape, dt=F32):
            return ctx.enter_context(nc.sbuf_tensor(name, shape, dt))

        def sem(name):
            return ctx.enter_context(nc.semaphore(name))

        ps = [ctx.enter_context(nc.psum_tensor(f"exps{i}", [P, 512], F32)) for i in range(8)]
        tbank, hbank, gbank, ybank = ps[0:2], ps[2:4], ps[4:6], ps[6:8]
        xg = sb("xg", [P, D])
        x_hi, x_lo = sb("xT_hi", [P, KD, P], F32R), sb("xT_lo", [P, KD, P], F32R)
        idx = sb("idx", [P, 1], I32)
        th, gg, hg = sb("th", [P, 2, HC]), sb("gg", [P, 2, HC]), sb("hg", [P, 2, HC])
        h_hi, h_lo = sb("hT_hi", [P, FE, P], F32R), sb("hT_lo", [P, FE, P], F32R)
        ysb = sb("ysb", [P, 2, 512])
        ident = sb("x_ident", [P, P])
        zeros = sb("zeros", [P, D])
        zeros_set, zeros_out = sem("zeros_set"), sem("zeros_out")
        idz, idn = sem("x_ident_zero"), sem("x_ident_set")
        idx_set, gathered, turned, x_high, x_split = sem("idx_set"), sem("gathered"), sem("x_turned"), sem("x_high"), sem("x_split")
        h_ps, tanh_d, gate_d, gated = sem("h_psum"), sem("h_tanh"), sem("h_gate"), sem("h_gated")
        h_turned, h_high, h_split = sem("h_turned"), sem("h_high"), sem("h_split")
        y_ps, y_free, y_out = sem("y_psum"), sem("y_read"), [sem(f"y_out{i}") for i in range(2)]
        passed = sem("x_passed")
        block = ctx.enter_context(nc.Block())

        def over_blocks(eng, block_of):
            def expert(e, split):
                b0 = eng.value_load(ends[0:1, ds(e, 1)], min_val=0, max_val=NB - 1)
                b1 = eng.value_load(ends[0:1, ds(e + 1, 1)], min_val=1, max_val=NB - 1)
                last = eng.snap(b1 - 1)
                with eng.If(b0 < last):
                    with eng.Fori(b0, last) as g:
                        block_of(g, None)
                block_of(last, eng.snap(e + 1) if split else None)

            with eng.Fori(0, E - 1) as e:
                expert(e, True)
            expert(E - 1, False)

        @block.sync
        def _(sp):
            with sp.Fori(0, E - 1) as e:
                for i in range(4):
                    sp.wait_ge(wt.split13, e * 4 + (i + 1))
                    wt.load13(sp, e + 1, i)
                sp.wait_ge(wt.split2, e * 4 + 4)
                wt.load2(sp, e + 1)
            total = sp.value_load(ends[0:1, E:E + 1], min_val=1, max_val=NB - 1)
            sp.wait_ge(zeros_set, 1)
            with sp.Fori(total, NB) as g:
                sp.dma_start(dram["y"][ds(g * P, P), :], zeros[:]).then_inc(zeros_out, 16)
            with sp.Fori(0, total) as g:
                sp.sem_inc(zeros_out, 16)
            sp.wait_ge(zeros_out, NB * 16)

        @block.gpsimd
        def _(pool):
            pool.memset(ident[:], 0.0).then_inc(idz, 1)
            pool.wait_ge(idz, 1)
            pool.affine_select(out=ident[:], in_=ident[:], compare_op=ALU.not_equal, fill=1.0, base=0,
                               pattern=[[-1, P]], channel_multiplier=1).then_inc(idn, 1)
            pool.memset(zeros[:], 0.0).then_inc(zeros_set, 1)

            def gather(g):
                pool.wait_ge(turned, g + 1)
                pool.sem_inc(passed, 1)
                pool.tensor_copy(idx[:], table[:, ds(g, 1)]).then_inc(idx_set, 1)
                pool.wait_ge(idx_set, g + 1)
                pool.sem_inc(passed, 1)
                pool.indirect_dma_start(xg[:], None, dram["xn"], bass.IndirectOffsetOnAxis(idx[:], 0)).then_inc(gathered, 16)

            def one(g, nxt):
                gather(g + 2)
                if nxt is not None:
                    wt.write_low2(pool, nxt)

            gather(0)
            gather(1)
            over_blocks(pool, one)
            total = pool.value_load(ends[0:1, E:E + 1], min_val=1, max_val=NB - 1)
            pool.wait_ge(gathered, total * 16 + 32)
            pool.sem_inc(passed, 1)

        @block.tensor
        def _(pe):
            def turn_x(g):
                pe.wait_ge(gathered, g * 16 + 16)
                for h in range(2):
                    for k in range(4):
                        last = pe.transpose(tbank[h][:, k * P:(k + 1) * P], xg[:, (4 * h + k) * P:(4 * h + k + 1) * P], ident[:])
                last.then_inc(turned, 1)

            def turn_h(g, j):
                pe.wait_ge(gated, g * 2 + (j + 3))
                for c in range(2):
                    last = pe.transpose(gbank[j][:, c * P:(c + 1) * P], hg[:, j, c * P:(c + 1) * P], ident[:])
                last.then_inc(h_turned, 1)

            pe.sem_inc(turned, 1)
            pe.sem_inc(h_ps, 1)
            pe.sem_inc(h_turned, 1)
            pe.sem_inc(y_ps, 1)
            pe.wait_ge(idn, 1)
            turn_x(0)
            with pe.Fori(0, E) as e:
                b0 = pe.value_load(ends[0:1, ds(e, 1)], min_val=0, max_val=NB - 1)
                b1 = pe.value_load(ends[0:1, ds(e + 1, 1)], min_val=1, max_val=NB - 1)
                e4 = pe.snap(e * 4)
                with pe.Fori(b0, b1) as g:
                    pe.wait_ge(x_split, g * 2 + 2)
                    for j in range(2):
                        pe.wait_ge(gated, g * 2 + (j + 1))
                        for w in range(2):
                            pe.wait_ge(wt.split13, e4 + (2 * j + w + 1))
                            for k in range(KD):
                                cols = slice(k * HC, (k + 1) * HC)
                                for n, (x, wts_part) in enumerate(((x_hi, wt.hi13), (x_hi, wt.lo13), (x_lo, wt.hi13))):
                                    last = pe.matmul(hbank[j][:, w * HC:(w + 1) * HC], x[:, k], wts_part[:, 2 * j + w, cols],
                                                     start=(k + n == 0), stop=(k == KD - 1 and n == 2))
                        last.then_inc(h_ps, 1)
                    turn_h(g, 0)
                    turn_x(g + 1)
                    turn_h(g, 1)
                    pe.wait_ge(wt.split2, e4 + 4)
                    for f in range(FE):
                        if f % 2 == 0:
                            pe.wait_ge(h_split, g * 2 + (f // 2 + 1))
                        for c in range(2):
                            if f == 0:
                                pe.wait_ge(y_free, g * 2 + (c + 1))
                            for n, (x, wts_part) in enumerate(((h_hi, wt.hi2), (h_hi, wt.lo2), (h_lo, wt.hi2))):
                                last = pe.matmul(ybank[c][:], x[:, f], wts_part[:, f, c * 512:(c + 1) * 512],
                                                 start=(f + n == 0), stop=(f == FE - 1 and n == 2))
                            if f == FE - 1:
                                last.then_inc(y_ps, 1)

        @block.scalar
        def _(act):
            act.sem_inc(y_free, 2)
            act.sem_inc(tanh_d, 1)
            act.sem_inc(h_high, 1)
            for n in range(2):
                act.sem_inc(y_out[n], 16)

            def high_x(g):
                act.wait_ge(turned, g + 2)
                for h in range(2):
                    act.activation(x_hi[:, 4 * h:4 * h + 4].rearrange("p k t -> p (k t)"), tbank[h][:], ACT.Copy).then_inc(x_high, 1)

            def tanh(g, j):
                act.wait_ge(h_ps, g * 2 + (j + 2))
                act.activation(th[:, j], hbank[j][:, 0:HC], ACT.Tanh, scale=0.5).then_inc(tanh_d, 1)

            def high_h(g, j):
                act.wait_ge(h_turned, g * 2 + (j + 2))
                act.activation(h_hi[:, 2 * j:2 * j + 2].rearrange("p f t -> p (f t)"), gbank[j][:, 0:HC], ACT.Copy).then_inc(h_high, 1)

            def one(g, nxt):
                tanh(g, 0)
                if nxt is not None:
                    for i in range(2):
                        wt.write_high13(act, nxt, i)
                tanh(g, 1)
                high_h(g, 0)
                high_x(g + 1)
                high_h(g, 1)
                if nxt is not None:
                    for i in range(2, 4):
                        wt.write_high13(act, nxt, i)
                for n in range(2):
                    act.wait_ge(y_ps, g * 2 + (n + 2))
                    act.wait_ge(y_out[n], g * 16 + 16)
                    act.activation(ysb[:, n], ybank[n][:], ACT.Copy, scale=0.5).then_inc(y_free, 1)
                    act.wait_ge(y_free, g * 2 + (n + 3))
                    act.dma_start(dram["y"][ds(g * P, P), n * 512:(n + 1) * 512], ysb[:, n]).then_inc(y_out[n], 16)
                if nxt is not None:
                    wt.write_high2(act, nxt)

            high_x(0)
            over_blocks(act, one)
            total = act.value_load(ends[0:1, E:E + 1], min_val=1, max_val=NB - 1)
            for n in range(2):
                act.wait_ge(y_out[n], total * 16 + 16)
            act.sem_inc(passed, 1)

        @block.vector
        def _(dve):
            dve.sem_inc(gated, 2)
            dve.sem_inc(gate_d, 1)

            def gate(g, j):
                dve.wait_ge(tanh_d, g * 2 + (j + 2))
                dve.scalar_tensor_tensor(gg[:, j], th[:, j], 1.0, hbank[j][:, 0:HC], ALU.add, ALU.mult).then_inc(gate_d, 1)
                dve.wait_ge(gate_d, g * 2 + (j + 2))
                dve.tensor_tensor(hg[:, j], gg[:, j], hbank[j][:, HC:2 * HC], ALU.mult).then_inc(gated, 1)

            def low_h(g, j):
                dve.wait_ge(h_high, g * 2 + (j + 2))
                hi, lo = (t[:, 2 * j:2 * j + 2].rearrange("p f t -> p (f t)") for t in (h_hi, h_lo))
                dve.tensor_tensor(lo, gbank[j][:, 0:HC], hi.bitcast(F32), ALU.subtract).then_inc(h_split, 1)

            def low_x(g):
                for h in range(2):
                    dve.wait_ge(x_high, g * 2 + (h + 1))
                    hi, lo = (t[:, 4 * h:4 * h + 4].rearrange("p k t -> p (k t)") for t in (x_hi, x_lo))
                    dve.tensor_tensor(lo, tbank[h][:], hi.bitcast(F32), ALU.subtract).then_inc(x_split, 1)

            def one(g, nxt):
                gate(g, 0)
                if nxt is not None:
                    wt.write_low13(dve, nxt, 0)
                gate(g, 1)
                low_h(g, 0)
                low_x(g + 1)
                low_h(g, 1)
                if nxt is not None:
                    for i in range(1, 4):
                        wt.write_low13(dve, nxt, i)

            low_x(0)
            over_blocks(dve, one)


def combine(nc, io, dram, pos, wts, out):
    with ExitStack() as ctx:
        def sb(name, shape, dt=F32):
            return ctx.enter_context(nc.sbuf_tensor(name, shape, dt))

        def sem(name):
            return ctx.enter_context(nc.semaphore(name))

        B, Q = 8, 4
        y = [sb(f"cy{k}", [P, B, D]) for k in range(2)]
        h = sb("ch", [P, B, D])
        o = sb("co", [P, B, D])
        sqj = sb("csq", [P, 2, D])
        fg = sb("fg", [P, D])
        ssq, msq, rst, rh, rt = (sb(f"c_st{i}", [P, B]) for i in range(5))
        idx = sb("cidx", [P, 2, TT], I32)
        y_in = [sem(f"cy_in{b}") for b in range(B)]
        h_in, o_out = ([sem(f"{n}{b}") for b in range(B // Q)] for n in ("ch_in", "co_out"))
        fg_in, acc, sq, done, step = sem("fg_in"), sem("c_sums"), sem("c_squares"), sem("c_done"), sem("c_steps")
        idx_set = sem("c_idx")
        block = ctx.enter_context(nc.Block())

        @block.sync
        def _(sp):
            sp.dma_start(fg[:], io["final_norm_g"].rearrange("(a n) -> a n", a=1).partition_broadcast(P)).then_inc(fg_in, 16)
            for i in range(TT):
                b = i % B
                if i >= B:
                    sp.wait_ge(done, i - B + 1)
                sp.dma_start(h[:, b], dram["h"][i * P:(i + 1) * P, :]).then_inc(h_in[b // Q], 16)

        @block.gpsimd
        def _(pool):
            for k in range(2):
                pool.tensor_copy(idx[:, k], pos[:, :, k]).then_inc(idx_set, 1)
            pool.wait_ge(idx_set, 2)
            for i in range(TT):
                b = i % B
                if i >= B:
                    pool.wait_ge(acc, 2 * (i - B) + 2)
                for k in range(2):
                    pool.indirect_dma_start(y[k][:, b], None, dram["y"], bass.IndirectOffsetOnAxis(idx[:, k, i:i + 1], 0)).then_inc(y_in[b], 16)

        @block.scalar
        def _(act):
            def store(i):
                act.wait_ge(done, i + 1)
                act.dma_start(out[0, i * P:(i + 1) * P, :], o[:, i % B]).then_inc(o_out[i % B // Q], 16)

            for i in range(TT):
                b = i % B
                act.wait_ge(acc, 2 * i + 2)
                if i >= 2:
                    act.wait_ge(sq, i - 1)
                act.activation(sqj[:, i % 2], h[:, b], ACT.Square, accum_out=ssq[:, b:b + 1]).then_inc(sq, 1)
                if i >= Q + 1:
                    store(i - Q - 1)
            for i in range(TT - Q - 1, TT):
                store(i)
            for b in range(B // Q):
                act.wait_ge(o_out[b], 16 * Q * TT // B)

        @block.vector
        def _(dve):
            s = Steps(dve, step)
            dve.wait_ge(fg_in, 16)

            def add(i):
                b, turn = i % B, i // B + 1
                dve.wait_ge(h_in[b // Q], 16 * Q * turn)
                dve.wait_ge(y_in[b], 32 * turn)
                for k in range(2):
                    dve.scalar_tensor_tensor(h[:, b], y[k][:, b], wts[:, i, k:k + 1], h[:, b], ALU.mult, ALU.add).then_inc(acc, 1)
                    dve.wait_ge(acc, 2 * i + k + 1)

            def norms(q):
                first = q * Q
                four = slice(first % B, first % B + Q)
                dve.wait_ge(sq, first + Q)
                s.link(dve.tensor_scalar(msq[:, four], ssq[:, four], 1.0 / D, EPS, ALU.mult, ALU.add))
                rsqrt_steps(dve, s, msq[:, four], rh[:, four], rst[:, four], rt[:, four])
                for i in range(first, first + Q):
                    b = i % B
                    if i >= B:
                        dve.wait_ge(o_out[b // Q], 16 * Q * (i // B))
                    dve.scalar_tensor_tensor(o[:, b], h[:, b], rst[:, b:b + 1], fg[:], ALU.mult, ALU.mult).then_inc(done, 1)

            for q in range(TT // Q):
                for i in range(q * Q, (q + 1) * Q):
                    add(i)
                    if i % Q == 0 and q:
                        norms(q - 1)
            norms(TT // Q - 1)


def trunk(nc, io, out):
    dram = {
        "xT": nc.dram_tensor("xn1_feature_major", [KD, P, T], F32, kind="Internal").ap(),
        "ys": nc.dram_tensor("branches", [NBR, 2, P, T], F32, kind="Internal").ap(),
        "h": nc.dram_tensor("residual", [T, D], F32, kind="Internal").ap(),
        "xn": nc.dram_tensor("xn2", [T, D], F32, kind="Internal").ap(),
        "y": nc.dram_tensor("expert_rows", [NB * P, D], F32, kind="Internal").ap(),
    }
    with ExitStack() as ctx:
        wts = ctx.enter_context(nc.sbuf_tensor("wts", [P, TT, 2], F32))
        pos = ctx.enter_context(nc.sbuf_tensor("pos", [P, TT, 2], I32))
        table = ctx.enter_context(nc.sbuf_tensor("table", [P, NB + 1], I32))
        ends = ctx.enter_context(nc.sbuf_tensor("ends", [P, E + 1], I32))
        mix_branches(nc, io, dram)
        with nc.sbuf_tensor("logits", [P, TT, R], F32) as logits:
            merge_branches(nc, io, dram, logits)
            with ExitStack() as weights_ctx:
                wt = ExpertWeights(weights_ctx, nc, io)
                route(nc, logits, table, pos, wts, ends, wt)
                run_experts(nc, dram, table, ends, wt)
        combine(nc, io, dram, pos, wts, out)


_INS = ["x", "norm1_g", "w_in", "conv_a_w", "pool_w", "pool_b", "pool_scale", "s5_lambda_re", "s5_lambda_im", "s5_log_step",
        "s5_b_re", "s5_b_im", "s5_c_re", "s5_c_im", "s5_d", "s5_glu_w", "s5_glu_b", "lru_conv_w", "lru_conv_b", "lru_wa", "lru_ba",
        "lru_wx", "lru_bx", "lru_lambda", "merge_gate_w", "merge_gate_b", "branch_w", "w_out", "norm2_g", "router_group_w",
        "router_group_b", "router_expert_w", "router_expert_b", "expert_w1", "expert_w3", "expert_w2", "final_norm_g"]


def kernel(**inputs):
    import numpy as _np
    import concourse.bacc as _bacc
    from concourse import mybir as _mybir
    from concourse.bass_utils import run_bass_kernel_spmd as _run

    nc = _bacc.Bacc("TRN2", target_bir_lowering=False, num_devices=1)
    arrays, io = {}, {}
    for name in _INS:
        a = _np.ascontiguousarray(inputs[name])
        arrays[f"in_{name}_dram"] = a
        io[name] = nc.dram_tensor(f"in_{name}_dram", a.shape, _mybir.dt.from_np(a.dtype), kind="ExternalInput").ap()
    out = nc.dram_tensor("out_dram", (1, T, D), F32, kind="ExternalOutput").ap()
    trunk(nc, io, out)
    r = _run(nc, [arrays], core_ids=[0])
    return r.results[0]["out_dram"]
```

```python
import math
from contextlib import ExitStack

import concourse.bass as bass
from concourse import mybir

F32 = mybir.dt.float32
F32R = mybir.dt.float32r
I32 = mybir.dt.int32
ALU = mybir.AluOpType
ACT = mybir.ActivationFunctionType
AX = mybir.AxisListType
ds = bass.ds

P = 128
T = 2048
D = 1024
KD = D // P
TT = T // P
W = 256
NF = 14
NBR = 4
G, EPG = 4, 8
E = G * EPG
DE = 512
FE = DE // P
R = G + E
NB = T * 2 // P + E
EPS = 1e-6
GELU_C = 0.044715
GELU_S = math.sqrt(2.0 / math.pi)
MAGIC = 12582912.0


class Ring:

    def __init__(self, full, free, banks, uses):
        self.full, self.free, self.banks, self.uses = full, free, banks, list(uses)
        assert len(self.uses) % len(banks) == 0
        self.per = len(self.uses)

    def bank(self, use):
        return self.banks[self.uses.index(use) % len(self.banks)]

    def turn(self, use):
        return self.uses.index(use) + 1


class Steps:

    def __init__(self, eng, sem, per=0):
        self.eng, self.sem, self.per, self.n, self.base = eng, sem, per, 0, 0

    def trip(self, base):
        self.base, self.n = base, 0

    def mark(self, inst):
        inst.then_inc(self.sem, 1)
        self.n += 1

    def settle(self):
        self.eng.wait_ge(self.sem, self.base + self.n)

    def link(self, inst):
        self.mark(inst)
        self.settle()


def rsqrt_steps(dve, s, mean_sq, half, y, t):
    s.link(dve.tensor_scalar(y.bitcast(I32), mean_sq.bitcast(I32), -0.5, 1597463007.0, ALU.mult, ALU.add))
    s.link(dve.tensor_scalar(half, mean_sq, -0.5, None, ALU.mult))
    for _ in range(4):
        s.link(dve.tensor_tensor(t, y, y, ALU.mult))
        s.link(dve.tensor_tensor(t, t, half, ALU.mult))
        s.link(dve.scalar_tensor_tensor(y, t, 1.5, y, ALU.add, ALU.mult))


def horner(dve, s, out, x, coefs):
    s.link(dve.tensor_scalar(out, x, coefs[-1], None, ALU.mult))
    for c in coefs[-2::-1]:
        s.link(dve.scalar_tensor_tensor(out, out, c, x, ALU.add, ALU.mult))


def exp_exact(dve, s, out, x, n, f, pw):
    s.link(dve.tensor_scalar(f, x, -87.0, 88.0, ALU.max, ALU.min))
    s.link(dve.tensor_scalar(n, f, 1.0 / math.log(2.0), MAGIC, ALU.mult, ALU.add))
    s.link(dve.tensor_scalar(n, n, -MAGIC, None, ALU.add))
    s.link(dve.scalar_tensor_tensor(f, n, -0.693359375, f, ALU.mult, ALU.add))
    s.link(dve.scalar_tensor_tensor(f, n, 2.12194440e-4, f, ALU.mult, ALU.add))
    s.link(dve.tensor_scalar(pw, n, 127.0, 8388608.0, ALU.add, ALU.mult))
    horner(dve, s, out, f, [1.0 / math.factorial(k) for k in range(1, 9)])
    s.link(dve.scalar_tensor_tensor(out, out, 1.0, pw.bitcast(F32), ALU.add, ALU.mult))


def mix_branches(nc, io, dram):
    CT = 512
    CH = T // CT
    TC = CT // P
    NS = 8
    MAXW = 16
    FIRST_F = [8, 9]
    SLOT_F = [10, 11, 12, 13, 6, 7, 2, 0, 4, 3, 1, 5]
    DVE_STEPS = 108

    with ExitStack() as ctx:
        def sb(name, shape, dt=F32):
            return ctx.enter_context(nc.sbuf_tensor(name, shape, dt))

        def sem(name):
            return ctx.enter_context(nc.semaphore(name))

        ps = [ctx.enter_context(nc.psum_tensor(f"mixps{i}", [P, CT], F32)) for i in range(8)]
        g_uses = []
        b_uses = []
        for n, f in enumerate(SLOT_F):
            (b_uses if f in (4, 5) else g_uses).append(("f", f))
            if n == 3:
                g_uses += [("r", 0), ("i", 0), ("r", 1), ("i", 1)]
            if n == 7:
                b_uses += [("pool", 0), ("pool", 1)]
        g_uses += [("t", k) for k in range(KD)] + [("glu", 0), ("glu", 1)] + [("f", f) for f in FIRST_F]
        PRE = KD + len(FIRST_F)
        gr = Ring(sem("act_tile_full"), sem("act_tile_free"), ps[0:2], g_uses)
        br = Ring(sem("dve_tile_full"), sem("dve_tile_free"), ps[2:4], b_uses)
        sre, sim_, yps = ps[4], ps[5], ps[6]

        NW = 7
        win = sb("win", [P, NW, KD, P])
        g1 = sb("g1", [P, KD])
        ident = sb("ident", [P, P])
        lamre, lamim = sb("lamre", [P, NS]), sb("lamim", [P, NS])
        ex = sb("ex", [P, NS + 2])
        lst = sb("lst", [P, 2 * NS])
        exo = sb("exo", [P, NS + 2])
        BT = [sb(f"BT{i}", [P, 2, P]) for i in range(2)]
        CTr = [sb(f"CTr{i}", [P, 2, P]) for i in range(2)]
        bd = sb("bd", [P, 3, 2, P])
        glw = sb("glw", [P, 2, W])
        cwa = sb("cwa", [P, 3, 2])
        cwl = sb("cwl", [P, 4, 2])
        vec = sb("vec", [P, 8, 2])
        LCB, PB, PSC, SD, GB, BA, BX, LAM = range(8)
        m4sp = sb("m4sp", [P, 2])
        invw, wcol = sb("invw", [P, 2]), sb("wcol", [P, 2])
        corr = sb("corr", [P, 2, MAXW])
        io16 = sb("io16", [P, MAXW], I32)
        tcos, tsin = sb("tcos", [P, NS, CT]), sb("tsin", [P, NS, CT])
        rdec = sb("rdec", [P, NS])
        pari = sb("pari", [P, NS + 2], I32)
        gpar = sb("gpar", [P, 2], I32)
        gmask = sb("gmask", [P, 2])

        xin = sb("xin", [P, TC, D])
        ssq, rst, rtmp, rhalf = sb("ssq", [P, TC]), sb("rst", [P, TC]), sb("rtmp", [P, TC]), sb("rhalf", [P, TC])
        msq = sb("msq", [P, TC])
        xT = sb("xT", [P, KD, CT])
        bgcg = sb("bgcg", [P, 4, CT])
        b_nat = [bgcg[:, i, 0:NS * 16].rearrange("p (s h) -> p s h", h=16) for i in range(2)]
        c_nat = [bgcg[:, i, 256:256 + P].rearrange("p (u h) -> p u h", u=2) for i in range(2)]
        par = bgcg[:, 2, 0:24 * NS].rearrange("p (i s) -> p i s", s=NS)
        va = sb("va", [P, 2, CT + 2])
        pu = sb("pu", [P, 2, CT + MAXW - 1])
        pw_ = [sb(f"pw{i}", [P, CT + MAXW - 1]) for i in range(2)]
        su = sb("su", [P, 2, CT])
        lx = sb("lx", [P, 2, CT + 3])
        xc = sb("xc", [P, 2, CT])
        lg = sb("lg", [P, 2, CT])
        lru = sb("lru", [P, 2, 4, CT])
        hcar = sb("hcar", [P, 2])
        m = sb("m", [P, 8, CT])
        hst = sb("hst", [P, 2, 2, CT])
        scar = sb("scar", [P, 2, NS])
        ys = sb("ys", [P, NBR, 2, CT])
        yg, yq = su, sb("yq", [P, 2, CT])
        lq = yq

        angle_in, par_in, bd_zero, bd_in = sem("angle_params_in"), sem("params_in"), sem("diag_zero"), sem("diag_in")
        win_in = [sem(f"win_in{i}") for i in range(NW)]
        F_ORDER = FIRST_F + SLOT_F
        assert NF % NW == 0
        consts, idz = sem("consts"), sem("ident_zero")
        pre, pre_full, pre_turned, pre_copied = sem("prep_steps"), sem("bc_ready"), sem("bc_turned"), sem("bc_copied")
        unit_rot, tabs = sem("unit_rotation"), sem("tables_steps")
        x_in = [sem(f"x_in{i}") for i in range(TC)]
        sq_done, xh_full, xT_out, rst_set, g1_in = sem("square_sum"), sem("xhat_full"), sem("xT_out"), sem("rms_scale"), sem("g1_in")
        dstep, astep, pstep = sem("dve_step"), sem("act_step"), sem("pool_step")
        pooled, xc_full = sem("pooled_full"), sem("xc_full")
        lru_a, lru_q, lru_m, gl_u, gl_t = sem("lru_acts"), sem("lru_q"), sem("lru_root"), sem("gate_poly"), sem("gate_tanh")
        s_full, s_free, rot_in, scan_d, rot_m, h_full = (sem("bu_full"), sem("bu_free"), sem("bu_products"), sem("scans_in"),
                                                        sem("state_products"), sem("state_full"))
        y_full, y_free, y_pre, y_sq, y_u, y_t, yg_full, glu_t = (sem("y_full"), sem("y_free"), sem("y_pre"), sem("y_sq"),
                                                               sem("y_poly"), sem("y_tanh"), sem("y_gelu"), sem("glu_tanh"))
        ys_full, ys_out = sem("ys_full"), [sem(f"ys_out{i}") for i in range(NBR)]
        passed = sem("mix_passed")
        block = ctx.enter_context(nc.Block())

        GPER, BPER = gr.per, br.per
        def held(eng, value):
            return value if isinstance(value, int) else eng.snap(value)

        GLU_EARLY = KD

        def first_turn(c, f):
            return c * GPER + (PRE - len(FIRST_F) + FIRST_F.index(f) + 1)

        halves = [slice(64 * q, 64 * q + 64) for q in range(2)]

        def vector(nm):
            v = io[nm][0]
            return (v.rearrange("a b -> (a b)") if len(v.shape) == 2 else v).rearrange("(j p) -> p j", p=P)

        angle_params = [(lst[:], io["s5_log_step"][0:1].partition_broadcast(P)), (vec[:, LAM, :], vector("lru_lambda"))]
        params = []
        for q, rows in enumerate(halves):
            angle_params += [(t[rows, :], io[nm][0].rearrange("(s q) p -> q p s", q=2)[q])
                             for t, nm in ((lamim, "s5_lambda_im"), (lamre, "s5_lambda_re"))]
            params += [(t[rows], io[nm][0].rearrange("(s q) p h -> q p s h", q=2)[q])
                       for t, nm in zip(b_nat, ("s5_b_re", "s5_b_im"))]
        for t, nm in zip(c_nat, ("s5_c_re", "s5_c_im")):
            params += [(t[:, u], io[nm][0, 8 * u:8 * u + 8].rearrange("g h p -> (g h) p")) for u in range(2)]
        params += [(vec[:, i, :], vector(nm)) for i, nm in ((LCB, "lru_conv_b"), (PB, "pool_b"), (PSC, "pool_scale"), (SD, "s5_d"),
                                                            (GB, "s5_glu_b"), (BA, "lru_ba"), (BX, "lru_bx"))]
        params += [(glw[:], io["s5_glu_w"][0].rearrange("(k p) n -> p k n", p=P)),
                   (cwa[:], io["conv_a_w"][0].rearrange("k (j p) -> p k j", p=P)),
                   (cwl[:], io["lru_conv_w"][0].rearrange("k (j p) -> p k j", p=P))]

        DVE_TABS = 4
        TAB_STEPS = 6 * (CT.bit_length() - 1)

        def rotation_tables(eng, steps, s0, s1):
            k = 1
            n = s1 - s0
            while k < CT:
                t1, t2 = (ys[:, 2 * i:2 * i + 2].rearrange("p a b t -> p (a b t)")[:, s0 * CT // 2:s0 * CT // 2 + n * k].rearrange(
                    "p (s t) -> p s t", s=n) for i in range(2))
                zc = tcos[:, s0:s1, k - 1:k].to_broadcast([P, n, k])
                zs = tsin[:, s0:s1, k - 1:k].to_broadcast([P, n, k])
                steps.mark(eng.tensor_tensor(t1, tcos[:, s0:s1, 0:k], zc, ALU.mult))
                steps.link(eng.tensor_tensor(t2, tsin[:, s0:s1, 0:k], zs, ALU.mult))
                steps.link(eng.tensor_tensor(tcos[:, s0:s1, k:2 * k], t1, t2, ALU.subtract))
                steps.mark(eng.tensor_tensor(t1, tsin[:, s0:s1, 0:k], zc, ALU.mult))
                steps.link(eng.tensor_tensor(t2, tcos[:, s0:s1, 0:k], zs, ALU.mult))
                steps.link(eng.tensor_tensor(tsin[:, s0:s1, k:2 * k], t1, t2, ALU.add))
                k *= 2

        @block.sync
        def _(sp):
            def load_win(i):
                f = F_ORDER[i]
                sp.dma_start(win[:, i % NW], io["w_in"][0, :, f * P:(f + 1) * P].rearrange("(k p) n -> p k n", p=P))\
                  .then_inc(win_in[i % NW], 16)

            def load_x(first):
                for t in range(TC):
                    sp.dma_start(xin[:, t], io["x"][0, ds(first + t * P, P), :]).then_inc(x_in[t], 16)

            def store_xT(first):
                sp.dma_start(dram["xT"][:, :, ds(first, CT)].rearrange("k p t -> p k t"), xT[:]).then_inc(xT_out, 16)

            for i in range(NBR):
                sp.sem_inc(ys_out[i], 16)
            sp.sem_inc(xT_out, 16)
            load_x(0)
            sp.dma_start(g1[:], io["norm1_g"][0].rearrange("(k p) -> p k", p=P), allow_slow_non_contiguous=True).then_inc(g1_in, 16)
            for dst, src in angle_params:
                sp.dma_start(dst, src, allow_slow_non_contiguous=True).then_inc(angle_in, 16)
            for i in range(len(FIRST_F)):
                load_win(i)
            for dst, src in params:
                sp.dma_start(dst, src, allow_slow_non_contiguous=True).then_inc(par_in, 16)
            sp.wait_ge(bd_zero, 1)
            for i, nm in enumerate(("pool_w", "lru_wa", "lru_wx")):
                for g in range(4):
                    q = 64 * (g % 2)
                    sp.dma_start(bd[q:q + 64, i, g // 2, q:q + 64], io[nm][0, g]).then_inc(bd_in, 16)

            for i in range(len(FIRST_F), NW):
                load_win(i)
            sp.wait_ge(gr.full, KD)
            load_x(CT)
            sp.wait_ge(gr.free, 2 + KD)
            store_xT(0)
            for i, f in enumerate(FIRST_F):
                sp.wait_ge(gr.full, first_turn(0, f))
                load_win(i + NW)

            def trip(c, last):
                gb, bb = held(sp, c * GPER + PRE), held(sp, c * BPER)
                c8 = held(sp, c * 8)
                ahead, nxt = held(sp, ((c + 2) % CH) * CT), held(sp, c * CT + CT)
                for i in range(len(FIRST_F), NF):
                    if last and i + NW >= NF:
                        break
                    f = F_ORDER[i]
                    if f in (4, 5):
                        sp.wait_ge(br.full, bb + br.turn(("f", f)))
                    else:
                        sp.wait_ge(gr.full, gb + gr.turn(("f", f)))
                    load_win((i + NW) % NF)
                if not last:
                    sp.wait_ge(gr.full, gb + gr.turn(("t", KD - 1)))
                    load_x(ahead)
                    sp.wait_ge(gr.free, gb + gr.turn(("t", KD - 1)) + 2)
                    store_xT(nxt)
                    for i, f in enumerate(FIRST_F):
                        sp.wait_ge(gr.full, gb + (first_turn(1, f) - PRE))
                        load_win(i + NW)
                for i, b in enumerate((1, 3, 0, 2)):
                    sp.wait_ge(ys_full, c8 + 2 * i + 2)
                    sp.sem_inc(passed, 1)
                    sp.dma_start(dram["ys"][b, :, :, ds(c * CT, CT)].rearrange("j p t -> p j t"), ys[:, b]).then_inc(ys_out[b], 16)

            with sp.Fori(0, CH - 1) as c:
                trip(c, False)
            trip(CH - 1, True)
            sp.wait_ge(xT_out, 16 * (CH + 1))
            for i in range(NBR):
                sp.wait_ge(ys_out[i], 16 * (CH + 1))
            for t in range(TC):
                sp.wait_ge(x_in[t], 16 * (CH + 1))

        @block.gpsimd
        def _(pool):
            pool.memset(bd[:], 0.0).then_inc(bd_zero, 1)
            pool.memset(ident[:], 0.0).then_inc(idz, 1)
            pool.wait_ge(idz, 1)
            pool.affine_select(out=ident[:], in_=ident[:], compare_op=ALU.not_equal, fill=1.0, base=0,
                               pattern=[[-1, P]], channel_multiplier=1).then_inc(consts, 1)
            pool.iota(gpar[:, 0:1], [[0, 1]], base=0, channel_multiplier=1).then_inc(consts, 1)
            pool.iota(io16[:], [[1, MAXW]], base=1, channel_multiplier=0).then_inc(consts, 1)
            pool.wait_ge(unit_rot, 2)
            rotation_tables(pool, Steps(pool, tabs), DVE_TABS, NS)
            with pool.Fori(0, CH) as c:
                for s in range(NS):
                    pool.wait_ge(rot_in, c * NS + s + 1)
                    pool.tensor_tensor(m[:, 0], m[:, 0], m[:, 1], ALU.add).then_inc(scan_d, 1)
                    pool.tensor_tensor(m[:, 2], m[:, 2], m[:, 3], ALU.subtract).then_inc(scan_d, 1)
                    pool.wait_ge(rot_m, c * NS + s + 1)
                    if s >= 2:
                        pool.wait_ge(y_full, c * NS + s - 1)
                    pool.tensor_tensor(hst[:, s % 2, 0], m[:, 4], m[:, 5], ALU.subtract).then_inc(pstep, 1)
                    pool.tensor_tensor(hst[:, s % 2, 1], m[:, 6], m[:, 7], ALU.add).then_inc(pstep, 1)
                    pool.wait_ge(pstep, c * 2 * NS + 2 * s + 2)
                    pool.sem_inc(passed, 1)
                    pool.tensor_copy(scar[:, 0:1, s], hst[:, s % 2, 0, CT - 1:CT]).then_inc(h_full, 1)
                    pool.tensor_copy(scar[:, 1:2, s], hst[:, s % 2, 1, CT - 1:CT]).then_inc(h_full, 1)

        @block.scalar
        def _(act):
            act.sem_inc(gr.free, 2)

            def squares(c):
                for t in range(TC):
                    act.wait_ge(x_in[t], c * 16 + 16)
                    act.activation(lru[:, t // 2, 2 * (t % 2):2 * (t % 2) + 2, :].rearrange("p a b -> p (a b)"), xin[:, t], ACT.Square,
                                   accum_out=ssq[:, t:t + 1]).then_inc(sq_done, 1)

            def scale_rows(c):
                act.wait_ge(rst_set, c + 1)
                for t in range(TC):
                    act.activation(xin[:, t], xin[:, t], ACT.Copy, scale=rst[:, t:t + 1]).then_inc(xh_full, 1)

            def copy_xT(c, base):
                act.wait_ge(xT_out, c * 16 + 16)
                for k in range(KD):
                    act.wait_ge(gr.full, base + k + 1)
                    act.activation(xT[:, k], gr.bank(("t", k))[:], ACT.Copy, scale=g1[:, k:k + 1]).then_inc(gr.free, 1)

            def evac_first(c):
                for f in FIRST_F:
                    act.wait_ge(gr.full, first_turn(c, f))
                    act.activation(DST[f], gr.bank(("f", f))[:], ACT.Copy).then_inc(gr.free, 1)

            DST = {0: bgcg[:, 0], 1: bgcg[:, 1], 2: bgcg[:, 2], 3: bgcg[:, 3],
                   6: pu[:, 0, MAXW - 1:], 7: pu[:, 1, MAXW - 1:], 8: su[:, 0], 9: su[:, 1],
                   10: lx[:, 0, 3:], 11: lx[:, 1, 3:], 12: lg[:, 0], 13: lg[:, 1]}
            squares(0)
            scale_rows(0)
            act.wait_ge(g1_in, 16)
            copy_xT(0, 0)
            evac_first(0)
            act.wait_ge(pre_turned, 1)
            for i in range(2):
                for u in range(2):
                    act.activation(BT[i][:, u], ps[4 + i][:, u * P:(u + 1) * P], ACT.Copy).then_inc(pre_copied, 1)
                    act.activation(CTr[i][:, u], ps[6 + i][:, u * P:(u + 1) * P], ACT.Copy,
                                   scale=(1.0 if i == 0 else -1.0)).then_inc(pre_copied, 1)

            def trip(c, last):
                gb, c8 = held(act, c * GPER + PRE), held(act, c * 8)

                def evac(dst, f):
                    act.wait_ge(gr.full, gb + gr.turn(("f", f)))
                    act.activation(dst, gr.bank(("f", f))[:], ACT.Copy).then_inc(gr.free, 1)

                for n, f in enumerate(SLOT_F):
                    if f in (4, 5):
                        continue
                    if f in (12, 13):
                        act.wait_ge(gr.full, gb + gr.turn(("f", f)))
                        act.activation(lq[:, f - 12], gr.bank(("f", f))[:], ACT.Square).then_inc(lru_a, 1)
                    evac(DST[f], f)
                    if n == 3:
                        for j in range(2):
                            for i, nm in enumerate(("r", "i")):
                                act.wait_ge(gr.full, gb + gr.turn((nm, j)))
                                act.activation(lru[:, j, i], gr.bank((nm, j))[:], ACT.Tanh, scale=0.5,
                                               bias=vec[:, BA + i, j:j + 1]).then_inc(gr.free, 1)
                            act.wait_ge(gr.free, gb + gr.turn(("i", j)) + 2)
                            act.activation(lru[:, j, 2], lru[:, j, 0], ACT.Exp, scale=m4sp[:, j:j + 1],
                                           bias=m4sp[:, j:j + 1]).then_inc(astep, 1)
                            act.wait_ge(astep, c * 2 + j + 1)
                            act.activation(lru[:, j, 0], lru[:, j, 0], ACT.Tanh, scale=m4sp[:, j:j + 1],
                                           bias=m4sp[:, j:j + 1]).then_inc(lru_a, 1)
                            act.activation(lru[:, j, 3], lru[:, j, 2], ACT.Square).then_inc(lru_a, 1)
                    if n == 5:
                        for j in range(2):
                            act.wait_ge(gl_u, c * 2 + j + 1)
                            act.activation(lq[:, j], lq[:, j], ACT.Tanh, scale=GELU_S).then_inc(gl_t, 1)
                    if n == 7:
                        for j in range(2):
                            act.wait_ge(lru_q, c * 2 + j + 1)
                            act.activation(lru[:, j, 3], lru[:, j, 3], ACT.Sqrt, scale=-0.25).then_inc(lru_m, 1)
                    if n == 9:
                        act.wait_ge(ys_full, c8 + 4)
                        if not last:
                            squares(c + 1)
                if not last:
                    scale_rows(c + 1)
                for j in range(2):
                    act.wait_ge(y_pre, c * 2 + j + 1)
                    act.activation(yq[:, j], yg[:, j], ACT.Square).then_inc(y_sq, 1)
                for j in range(2):
                    act.wait_ge(y_u, c * 2 + j + 1)
                    act.activation(yq[:, j], yq[:, j], ACT.Tanh, scale=GELU_S).then_inc(y_t, 1)
                if not last:
                    copy_xT(c + 1, gb + (gr.turn(("t", 0)) - 1))
                early = GLU_EARLY if last else 0
                for j in range(2):
                    act.wait_ge(gr.full, gb + gr.turn(("glu", j)) - early)
                    act.activation(yq[:, j], gr.bank(("glu", j))[:], ACT.Tanh, scale=0.25,
                                   bias=vec[:, GB, j:j + 1]).then_inc(gr.free, 1)
                if not last:
                    act.wait_ge(ys_full, c * 8 + 8)
                    evac_first(c + 1)

            with act.Fori(0, CH - 1) as c:
                trip(c, False)
            trip(CH - 1, True)

        @block.tensor
        def _(pe):
            def project(c, f, turn, ring):
                i = F_ORDER.index(f)
                pe.wait_ge(win_in[i % NW], 16 * (NF // NW) * c + 16 * (i // NW + 1))
                pe.wait_ge(ring.free, turn + 1)
                for k in range(KD):
                    last = pe.matmul(ring.bank(("f", f))[:], win[:, i % NW, k], xT[:, k, :],
                                     start=(k == 0), stop=(k == KD - 1))
                last.then_inc(ring.full, 1)

            def turn_x(c, base):
                pe.wait_ge(xh_full, c * TC + TC)
                for k in range(KD):
                    pe.wait_ge(gr.free, base + k + 1)
                    for t in range(TC):
                        last = pe.transpose(gr.bank(("t", k))[:, t * P:(t + 1) * P], xin[:, t, k * P:(k + 1) * P], ident[:])
                    last.then_inc(gr.full, 1)

            def project_first(c, xT_copied):
                pe.wait_ge(gr.free, xT_copied + 2)
                for f in FIRST_F:
                    project(c, f, first_turn(c, f) - 1, gr)

            pe.wait_ge(consts, 3)
            turn_x(0, 0)
            project_first(0, KD)
            pe.wait_ge(pre_full, 1)
            for i in range(2):
                for u in range(2):
                    pe.transpose(ps[4 + i][:, u * P:(u + 1) * P], m[:, i, u * P:(u + 1) * P], ident[:])
                    last = pe.transpose(ps[6 + i][:, u * P:(u + 1) * P], m[:, 2 + i, u * P:(u + 1) * P], ident[:])
            last.then_inc(pre_turned, 1)
            pe.wait_ge(pre_copied, 8)
            pe.wait_ge(par_in, 16 * len(params))
            pe.wait_ge(bd_in, 16 * 12)

            def trip(c, last_trip):
                gb, bb, sb_ = held(pe, c * GPER + PRE), held(pe, c * BPER), held(pe, c * NS)
                pe.wait_ge(gr.free, first_turn(c, 9) + 2)
                for n, f in enumerate(SLOT_F):
                    if n < NS:
                        s, u, q = n, n // 4, 32 * (n % 4)
                        pe.wait_ge(s_free, sb_ + s + 1)
                        pe.matmul(sre[:], BT[0][q:q + 32, u, :], su[q:q + 32, u, :], start=True, stop=True)
                        pe.matmul(sim_[:], BT[1][q:q + 32, u, :], su[q:q + 32, u, :], start=True, stop=True).then_inc(s_full, 1)
                    ring, base = (br, bb) if f in (4, 5) else (gr, gb)
                    project(c, f, base + ring.turn(("f", f)) - 1, ring)
                    if n == NF - len(FIRST_F) - 1 and not last_trip:
                        turn_x(c + 1, gb + (gr.turn(("t", 0)) - 1))
                    if n == 3:
                        for j in range(2):
                            pe.wait_ge(xc_full, c * 2 + j + 1)
                            for i, nm in enumerate(("r", "i")):
                                pe.wait_ge(gr.free, gb + gr.turn((nm, j)))
                                pe.matmul(gr.bank((nm, j))[:], bd[:, 1 + i, j], xc[:, j], start=True, stop=True).then_inc(gr.full, 1)
                    if n == 7:
                        for j in range(2):
                            pe.wait_ge(pooled, c * 2 + j + 1)
                            pe.wait_ge(br.free, bb + br.turn(("pool", j)))
                            pe.matmul(br.bank(("pool", j))[:], bd[:, 0, j], ys[:, 1, j], start=True, stop=True).then_inc(br.full, 1)
                    if 2 <= n < NS + 2:
                        s = n - 2
                        u, q = s // 4, 32 * (s % 4)
                        if s % 4 == 0:
                            pe.wait_ge(y_free, c * 2 + u + 1)
                        pe.wait_ge(h_full, 2 * sb_ + 2 * s + 2)
                        pe.matmul(yps[q:q + 32, :], CTr[0][:, u, q:q + 32], hst[:, s % 2, 0], start=True, stop=False)
                        last = pe.matmul(yps[q:q + 32, :], CTr[1][:, u, q:q + 32], hst[:, s % 2, 1], start=False, stop=True)
                        last.then_inc(y_full, 1)
                pe.wait_ge(yg_full, c * 2 + 2)
                early = GLU_EARLY if last_trip else 0
                for j in range(2):
                    pe.wait_ge(gr.free, gb + gr.turn(("glu", j)) - early)
                    for k in range(2):
                        last = pe.matmul(gr.bank(("glu", j))[:], glw[:, k, j * P:(j + 1) * P], yg[:, k],
                                         start=(k == 0), stop=(k == 1))
                    last.then_inc(gr.full, 1)
                if not last_trip:
                    project_first(c + 1, gb + gr.turn(("t", KD - 1)))

            with pe.Fori(0, CH - 1) as c:
                trip(c, False)
            trip(CH - 1, True)

        @block.vector
        def _(dve):
            s = Steps(dve, pre)
            for b in range(2):
                dve.sem_inc(br.free, 1)
            dve.sem_inc(s_free, 1)
            dve.sem_inc(y_free, 1)

            def rms_scale(steps, c):
                dve.wait_ge(sq_done, c * TC + TC)
                steps.link(dve.tensor_scalar(msq[:], ssq[:], 1.0 / D, EPS, ALU.mult, ALU.add))
                rsqrt_steps(dve, steps, msq[:], rhalf[:], rst[:], rtmp[:])
                dve.sem_inc(rst_set, 1)

            for z in (va[:, :, 0:2], pu[:, :, 0:MAXW - 1], lx[:, :, 0:3], hcar[:], scar[:], m[:, 0:4, :]):
                s.mark(dve.memset(z, 0.0))
            for j in range(2):
                for q in range(2):
                    w = float(2 ** (2 * j + q + 1))
                    s.mark(dve.memset(wcol[64 * q:64 * q + 64, j:j + 1], w))
                    s.mark(dve.memset(invw[64 * q:64 * q + 64, j:j + 1], 1.0 / w))
            s.settle()
            rms_scale(s, 0)
            dve.wait_ge(consts, 3)
            dve.wait_ge(angle_in, 16 * len(angle_params))
            pt = lambda i: par[:, i, :]
            for q in range(2):
                s.mark(dve.tensor_copy(ex[64 * q:64 * q + 64, 0:NS],
                                       lst[64 * q:64 * q + 64, :].rearrange("p (s q) -> p q s", q=2)[:, q]))
            neg, mabs = par[:, 19, 0:2], ex[:, NS:NS + 2]
            s.link(dve.tensor_scalar(neg, vec[:, LAM, :], -1.0, None, ALU.mult))
            s.link(dve.tensor_tensor(mabs, neg, vec[:, LAM, :], ALU.min))
            nn, ff = par[:, 1:3, :].rearrange("p a b -> p (a b)")[:, 0:NS + 2], par[:, 3:5, :].rearrange("p a b -> p (a b)")[:, 0:NS + 2]
            exp_exact(dve, s, exo[:], ex[:], nn, ff, pari[:])
            LR, X, TH, Q, V, V2, SN, CS, ER, CM1, ST, CO, AR, AI, DEN, CRE, CIM, T1, T2 = range(0, 19)
            step = exo[:, 0:NS]
            s.link(dve.tensor_scalar(pt(LR), lamre[:], -1e-4, None, ALU.min))
            s.link(dve.tensor_tensor(pt(X), pt(LR), step, ALU.mult))
            s.link(dve.tensor_tensor(pt(TH), lamim[:], step, ALU.mult))
            s.link(dve.tensor_scalar(pt(Q), pt(TH), 1.0 / (2 * math.pi), MAGIC, ALU.mult, ALU.add))
            s.link(dve.tensor_scalar(pt(Q), pt(Q), -MAGIC, None, ALU.add))
            s.link(dve.tensor_scalar(pt(V), pt(TH), 0.5, None, ALU.mult))
            pi1 = 3.140625
            pi2 = 9.670257568359375e-4
            pi3 = math.pi - pi1 - pi2
            for pc in (pi1, pi2, pi3):
                s.link(dve.scalar_tensor_tensor(pt(V), pt(Q), -pc, pt(V), ALU.mult, ALU.add))
            s.link(dve.tensor_tensor(pt(V2), pt(V), pt(V), ALU.mult))
            horner(dve, s, pt(SN), pt(V2), [(-1.0) ** k / math.factorial(2 * k + 1) for k in range(1, 8)])
            s.link(dve.scalar_tensor_tensor(pt(SN), pt(SN), 1.0, pt(V), ALU.add, ALU.mult))
            horner(dve, s, pt(CS), pt(V2), [(-1.0) ** k / math.factorial(2 * k) for k in range(1, 9)])
            s.link(dve.tensor_scalar(pt(CS), pt(CS), 1.0, None, ALU.add))
            s.link(dve.tensor_tensor(pt(CM1), pt(SN), pt(SN), ALU.mult))
            s.link(dve.tensor_scalar(pt(CM1), pt(CM1), -2.0, None, ALU.mult))
            s.link(dve.tensor_tensor(pt(ST), pt(SN), pt(CS), ALU.mult))
            s.link(dve.tensor_scalar(pt(ST), pt(ST), 2.0, None, ALU.mult))
            s.link(dve.tensor_scalar(pt(CO), pt(CM1), 1.0, None, ALU.add))
            dve.tensor_copy(tcos[:, :, 0:1], pt(CO).unsqueeze(2)).then_inc(unit_rot, 1)
            dve.tensor_copy(tsin[:, :, 0:1], pt(ST).unsqueeze(2)).then_inc(unit_rot, 1)
            e_, z, z2, po = exo[:, NS:NS + 2], par[:, 20, 0:2], par[:, 21, 0:2], par[:, 22, 0:2]
            s.link(dve.tensor_scalar(z, e_, 2.0, None, ALU.add))
            s.link(dve.reciprocal(z, z))
            s.link(dve.tensor_tensor(z, z, e_, ALU.mult))
            s.link(dve.tensor_tensor(z2, z, z, ALU.mult))
            horner(dve, s, po, z2, [1.0 / k for k in range(3, 17, 2)])
            s.link(dve.scalar_tensor_tensor(po, po, 1.0, z, ALU.add, ALU.mult))
            s.link(dve.tensor_scalar(neg, neg, 0.0, None, ALU.max))
            s.link(dve.scalar_tensor_tensor(po, po, 2.0, neg, ALU.mult, ALU.add))
            s.link(dve.tensor_scalar(m4sp[:], po, -4.0, None, ALU.mult))
            s.link(dve.tensor_scalar(pt(T1), pt(X), -88.0, 1.0 / 128, ALU.max, ALU.mult))
            horner(dve, s, pt(ER), pt(T1), [1.0 / math.factorial(k) for k in range(1, 11)])
            for _ in range(7):
                s.link(dve.scalar_tensor_tensor(pt(ER), pt(ER), 2.0, pt(ER), ALU.add, ALU.mult))
            s.link(dve.tensor_scalar(rdec[:], pt(ER), 1.0, None, ALU.add))
            s.link(dve.tensor_tensor(pt(AR), pt(ER), pt(CO), ALU.mult))
            s.link(dve.tensor_tensor(pt(AR), pt(AR), pt(CM1), ALU.add))
            s.link(dve.tensor_tensor(pt(AI), rdec[:], pt(ST), ALU.mult))
            s.link(dve.tensor_tensor(pt(T1), pt(LR), pt(LR), ALU.mult))
            s.link(dve.tensor_tensor(pt(DEN), lamim[:], lamim[:], ALU.mult))
            s.link(dve.tensor_tensor(pt(DEN), pt(DEN), pt(T1), ALU.add))
            s.link(dve.reciprocal(pt(DEN), pt(DEN)))
            s.link(dve.tensor_tensor(pt(T1), pt(AR), pt(LR), ALU.mult))
            s.link(dve.tensor_tensor(pt(T2), pt(AI), lamim[:], ALU.mult))
            s.link(dve.tensor_tensor(pt(CRE), pt(T1), pt(T2), ALU.add))
            s.link(dve.tensor_tensor(pt(CRE), pt(CRE), pt(DEN), ALU.mult))
            s.link(dve.tensor_tensor(pt(T1), pt(AI), pt(LR), ALU.mult))
            s.link(dve.tensor_tensor(pt(T2), pt(AR), lamim[:], ALU.mult))
            s.link(dve.tensor_tensor(pt(CIM), pt(T1), pt(T2), ALU.subtract))
            s.link(dve.tensor_tensor(pt(CIM), pt(CIM), pt(DEN), ALU.mult))
            dve.wait_ge(par_in, 16 * len(params))
            for i in (BA, BX, GB):
                s.mark(dve.tensor_scalar(vec[:, i, :], vec[:, i, :], 0.5, None, ALU.mult))
            for j in range(2):
                cj = corr[:, j, :]
                s.link(dve.tensor_copy(cj, io16[:]))
                s.link(dve.tensor_scalar(cj, cj, wcol[:, j:j + 1], None, ALU.min))
                s.link(dve.reciprocal(cj, cj))
                s.link(dve.tensor_scalar(cj, cj, wcol[:, j:j + 1], None, ALU.mult))
            s.link(dve.tensor_scalar(gpar[:, 1:2], gpar[:, 0:1], 4, 1, ALU.logical_shift_right, ALU.bitwise_and))
            s.link(dve.tensor_copy(gmask[:, 1:2], gpar[:, 1:2]))
            s.link(dve.tensor_scalar(gmask[:, 0:1], gmask[:, 1:2], -1.0, 1.0, ALU.mult, ALU.add))
            cre = pt(CRE).unsqueeze(2).to_broadcast([P, NS, 16])
            cim = pt(CIM).unsqueeze(2).to_broadcast([P, NS, 16])
            tb = [m[:, 4 + i, 0:NS * 16].rearrange("p (s h) -> p s h", h=16) for i in range(4)]
            s.mark(dve.tensor_tensor(tb[0], b_nat[0], cre, ALU.mult))
            s.mark(dve.tensor_tensor(tb[1], b_nat[1], cim, ALU.mult))
            s.mark(dve.tensor_tensor(tb[2], b_nat[1], cre, ALU.mult))
            s.link(dve.tensor_tensor(tb[3], b_nat[0], cim, ALU.mult))
            for q in range(2):
                rows = slice(64 * q, 64 * q + 64)
                for i, op in enumerate((ALU.subtract, ALU.add)):
                    dst = m[rows, i, 0:2 * P].rearrange("p (s h) -> p s h", h=32)[:, :, 16 * q:16 * q + 16]
                    s.link(dve.tensor_tensor(dst, tb[2 * i][rows], tb[2 * i + 1][rows], op))
            for i in range(2):
                for q in range(2):
                    dst = m[:, 2 + i, 0:2 * P].rearrange("p (u w) -> p u w", w=P)[:, :, 64 * q:64 * q + 64]
                    s.link(dve.tensor_scalar(dst, c_nat[i], gmask[:, q:q + 1], None, ALU.mult))
            dve.sem_inc(pre_full, 1)
            rotation_tables(dve, s, 0, DVE_TABS)
            dve.wait_ge(pre_turned, 1)
            dve.sem_inc(passed, 1)

            s = Steps(dve, dstep, DVE_STEPS)

            def trip(c, last):
                s.trip(held(dve, c * DVE_STEPS))
                gb, bb, cs, c2 = held(dve, c * GPER + PRE), held(dve, c * BPER), held(dve, c * NS), held(dve, c * 2)

                def stood(f):
                    dve.wait_ge(gr.free, (first_turn(c, f) if f in FIRST_F else gb + gr.turn(("f", f))) + 2)

                def lru_conv():
                    for j in range(2):
                        stood(10 + j)
                        s.link(dve.tensor_scalar(xc[:, j], lx[:, j, 3:3 + CT], cwl[:, 3, j:j + 1], vec[:, LCB, j:j + 1], ALU.mult, ALU.add))
                        for k in (2, 1, 0):
                            i = dve.scalar_tensor_tensor(xc[:, j], lx[:, j, k:k + CT], cwl[:, k, j:j + 1], xc[:, j], ALU.mult, ALU.add)
                            if k:
                                s.link(i)
                        i.then_inc(xc_full, 1)
                    dve.wait_ge(xc_full, c2 + 2)
                    s.mark(dve.tensor_copy(lx[:, :, 0:3], lx[:, :, CT:CT + 3]))

                def s5_in(n):
                    dve.wait_ge(s_full, cs + n + 1)
                    dve.tensor_tensor(m[:, 0], sre[:], tcos[:, n], ALU.mult)
                    s.mark(dve.tensor_tensor(m[:, 1], sim_[:], tsin[:, n], ALU.mult))
                    dve.tensor_tensor(m[:, 2], sim_[:], tcos[:, n], ALU.mult)
                    s.link(dve.tensor_tensor(m[:, 3], sre[:], tsin[:, n], ALU.mult))
                    dve.sem_inc(s_free, 1)
                    dve.sem_inc(rot_in, 1)

                def s5_scan(n):
                    dve.wait_ge(scan_d, 2 * cs + 2 * n + 2)
                    r = rdec[:, n:n + 1].to_broadcast([P, CT])
                    s.mark(dve.tensor_tensor_scan(m[:, 1], r, m[:, 0], scar[:, 0, n:n + 1], ALU.mult, ALU.add))
                    s.link(dve.tensor_tensor_scan(m[:, 3], r, m[:, 2], scar[:, 1, n:n + 1], ALU.mult, ALU.add))
                    dve.wait_ge(h_full, 2 * cs + 2 * n) if n else None
                    dve.tensor_tensor(m[:, 4], m[:, 1], tcos[:, n], ALU.mult)
                    s.mark(dve.tensor_tensor(m[:, 5], m[:, 3], tsin[:, n], ALU.mult))
                    dve.tensor_tensor(m[:, 6], m[:, 3], tcos[:, n], ALU.mult)
                    s.link(dve.tensor_tensor(m[:, 7], m[:, 1], tsin[:, n], ALU.mult))
                    dve.sem_inc(rot_m, 1)

                def lru_gate_poly():
                    for j in range(2):
                        stood(12 + j)
                        s.link(dve.tensor_scalar(lq[:, j], lq[:, j], GELU_C, 1.0, ALU.mult, ALU.add))
                        dve.tensor_tensor(lq[:, j], lq[:, j], lg[:, j], ALU.mult).then_inc(gl_u, 1)

                def lru_q_():
                    for j in range(2):
                        dve.wait_ge(lru_a, c * 6 + 2 + 2 * j + 2)
                        dve.scalar_tensor_tensor(lru[:, j, 3], lru[:, j, 3], 1.0, lru[:, j, 0], ALU.add, ALU.mult).then_inc(lru_q, 1)

                def lru_out():
                    dve.wait_ge(ys_out[3], 16 * c + 16)
                    for j in range(2):
                        dve.wait_ge(lru_m, c2 + j + 1)
                        s.link(dve.scalar_tensor_tensor(lru[:, j, 1], lru[:, j, 1], 1.0, xc[:, j], ALU.add, ALU.mult))
                        s.link(dve.tensor_tensor(lru[:, j, 1], lru[:, j, 1], lru[:, j, 3], ALU.mult))
                        s.link(dve.tensor_tensor_scan(lru[:, j, 0], lru[:, j, 2], lru[:, j, 1], hcar[:, j:j + 1], ALU.mult, ALU.add))
                        s.mark(dve.tensor_copy(hcar[:, j:j + 1], lru[:, j, 0, CT - 1:CT]))
                        dve.wait_ge(gl_t, c2 + j + 1)
                        s.link(dve.scalar_tensor_tensor(lg[:, j], lq[:, j], 1.0, lg[:, j], ALU.add, ALU.mult))
                        dve.scalar_tensor_tensor(ys[:, 3, j], lru[:, j, 0], 0.5, lg[:, j], ALU.mult, ALU.mult).then_inc(ys_full, 1)

                def pool_mix():
                    dve.wait_ge(ys_out[1], 16 * c + 16)
                    H = MAXW - 1
                    N = CT + H
                    for j in range(2):
                        stood(6 + j)
                        u = pu[:, j]
                        a, b = pw_[0], pw_[1]
                        if j == 0:
                            s.mark(dve.tensor_tensor(b[0:64, H:N], u[0:64, H:N], u[0:64, H - 1:N - 1], ALU.add))
                            s.link(dve.tensor_tensor(a[64:P, 1:N], u[64:P, 1:N], u[64:P, 0:N - 1], ALU.add))
                            s.link(dve.tensor_tensor(b[64:P, H:N], a[64:P, H:N], a[64:P, H - 2:N - 2], ALU.add))
                        else:
                            s.link(dve.tensor_tensor(a[:, 1:N], u[:, 1:N], u[:, 0:N - 1], ALU.add))
                            s.link(dve.tensor_tensor(b[:, 3:N], a[:, 3:N], a[:, 1:N - 2], ALU.add))
                            s.link(dve.tensor_tensor(a[:, 7:N], b[:, 7:N], b[:, 3:N - 4], ALU.add))
                            s.mark(dve.tensor_copy(b[0:64, H:N], a[0:64, H:N]))
                            s.link(dve.tensor_tensor(b[64:P, H:N], a[64:P, H:N], a[64:P, H - 8:N - 8], ALU.add))
                        s.link(dve.tensor_tensor(b[:, H:H + MAXW], b[:, H:H + MAXW], corr[:, j], ALU.mult))
                        dve.scalar_tensor_tensor(ys[:, 1, j], b[:, H:N], invw[:, j:j + 1], u[:, H:N], ALU.mult, ALU.subtract).then_inc(pooled, 1)
                        dve.wait_ge(pooled, c2 + j + 1)
                    s.mark(dve.tensor_copy(pu[:, :, 0:H], pu[:, :, CT:N]))
                    s.mark(dve.memset(corr[:], 1.0))

                def pool_out():
                    for j in range(2):
                        dve.wait_ge(br.full, bb + br.turn(("pool", j)))
                        s.link(dve.tensor_scalar(ys[:, 1, j], br.bank(("pool", j))[:], vec[:, PB, j:j + 1], vec[:, PSC, j:j + 1], ALU.add, ALU.mult))
                        dve.sem_inc(br.free, 1)
                        dve.sem_inc(ys_full, 1)

                def conv_a(j):
                    stood(2 + j)
                    dve.wait_ge(br.full, bb + br.turn(("f", 4 + j)))
                    dve.tensor_tensor(va[:, j, 2:2 + CT], br.bank(("f", 4 + j))[:], bgcg[:, 2 + j], ALU.mult).then_inc(br.free, 1)
                    dve.wait_ge(br.free, bb + br.turn(("f", 4 + j)) + 2)
                    y = pw_[j][:, 0:CT]
                    s.link(dve.tensor_scalar(y, va[:, j, 2:2 + CT], cwa[:, 2, j:j + 1], None, ALU.mult))
                    for k in (1, 0):
                        s.link(dve.scalar_tensor_tensor(y, va[:, j, k:k + CT], cwa[:, k, j:j + 1], y, ALU.mult, ALU.add))
                    stood(j)
                    if j == 0:
                        dve.wait_ge(ys_out[0], 16 * c + 16)
                    dve.tensor_tensor(ys[:, 0, j], y, bgcg[:, j], ALU.mult).then_inc(ys_full, 1)
                    s.mark(dve.tensor_copy(va[:, j, 0:2], va[:, j, CT:CT + 2]))

                def y_in(u):
                    dve.wait_ge(y_full, cs + 4 * u + 4)
                    dve.scalar_tensor_tensor(yg[:, u], su[:, u], vec[:, SD, u:u + 1], yps[:], ALU.mult, ALU.add).then_inc(y_free, 1)
                    dve.wait_ge(y_free, c2 + u + 2)
                    dve.sem_inc(y_pre, 1)

                for n in range(NS + 3):
                    if n >= 1 and n <= NS:
                        s5_scan(n - 1)
                    if n == 0:
                        dve.wait_ge(tabs, TAB_STEPS)
                    if n < NS:
                        s5_in(n)
                    if n == 2:
                        lru_conv()
                    if n == 3:
                        lru_gate_poly()
                    if n == 4:
                        lru_q_()
                    if n == 6:
                        pool_mix()
                        y_in(0)
                    if n == 7:
                        pool_out()
                    if n == 8:
                        lru_out()
                    if n == 9:
                        y_in(1)
                        conv_a(0)
                    if n == 10 and not last:
                        rms_scale(s, c + 1)
                for j in range(2):
                    dve.wait_ge(y_sq, c2 + j + 1)
                    s.link(dve.tensor_scalar(yq[:, j], yq[:, j], GELU_C, 1.0, ALU.mult, ALU.add))
                    dve.tensor_tensor(yq[:, j], yq[:, j], yg[:, j], ALU.mult).then_inc(y_u, 1)
                for j in range(2):
                    dve.wait_ge(y_t, c2 + j + 1)
                    dve.scalar_tensor_tensor(yg[:, j], yq[:, j], 1.0, yg[:, j], ALU.add, ALU.mult).then_inc(yg_full, 1)
                conv_a(1)
                dve.wait_ge(ys_out[2], 16 * c + 16)
                for j in range(2):
                    dve.wait_ge(gr.free, gb + gr.turn(("glu", j)) + 2 - (GLU_EARLY if last else 0))
                    dve.wait_ge(yg_full, c2 + 2)
                    s.link(dve.scalar_tensor_tensor(yq[:, j], yq[:, j], 1.0, yg[:, j], ALU.add, ALU.mult))
                    dve.tensor_scalar(ys[:, 2, j], yq[:, j], 0.25, None, ALU.mult).then_inc(ys_full, 1)
                assert last or s.n == DVE_STEPS, s.n

            with dve.Fori(0, CH - 1) as c:
                trip(c, False)
            trip(CH - 1, True)


def merge_branches(nc, io, dram, logits):
    TM = 512
    TRIPS = T // TM
    MT = TM // P
    RSQ = 14
    NORM_STEPS = 1 + RSQ
    STEP_DVE = NBR - 1
    TRIP_DVE = KD * STEP_DVE + MT * NORM_STEPS
    WK = KD + 2
    PIECE = 4
    PIECES = (KD + 2 * NBR) // PIECE
    SU = NBR
    assert PIECES == MT == 4
    with ExitStack() as ctx:
        def sb(name, shape, dt=F32):
            return ctx.enter_context(nc.sbuf_tensor(name, shape, dt))

        def sem(name):
            return ctx.enter_context(nc.semaphore(name))

        ps = [ctx.enter_context(nc.psum_tensor(f"mrgps{i}", [P, 512], F32)) for i in range(5)]
        act_hi, act_lo = sb("act_hi", [P, KD + 2 * NBR, TM], F32R), sb("act_lo", [P, KD + 2 * NBR, TM], F32R)
        act_raw = sb("act_raw", [P, 2, PIECE * TM])
        merged = sb("merged", [P, KD, TM])
        wout = sb("wout", [P, KD, D])
        w_raw = sb("w_raw", [P, NBR, WK, P])
        w_hi, w_lo = sb("w_hi", [P, 2, WK, P], F32R), sb("w_lo", [P, 2, WK, P], F32R)
        gt, tmp = sb("gt", [P, TM]), sb("tmp", [P, TM])
        xr, xn = sb("xr", [P, 2, D]), sb("xn", [P, 2, D])
        xnT = sb("xnT", [P, KD, P])
        sqj = sb("sqj", [P, D])
        g2 = sb("g2", [P, D])
        rw = sb("rw", [P, KD, R])
        rb = sb("rb", [P, R])
        mb = sb("mb", [P, NBR, KD])
        ident = sb("m_ident", [P, P])
        ssq, msq, rst, rh, rt = (sb(f"m_st{i}", [P, 2]) for i in range(5))

        GPER = BPER = KD * SU + 2 * MT
        g_full, g_free, b_full, b_free = sem("gate_full"), sem("gate_free"), sem("prod_full"), sem("prod_free")
        gbank, bbank, rps = ps[0:2], ps[2:4], ps[4]
        r_full, r_free = sem("router_full"), sem("router_free")
        par_in, idz, idn = sem("m_params_in"), sem("m_ident_zero"), sem("m_ident")
        w_in, w_hi_set, w_split = [sem(f"mw_in{k}") for k in range(NBR)], sem("w_hi_set"), sem("w_split")
        act_in, act_hi_set, act_split = [sem(f"acts_in{i}") for i in range(2)], sem("act_hi_set"), sem("act_split")
        wout_in = sem("wout_in")
        x_in, h_out, n_out = ([sem(f"{n}{i}") for i in range(2)] for n in ("xr_in", "h_out", "n_out"))
        h_done, sq_done, n_full = sem("h_done"), sem("h_squared"), sem("xn_full")
        half_b, dstep, passed = sem("half_bias"), sem("m_dve_step"), sem("m_passed")
        block = ctx.enter_context(nc.Block())

        params = ((mb[:], io["merge_gate_b"][0].rearrange("(k d p) -> p k d", k=NBR, p=P)),
                  (g2[:], io["norm2_g"][0:1].partition_broadcast(P)),
                  (rw[:, :, 0:G], io["router_group_w"][0].rearrange("(k p) n -> p k n", p=P)),
                  (rw[:, :, G:R], io["router_expert_w"][0].rearrange("(k p) n -> p k n", p=P)),
                  (rb[:, 0:G], io["router_group_b"][0:1].partition_broadcast(P)),
                  (rb[:, G:R], io["router_expert_b"][0:1].partition_broadcast(P)))

        @block.sync
        def _(sp):
            def load_piece(m, c):
                cols = ds(m * TM, TM)
                if c < PIECES // 2:
                    src = dram["xT"][PIECE * c:PIECE * (c + 1), :, cols].rearrange("k p t -> p k t")
                else:
                    b = 2 * (c - PIECES // 2)
                    src = dram["ys"][b:b + 2, :, :, cols].rearrange("b j p t -> p (b j) t")
                sp.dma_start(act_raw[:, c % 2].rearrange("p (k t) -> p k t", t=TM), src).then_inc(act_in[c % 2], 16)

            def load_weights(k, d):
                sp.dma_start(w_raw[:, k, 0:KD], io["merge_gate_w"][0, :, ds(k * D + d * P, P)].rearrange("(k p) n -> p k n", p=P))\
                  .then_inc(w_in[k], 16)
                sp.dma_start(w_raw[:, k, KD:WK], io["branch_w"][0, k, :, ds(d * P, P)].rearrange("(k p) n -> p k n", p=P))\
                  .then_inc(w_in[k], 16)

            load_piece(0, 0)
            load_weights(0, 0)
            load_piece(0, 1)
            for k in range(1, NBR):
                load_weights(k, 0)
            for c in range(2, PIECES):
                sp.wait_ge(act_split, c - 1)
                load_piece(0, c)
            for dst, src in params:
                sp.dma_start(dst, src, allow_slow_non_contiguous=True).then_inc(par_in, 16)
            sp.dma_start(wout[:], io["w_out"][0].rearrange("(k p) n -> p k n", p=P)).then_inc(wout_in, 16)
            for i in range(2):
                sp.sem_inc(h_out[i], 16)
                sp.sem_inc(n_out[i], 16)
            with sp.Fori(0, TRIPS) as m:
                with sp.Fori(0, KD) as d:
                    for k in range(NBR):
                        sp.wait_ge(w_split, (m * KD + d) * SU + (k + 1))
                        load_weights(k, (d + 1) % KD)
                m8 = sp.snap(m * MT)

                def load_x(t):
                    sp.wait_ge(h_out[t % 2], 16 * (MT // 2) * m + 16 * (t // 2) + 16)
                    sp.dma_start(xr[:, t % 2], io["x"][0, ds(m * TM + t * P, P), :]).then_inc(x_in[t % 2], 16)

                load_x(0)
                load_x(1)
                for c in range(2):
                    sp.wait_ge(act_split, m * PIECES + (PIECES + c - 1))
                    load_piece((m + 1) % TRIPS, c)
                for t in range(MT):
                    if t + 2 < PIECES:
                        sp.wait_ge(act_split, m * PIECES + (PIECES + t + 1))
                        load_piece((m + 1) % TRIPS, t + 2)
                    sp.wait_ge(h_done, m8 + t + 1)
                    sp.dma_start(dram["h"][ds(m * TM + t * P, P), :], xr[:, t % 2]).then_inc(h_out[t % 2], 16)
                    sp.wait_ge(n_full, m8 + t + 1)
                    sp.dma_start(dram["xn"][ds(m * TM + t * P, P), :], xn[:, t % 2]).then_inc(n_out[t % 2], 16)
                    if t + 2 < MT:
                        load_x(t + 2)
            for i in range(2):
                sp.wait_ge(h_out[i], 16 + 16 * TRIPS * MT // 2)
                sp.wait_ge(n_out[i], 16 + 16 * TRIPS * MT // 2)
            for k in range(NBR):
                sp.wait_ge(w_in[k], 32 * (1 + TRIPS * KD))

        @block.gpsimd
        def _(pool):
            pool.memset(ident[:], 0.0).then_inc(idz, 1)
            pool.wait_ge(idz, 1)
            pool.affine_select(out=ident[:], in_=ident[:], compare_op=ALU.not_equal, fill=1.0, base=0,
                               pattern=[[-1, P]], channel_multiplier=1).then_inc(idn, 1)

        @block.scalar
        def _(act):
            act.sem_inc(g_free, 2)

            def piece_high(n, c):
                act.wait_ge(act_in[c % 2], n * 16)
                act.sem_inc(passed, 1)
                act.activation(act_hi[:, PIECE * c:PIECE * (c + 1)].rearrange("p k t -> p (k t)"), act_raw[:, c % 2],
                               ACT.Copy).then_inc(act_hi_set, 1)

            def weights_high(n, k):
                act.wait_ge(w_in[k], n * 32)
                act.sem_inc(passed, 1)
                act.activation(w_hi[:, k % 2].rearrange("p k n -> p (k n)"), w_raw[:, k].rearrange("p k n -> p (k n)"),
                               ACT.Copy).then_inc(w_hi_set, 1)

            piece_high(1, 0)
            weights_high(1, 0)
            for c in range(1, PIECES):
                piece_high(c // 2 + 1, c)
            act.wait_ge(half_b, 1)
            with act.Fori(0, TRIPS) as m:
                with act.Fori(0, KD) as d:
                    gb = act.snap(m * GPER + d * SU)
                    md = act.snap(m * KD + d)
                    for k in range(NBR):
                        act.wait_ge(b_free, gb + k + 2)
                        weights_high(md + (1 if k + 1 < NBR else 2), (k + 1) % NBR)
                        act.wait_ge(g_full, gb + k + 1)
                        act.sem_inc(passed, 1)
                        act.activation(gt[:], gbank[k % 2][:], ACT.Tanh, scale=0.5, bias=mb[:, k, ds(d, 1)]).then_inc(g_free, 1)
                gb = act.snap(m * GPER + KD * SU)
                m8 = act.snap(m * MT)

                def square(t):
                    act.wait_ge(h_done, m8 + t + 1)
                    act.wait_ge(sq_done, m8 + t + 1)
                    act.activation(sqj[:], xr[:, t % 2], ACT.Square, accum_out=ssq[:, t % 2:t % 2 + 1]).then_inc(sq_done, 1)

                def turn(t):
                    act.wait_ge(r_full, m8 + t + 1)
                    for h in range(2):
                        act.wait_ge(g_full, gb + 2 * t + h + 1)
                        act.activation(xnT[:, 4 * h:4 * h + 4, :].rearrange("p k t -> p (k t)"), gbank[h][:],
                                       ACT.Copy).then_inc(g_free, 1)

                act.wait_ge(b_free, gb + 2)
                piece_high(m * 2 + 3, 0)
                square(0)
                for t in range(1, MT):
                    piece_high(m * 2 + (t // 2 + 3), t)
                    square(t)
                    turn(t - 1)
                turn(MT - 1)

        @block.tensor
        def _(pe):
            pe.sem_inc(r_full, 1)
            pe.wait_ge(idn, 1)
            with pe.Fori(0, TRIPS) as m:
                with pe.Fori(0, KD) as d:
                    base = pe.snap(m * GPER + d * SU)
                    first = pe.snap((m * KD + d) * SU)
                    pieces = pe.snap(m * PIECES + 1)

                    def product(bank, k, w_tiles, a_tile):
                        for kk in w_tiles:
                            a = a_tile + kk - w_tiles[0]
                            if k == 0 and a % PIECE == 0:
                                pe.wait_ge(act_split, pieces + a // PIECE)
                            for w, x in ((w_hi, act_hi), (w_hi, act_lo), (w_lo, act_hi)):
                                last = pe.matmul(bank[:], w[:, k % 2, kk], x[:, a], start=(kk == w_tiles[0] and x is act_hi and w is w_hi),
                                                 stop=(kk == w_tiles[-1] and w is w_lo))
                        return last

                    for k in range(NBR):
                        pe.wait_ge(w_split, first + k + 1)
                        pe.wait_ge(g_free, base + k + 1)
                        product(gbank[k % 2], k, range(KD), 0).then_inc(g_full, 1)
                        if k == 2:
                            pe.wait_ge(act_split, pieces + (PIECES - 1))
                        pe.wait_ge(b_free, base + k + 1)
                        product(bbank[k % 2], k, range(KD, WK), KD + 2 * k).then_inc(b_full, 1)
                base = pe.snap(m * GPER + KD * SU)
                m8 = pe.snap(m * MT)

                def project(t):
                    for h in range(2):
                        pe.wait_ge(b_free, base + 2 * t + h + 1)
                        for kk in range(KD):
                            last = pe.matmul(bbank[h][:], merged[:, kk, t * P:(t + 1) * P], wout[:, kk, h * 512:(h + 1) * 512],
                                             start=(kk == 0), stop=(kk == KD - 1))
                        last.then_inc(b_full, 1)

                def turn(t):
                    pe.wait_ge(n_full, m8 + t + 1)
                    for h in range(2):
                        pe.wait_ge(g_free, base + 2 * t + h + 1)
                        for kk in range(4):
                            last = pe.transpose(gbank[h][:, kk * P:(kk + 1) * P], xn[:, t % 2, (4 * h + kk) * P:(4 * h + kk + 1) * P], ident[:])
                        last.then_inc(g_full, 1)

                def rout(t):
                    pe.wait_ge(g_free, base + 2 * t + 4)
                    pe.wait_ge(r_free, m8 + t + 1)
                    for kk in range(KD):
                        last = pe.matmul(rps[:, 0:R], xnT[:, kk], rw[:, kk], start=(kk == 0), stop=(kk == KD - 1))
                    last.then_inc(r_full, 1)

                pe.wait_ge(wout_in, 16)
                pe.wait_ge(par_in, 16 * len(params))
                pe.wait_ge(dstep, m * TRIP_DVE + KD * STEP_DVE)
                project(0)
                for t in range(1, MT):
                    project(t)
                    if t >= 2:
                        rout(t - 2)
                    turn(t - 1)
                rout(MT - 2)
                turn(MT - 1)
                rout(MT - 1)

        @block.vector
        def _(dve):
            dve.sem_inc(b_free, 2)
            dve.sem_inc(r_free, 1)
            dve.sem_inc(sq_done, 1)

            def piece_low(n, c):
                dve.wait_ge(act_hi_set, n)
                hi = act_hi[:, PIECE * c:PIECE * (c + 1)].rearrange("p k t -> p (k t)")
                dve.tensor_tensor(act_lo[:, PIECE * c:PIECE * (c + 1)].rearrange("p k t -> p (k t)"), act_raw[:, c % 2],
                                  hi.bitcast(F32), ALU.subtract).then_inc(act_split, 1)

            def weights_low(n, k):
                dve.wait_ge(w_hi_set, n)
                hi, lo = (w[:, k % 2].rearrange("p k n -> p (k n)") for w in (w_hi, w_lo))
                dve.tensor_tensor(lo, w_raw[:, k].rearrange("p k n -> p (k n)"), hi.bitcast(F32), ALU.subtract).then_inc(w_split, 1)

            piece_low(1, 0)
            weights_low(1, 0)
            for c in range(1, PIECES):
                piece_low(c + 1, c)
            dve.wait_ge(par_in, 16 * len(params))
            dve.tensor_scalar(mb[:], mb[:], 0.5, None, ALU.mult).then_inc(half_b, 1)
            s = Steps(dve, dstep)
            with dve.Fori(0, TRIPS) as m:
                with dve.Fori(0, KD) as d:
                    gb = dve.snap(m * GPER + d * SU)
                    s.trip(dve.snap(m * TRIP_DVE + d * STEP_DVE))
                    first = dve.snap((m * KD + d) * SU)
                    acc = merged[:, ds(d, 1), :].rearrange("p a t -> p (a t)")
                    for k in range(NBR):
                        weights_low(first + k + 2, (k + 1) % NBR)
                        dve.wait_ge(b_full, gb + k + 1)
                        dve.wait_ge(g_free, gb + k + 3)
                        if k == 0:
                            dve.scalar_tensor_tensor(acc, gt[:], 1.0, bbank[k % 2][:], ALU.add, ALU.mult).then_inc(b_free, 1)
                        else:
                            dve.scalar_tensor_tensor(tmp[:], gt[:], 1.0, bbank[k % 2][:], ALU.add, ALU.mult).then_inc(b_free, 1)
                            dve.wait_ge(b_free, gb + k + 3)
                            s.link(dve.tensor_tensor(acc, acc, tmp[:], ALU.add))
                gb = dve.snap(m * GPER + KD * SU)
                m8 = dve.snap(m * MT)
                s.trip(dve.snap(m * TRIP_DVE + KD * STEP_DVE))

                def residual(t):
                    dve.wait_ge(x_in[t % 2], 16 * (MT // 2) * m + 16 * (t // 2) + 16)
                    for h in range(2):
                        half = xr[:, t % 2, h * 512:(h + 1) * 512]
                        dve.wait_ge(b_full, gb + 2 * t + h + 1)
                        dve.scalar_tensor_tensor(half, bbank[h][:], 0.5, half, ALU.mult, ALU.add).then_inc(b_free, 1)
                    dve.wait_ge(b_free, gb + 2 * t + 4)
                    dve.sem_inc(h_done, 1)

                def norm(t):
                    p = t % 2
                    one = slice(p, p + 1)
                    dve.wait_ge(sq_done, m8 + t + 2)
                    s.link(dve.tensor_scalar(msq[:, one], ssq[:, one], 1.0 / D, EPS, ALU.mult, ALU.add))
                    rsqrt_steps(dve, s, msq[:, one], rh[:, one], rst[:, one], rt[:, one])
                    if t >= 2:
                        dve.wait_ge(g_full, gb + 2 * (t - 2) + 2)
                    dve.wait_ge(n_out[p], 16 * (MT // 2) * m + 16 * (t // 2) + 16)
                    dve.scalar_tensor_tensor(xn[:, p], xr[:, p], rst[:, one], g2[:], ALU.mult, ALU.mult).then_inc(n_full, 1)

                def logit(t):
                    dve.wait_ge(r_full, m8 + t + 2)
                    dve.tensor_tensor(logits[:, ds(m8 + t, 1), :].rearrange("p a r -> p (a r)"), rps[:, 0:R], rb[:], ALU.add).then_inc(r_free, 1)

                pieces = dve.snap(m * PIECES + PIECES)
                piece_low(pieces + 1, 0)
                residual(0)
                for t in range(1, MT):
                    norm(t - 1)
                    piece_low(pieces + (t + 1), t)
                    residual(t)
                    if t >= 3:
                        logit(t - 3)
                norm(MT - 1)
                for t in range(MT - 3, MT):
                    logit(t)
                assert s.n == MT * NORM_STEPS, s.n


def route(nc, logits, table, pos, wts, ends, wt):
    with ExitStack() as ctx:
        def sb(name, shape, dt=F32):
            return ctx.enter_context(nc.sbuf_tensor(name, shape, dt))

        def sem(name):
            return ctx.enter_context(nc.semaphore(name))

        rank_ps, tot_ps, tab_ps = (ctx.enter_context(nc.psum_tensor(f"rtps{i}", [P, 512], F32)) for i in range(3))
        NBT = table.shape[1]
        gmax, gsum, gval = (sb(f"rt_g{i}", [P, TT]) for i in range(3))
        gd, geq = sb("gd", [P, TT, G]), sb("geq", [P, TT, G])
        gi, m1, m2, dd = (sb(f"rt_m{i}", [P, TT]) for i in range(4))
        em, eq = sb("em", [P, TT, E]), sb("eq", [P, TT, E])
        oh = [sb(f"oh{i}", [P, TT, E]) for i in range(2)]
        hot = sb("hot", [P, TT, E])
        io_g, io_e, io_s, io_b, io_tok, io_blk = (sb("io_g", [P, G]), sb("io_e", [P, E]), sb("io_s", [P, P]), sb("io_b", [P, NBT]),
                                                  sb("io_tok", [P, TT]), sb("io_blk", [P, TT]))
        tri, ones = sb("tri", [P, P]), sb("ones", [P, P])
        cum, tot = sb("cum", [P, TT, E]), sb("tot", [P, TT, E])
        cnt, nb, nbi, nbe, e1 = (sb(f"rt_c{i}", [P, E]) for i in range(5))
        big = sb("big", [P, E, TT])
        off = sb("off", [P, TT, E])
        posf = sb("posf", [P, TT, 2])
        posb, poss = sb("posb", [P, TT, 2], I32), sb("poss", [P, TT, 2], I32)
        blkf, slotf = sb("blkf", [P, TT, 2]), sb("slotf", [P, TT, 2])
        V, U = sb("V", [P, TT, 2, P], F32R), sb("U", [P, TT, 2, NBT], F32R)
        consts, ones_set, step = sem("rt_consts"), sem("rt_ones"), sem("rt_steps")
        d_ready, e_done, d2_ready, e2_done = sem("group_diff"), sem("group_exp"), sem("expert_diff"), sem("expert_exp")
        hot_ready, ranks, uv_ready, tab_ready = sem("hot_ready"), sem("ranks"), sem("uv_ready"), sem("table_ready")
        block = ctx.enter_context(nc.Block())

        @block.gpsimd
        def _(pool):
            kw = dict(allow_small_or_imprecise_dtypes=True)
            pool.iota(io_g[:], [[1, G]], base=0, channel_multiplier=0, **kw).then_inc(consts, 1)
            pool.iota(io_e[:], [[1, E]], base=0, channel_multiplier=0, **kw).then_inc(consts, 1)
            pool.iota(io_s[:], [[1, P]], base=0, channel_multiplier=0, **kw).then_inc(consts, 1)
            pool.iota(io_b[:], [[1, NBT]], base=0, channel_multiplier=0, **kw).then_inc(consts, 1)
            pool.iota(io_tok[:], [[P, TT]], base=0, channel_multiplier=1, **kw).then_inc(consts, 1)
            pool.iota(io_blk[:], [[P, TT]], base=0, channel_multiplier=0, **kw).then_inc(consts, 1)
            pool.memset(ones[:], 1.0).then_inc(consts, 1)
            pool.wait_ge(consts, 7)
            pool.affine_select(out=tri[:], in_=ones[:], compare_op=ALU.is_gt, fill=0.0, base=0,
                               pattern=[[1, P]], channel_multiplier=-1).then_inc(consts, 1)
            for i in range(4):
                wt.write_low13(pool, 0, i)
            wt.write_low2(pool, 0)

        @block.sync
        def _(sp):
            for i in range(4):
                wt.load13(sp, 0, i)
            wt.load2(sp, 0)

        @block.scalar
        def _(act):
            act.wait_ge(d_ready, 1)
            act.activation(geq[:], gd[:], ACT.Exp).then_inc(e_done, 1)
            act.wait_ge(d2_ready, 1)
            act.activation(dd[:], dd[:], ACT.Exp).then_inc(e2_done, 1)
            for i in range(4):
                wt.write_high13(act, 0, i)
            wt.write_high2(act, 0)

        @block.tensor
        def _(pe):
            pe.wait_ge(consts, 8)
            pe.wait_ge(hot_ready, 1)
            h = hot[:].rearrange("p t e -> p (t e)")
            pe.matmul(rank_ps[:], tri[:], h, start=True, stop=True)
            pe.matmul(tot_ps[:], ones[:], h, start=True, stop=True).then_inc(ranks, 1)
            for k in range(2):
                pe.wait_ge(uv_ready, k + 1)
                for i in range(TT):
                    last = pe.matmul(tab_ps[:, 0:NBT], V[:, i, k], U[:, i, k], start=(i + k == 0), stop=(i == TT - 1 and k == 1))
            last.then_inc(tab_ready, 1)

        @block.vector
        def _(dve):
            s = Steps(dve, step)
            TTc = dve.tensor_tensor
            bc = lambda ap, n: ap.unsqueeze(2).to_broadcast([P, TT, n])
            row = lambda ap, n: ap.unsqueeze(1).to_broadcast([P, TT, n])
            lgG, lgE = logits[:, :, 0:G], logits[:, :, G:R]

            def first_hot(dst, vals, best, iota_row, n, tmpv, idx):
                s.link(TTc(tmpv, vals, bc(best, n), ALU.is_equal))
                s.link(dve.scalar_tensor_tensor(tmpv, tmpv, -64.0, row(iota_row, n), ALU.mult, ALU.add))
                s.link(dve.tensor_reduce(idx, tmpv, AX.X, ALU.min))
                s.link(dve.tensor_scalar(idx, idx, 64.0, None, ALU.add))
                s.link(TTc(dst, row(iota_row, n), bc(idx, n), ALU.is_equal))

            s.link(dve.tensor_reduce(gmax[:], lgG, AX.X, ALU.max))
            TTc(gd[:], lgG, bc(gmax[:], G), ALU.subtract).then_inc(d_ready, 1)
            dve.wait_ge(e_done, 1)
            s.link(dve.tensor_reduce(gsum[:], geq[:], AX.X, ALU.add))
            s.link(dve.reciprocal(gval[:], gsum[:]))
            dve.wait_ge(consts, 8)
            first_hot(gd[:], lgG, gmax[:], io_g[:], G, geq[:], gi[:])
            s.link(dve.tensor_scalar(gd[:], gd[:], -1.0, 1e30, ALU.add, ALU.mult))
            for g in range(G):
                s.mark(TTc(em[:, :, EPG * g:EPG * (g + 1)], lgE[:, :, EPG * g:EPG * (g + 1)],
                           gd[:, :, g:g + 1].to_broadcast([P, TT, EPG]), ALU.add))
            s.settle()
            s.link(dve.tensor_reduce(m1[:], em[:], AX.X, ALU.max))
            first_hot(oh[0][:], em[:], m1[:], io_e[:], E, eq[:], gi[:])
            s.link(dve.scalar_tensor_tensor(em[:], oh[0][:], -3e38, em[:], ALU.mult, ALU.add))
            s.link(dve.tensor_reduce(m2[:], em[:], AX.X, ALU.max))
            TTc(dd[:], m2[:], m1[:], ALU.subtract).then_inc(d2_ready, 1)
            first_hot(oh[1][:], em[:], m2[:], io_e[:], E, eq[:], gi[:])
            TTc(hot[:], oh[0][:], oh[1][:], ALU.add).then_inc(hot_ready, 1)
            dve.wait_ge(e2_done, 1)
            s.link(dve.tensor_scalar(gsum[:], dd[:], 1.0, None, ALU.add))
            s.link(dve.reciprocal(gsum[:], gsum[:]))
            s.link(TTc(gsum[:], gsum[:], gval[:], ALU.mult))
            s.mark(dve.tensor_copy(wts[:, :, 0], gsum[:]))
            s.mark(TTc(wts[:, :, 1], gsum[:], dd[:], ALU.mult))
            dve.wait_ge(ranks, 1)
            s.link(dve.tensor_copy(tot[:].rearrange("p t e -> p (t e)"), tot_ps[:]))
            s.link(dve.memset(cum[:, 0], 0.0))
            for i in range(1, TT):
                s.link(TTc(cum[:, i], cum[:, i - 1], tot[:, i - 1], ALU.add))
            s.link(TTc(cnt[:], cum[:, TT - 1], tot[:, TT - 1], ALU.add))
            s.link(TTc(big[:], cnt[:].unsqueeze(2).to_broadcast([P, E, TT]), io_blk[:].unsqueeze(1).to_broadcast([P, E, TT]), ALU.is_gt))
            s.link(dve.tensor_reduce(nb[:], big[:], AX.X, ALU.add))
            s.link(dve.tensor_scalar(nb[:], nb[:], 1.0, None, ALU.max))
            s.link(dve.memset(e1[:], 1.0))
            s.link(dve.tensor_tensor_scan(nbi[:], e1[:], nb[:], 0.0, ALU.mult, ALU.add))
            s.link(TTc(nbe[:], nbi[:], nb[:], ALU.subtract))
            s.mark(dve.memset(ends[:, 0:1], 0))
            s.mark(dve.tensor_copy(ends[:, 1:E + 1], nbi[:]))
            s.link(dve.tensor_scalar(nbe[:], nbe[:], float(P), None, ALU.mult))
            s.link(TTc(off[:].rearrange("p t e -> p (t e)"), rank_ps[:], cum[:].rearrange("p t e -> p (t e)"), ALU.add))
            s.link(TTc(off[:], off[:], row(nbe[:], E), ALU.add))
            for k in range(2):
                s.link(TTc(eq[:], oh[k][:], off[:], ALU.mult))
                s.link(dve.tensor_reduce(posf[:, :, k], eq[:], AX.X, ALU.add))
            s.link(dve.tensor_copy(pos[:], posf[:]))
            s.mark(dve.tensor_scalar(posb[:], pos[:], 7, None, ALU.logical_shift_right))
            s.link(dve.tensor_scalar(poss[:], pos[:], P - 1, None, ALU.bitwise_and))
            s.mark(dve.tensor_copy(blkf[:], posb[:]))
            s.link(dve.tensor_copy(slotf[:], poss[:]))
            for k in range(2):
                s.mark(TTc(V[:, :, k], row(io_s[:], P), bc(slotf[:, :, k], P), ALU.is_equal))
                s.link(TTc(U[:, :, k], row(io_b[:], NBT), bc(blkf[:, :, k], NBT), ALU.is_equal))
                s.link(TTc(U[:, :, k], U[:, :, k].bitcast(F32), bc(io_tok[:], NBT), ALU.mult))
                dve.sem_inc(uv_ready, 1)
            dve.wait_ge(tab_ready, 1)
            s.link(dve.tensor_copy(table[:], tab_ps[:, 0:NBT]))


class ExpertWeights:

    def __init__(self, ctx, nc, io):
        def sb(name, shape, dt):
            return ctx.enter_context(nc.sbuf_tensor(name, shape, dt))

        def sem(name):
            return ctx.enter_context(nc.semaphore(name))

        self.io = io
        self.raw13, self.hi13, self.lo13 = (sb(f"w13_{n}", [P, 4, KD * P * 2], dt) for n, dt in (("raw", F32), ("hi", F32R), ("lo", F32R)))
        self.raw2, self.hi2, self.lo2 = (sb(f"w2_{n}", [P, FE, D], dt) for n, dt in (("raw", F32), ("hi", F32R), ("lo", F32R)))
        self.in13, self.in2 = [sem(f"w13_in{i}") for i in range(4)], sem("w2_in")
        self.high13, self.split13, self.high2, self.split2 = sem("w13_high"), sem("w13_split"), sem("w2_high"), sem("w2_split")

    def load13(self, eng, e, i):
        j, name = i // 2, ("expert_w1", "expert_w3")[i % 2]
        src = self.io[name][0, ds(e, 1), :, j * 256:(j + 1) * 256].rearrange("o (k p) n -> p (o k) n", p=P)
        eng.dma_start(self.raw13[:, i].rearrange("p (k n) -> p k n", n=256), src).then_inc(self.in13[i], 16)

    def load2(self, eng, e):
        eng.dma_start(self.raw2[:], self.io["expert_w2"][0, ds(e, 1)].rearrange("o (k p) n -> p (o k) n", p=P)).then_inc(self.in2, 16)

    def write_high13(self, act, e, i):
        act.wait_ge(self.in13[i], e * 16 + 16)
        act.activation(self.hi13[:, i], self.raw13[:, i], ACT.Copy).then_inc(self.high13, 1)

    def write_high2(self, act, e):
        act.wait_ge(self.in2, e * 16 + 16)
        for f in range(FE):
            act.activation(self.hi2[:, f], self.raw2[:, f], ACT.Copy).then_inc(self.high2, 1)

    def write_low13(self, eng, e, i):
        eng.wait_ge(self.high13, e * 4 + (i + 1))
        eng.tensor_tensor(self.lo13[:, i], self.raw13[:, i], self.hi13[:, i].bitcast(F32), ALU.subtract).then_inc(self.split13, 1)

    def write_low2(self, eng, e):
        for f in range(FE):
            eng.wait_ge(self.high2, e * 4 + (f + 1))
            eng.tensor_tensor(self.lo2[:, f], self.raw2[:, f], self.hi2[:, f].bitcast(F32), ALU.subtract).then_inc(self.split2, 1)


def run_experts(nc, dram, table, ends, wt):
    HC = 256
    with ExitStack() as ctx:
        def sb(name, shape, dt=F32):
            return ctx.enter_context(nc.sbuf_tensor(name, shape, dt))

        def sem(name):
            return ctx.enter_context(nc.semaphore(name))

        ps = [ctx.enter_context(nc.psum_tensor(f"exps{i}", [P, 512], F32)) for i in range(8)]
        tbank, hbank, gbank, ybank = ps[0:2], ps[2:4], ps[4:6], ps[6:8]
        xg = sb("xg", [P, D])
        x_hi, x_lo = sb("xT_hi", [P, KD, P], F32R), sb("xT_lo", [P, KD, P], F32R)
        idx = sb("idx", [P, 1], I32)
        th, gg, hg = sb("th", [P, 2, HC]), sb("gg", [P, 2, HC]), sb("hg", [P, 2, HC])
        h_hi, h_lo = sb("hT_hi", [P, FE, P], F32R), sb("hT_lo", [P, FE, P], F32R)
        ysb = sb("ysb", [P, 2, 512])
        ident = sb("x_ident", [P, P])
        zeros = sb("zeros", [P, D])
        zeros_set, zeros_out = sem("zeros_set"), sem("zeros_out")
        idz, idn = sem("x_ident_zero"), sem("x_ident_set")
        idx_set, gathered, turned, x_high, x_split = sem("idx_set"), sem("gathered"), sem("x_turned"), sem("x_high"), sem("x_split")
        h_ps, tanh_d, gate_d, gated = sem("h_psum"), sem("h_tanh"), sem("h_gate"), sem("h_gated")
        h_turned, h_high, h_split = sem("h_turned"), sem("h_high"), sem("h_split")
        y_ps, y_free, y_out = sem("y_psum"), sem("y_read"), [sem(f"y_out{i}") for i in range(2)]
        passed = sem("x_passed")
        block = ctx.enter_context(nc.Block())

        def over_blocks(eng, block_of):
            def expert(e, split):
                b0 = eng.value_load(ends[0:1, ds(e, 1)], min_val=0, max_val=NB - 1)
                b1 = eng.value_load(ends[0:1, ds(e + 1, 1)], min_val=1, max_val=NB - 1)
                last = eng.snap(b1 - 1)
                with eng.If(b0 < last):
                    with eng.Fori(b0, last) as g:
                        block_of(g, None)
                block_of(last, eng.snap(e + 1) if split else None)

            with eng.Fori(0, E - 1) as e:
                expert(e, True)
            expert(E - 1, False)

        @block.sync
        def _(sp):
            total = sp.value_load(ends[0:1, E:E + 1], min_val=1, max_val=NB - 1)

            def fill(n):
                with sp.If(total + n < NB):
                    sp.dma_start(dram["y"][ds((n * -1 + (NB - 1)) * P, P), :], zeros[:]).then_inc(zeros_out, 16)

            sp.wait_ge(zeros_set, 1)
            with sp.Fori(0, E - 1) as e:
                for i in range(4):
                    sp.wait_ge(wt.split13, e * 4 + (i + 1))
                    wt.load13(sp, e + 1, i)
                sp.wait_ge(wt.split2, e * 4 + 4)
                wt.load2(sp, e + 1)
                fill(e)
            fill(E - 1)
            with sp.Fori(0, total) as g:
                sp.sem_inc(zeros_out, 16)
            sp.wait_ge(zeros_out, NB * 16)

        @block.gpsimd
        def _(pool):
            def gather(g):
                pool.wait_ge(turned, g + 1)
                pool.sem_inc(passed, 1)
                pool.tensor_copy(idx[:], table[:, ds(g, 1)]).then_inc(idx_set, 1)
                pool.wait_ge(idx_set, g + 1)
                pool.sem_inc(passed, 1)
                pool.indirect_dma_start(xg[:], None, dram["xn"], bass.IndirectOffsetOnAxis(idx[:], 0)).then_inc(gathered, 16)

            def one(g, nxt):
                gather(g + 2)
                if nxt is not None:
                    wt.write_low2(pool, nxt)

            gather(0)
            pool.memset(ident[:], 0.0).then_inc(idz, 1)
            pool.wait_ge(idz, 1)
            pool.affine_select(out=ident[:], in_=ident[:], compare_op=ALU.not_equal, fill=1.0, base=0,
                               pattern=[[-1, P]], channel_multiplier=1).then_inc(idn, 1)
            pool.memset(zeros[:], 0.0).then_inc(zeros_set, 1)
            gather(1)
            over_blocks(pool, one)
            total = pool.value_load(ends[0:1, E:E + 1], min_val=1, max_val=NB - 1)
            pool.wait_ge(gathered, total * 16 + 32)
            pool.sem_inc(passed, 1)

        @block.tensor
        def _(pe):
            def turn_x(g):
                pe.wait_ge(gathered, g * 16 + 16)
                for h in range(2):
                    for k in range(4):
                        last = pe.transpose(tbank[h][:, k * P:(k + 1) * P], xg[:, (4 * h + k) * P:(4 * h + k + 1) * P], ident[:])
                last.then_inc(turned, 1)

            def turn_h(g, j):
                pe.wait_ge(gated, g * 2 + (j + 3))
                for c in range(2):
                    last = pe.transpose(gbank[j][:, c * P:(c + 1) * P], hg[:, j, c * P:(c + 1) * P], ident[:])
                last.then_inc(h_turned, 1)

            pe.sem_inc(turned, 1)
            pe.sem_inc(h_ps, 1)
            pe.sem_inc(h_turned, 1)
            pe.sem_inc(y_ps, 1)
            pe.wait_ge(idn, 1)
            turn_x(0)
            with pe.Fori(0, E) as e:
                b0 = pe.value_load(ends[0:1, ds(e, 1)], min_val=0, max_val=NB - 1)
                b1 = pe.value_load(ends[0:1, ds(e + 1, 1)], min_val=1, max_val=NB - 1)
                e4 = pe.snap(e * 4)
                with pe.Fori(b0, b1) as g:
                    pe.wait_ge(x_split, g * 2 + 2)
                    for j in range(2):
                        pe.wait_ge(gated, g * 2 + (j + 1))
                        for w in range(2):
                            pe.wait_ge(wt.split13, e4 + (2 * j + w + 1))
                            for k in range(KD):
                                cols = slice(k * HC, (k + 1) * HC)
                                for n, (x, wts_part) in enumerate(((x_hi, wt.hi13), (x_hi, wt.lo13), (x_lo, wt.hi13))):
                                    last = pe.matmul(hbank[j][:, w * HC:(w + 1) * HC], x[:, k], wts_part[:, 2 * j + w, cols],
                                                     start=(k + n == 0), stop=(k == KD - 1 and n == 2))
                        last.then_inc(h_ps, 1)
                    turn_h(g, 0)
                    turn_x(g + 1)
                    turn_h(g, 1)
                    pe.wait_ge(wt.split2, e4 + 4)
                    for f in range(FE):
                        if f % 2 == 0:
                            pe.wait_ge(h_split, g * 2 + (f // 2 + 1))
                        for c in range(2):
                            if f == 0:
                                pe.wait_ge(y_free, g * 2 + (c + 1))
                            for n, (x, wts_part) in enumerate(((h_hi, wt.hi2), (h_hi, wt.lo2), (h_lo, wt.hi2))):
                                last = pe.matmul(ybank[c][:], x[:, f], wts_part[:, f, c * 512:(c + 1) * 512],
                                                 start=(f + n == 0), stop=(f == FE - 1 and n == 2))
                            if f == FE - 1:
                                last.then_inc(y_ps, 1)

        @block.scalar
        def _(act):
            act.sem_inc(y_free, 2)
            act.sem_inc(tanh_d, 1)
            act.sem_inc(h_high, 1)
            for n in range(2):
                act.sem_inc(y_out[n], 16)

            def high_x(g):
                act.wait_ge(turned, g + 2)
                for h in range(2):
                    act.activation(x_hi[:, 4 * h:4 * h + 4].rearrange("p k t -> p (k t)"), tbank[h][:], ACT.Copy).then_inc(x_high, 1)

            def tanh(g, j):
                act.wait_ge(h_ps, g * 2 + (j + 2))
                act.activation(th[:, j], hbank[j][:, 0:HC], ACT.Tanh, scale=0.5).then_inc(tanh_d, 1)

            def high_h(g, j):
                act.wait_ge(h_turned, g * 2 + (j + 2))
                act.activation(h_hi[:, 2 * j:2 * j + 2].rearrange("p f t -> p (f t)"), gbank[j][:, 0:HC], ACT.Copy).then_inc(h_high, 1)

            def one(g, nxt):
                tanh(g, 0)
                if nxt is not None:
                    for i in range(2):
                        wt.write_high13(act, nxt, i)
                tanh(g, 1)
                high_h(g, 0)
                high_x(g + 1)
                high_h(g, 1)
                if nxt is not None:
                    for i in range(2, 4):
                        wt.write_high13(act, nxt, i)
                for n in range(2):
                    act.wait_ge(y_ps, g * 2 + (n + 2))
                    act.wait_ge(y_out[n], g * 16 + 16)
                    act.activation(ysb[:, n], ybank[n][:], ACT.Copy, scale=0.5).then_inc(y_free, 1)
                    act.wait_ge(y_free, g * 2 + (n + 3))
                    act.dma_start(dram["y"][ds(g * P, P), n * 512:(n + 1) * 512], ysb[:, n]).then_inc(y_out[n], 16)
                if nxt is not None:
                    wt.write_high2(act, nxt)

            high_x(0)
            over_blocks(act, one)
            total = act.value_load(ends[0:1, E:E + 1], min_val=1, max_val=NB - 1)
            for n in range(2):
                act.wait_ge(y_out[n], total * 16 + 16)
            act.sem_inc(passed, 1)

        @block.vector
        def _(dve):
            dve.sem_inc(gated, 2)
            dve.sem_inc(gate_d, 1)

            def gate(g, j):
                dve.wait_ge(tanh_d, g * 2 + (j + 2))
                dve.scalar_tensor_tensor(gg[:, j], th[:, j], 1.0, hbank[j][:, 0:HC], ALU.add, ALU.mult).then_inc(gate_d, 1)
                dve.wait_ge(gate_d, g * 2 + (j + 2))
                dve.tensor_tensor(hg[:, j], gg[:, j], hbank[j][:, HC:2 * HC], ALU.mult).then_inc(gated, 1)

            def low_h(g, j):
                dve.wait_ge(h_high, g * 2 + (j + 2))
                hi, lo = (t[:, 2 * j:2 * j + 2].rearrange("p f t -> p (f t)") for t in (h_hi, h_lo))
                dve.tensor_tensor(lo, gbank[j][:, 0:HC], hi.bitcast(F32), ALU.subtract).then_inc(h_split, 1)

            def low_x(g):
                for h in range(2):
                    dve.wait_ge(x_high, g * 2 + (h + 1))
                    hi, lo = (t[:, 4 * h:4 * h + 4].rearrange("p k t -> p (k t)") for t in (x_hi, x_lo))
                    dve.tensor_tensor(lo, tbank[h][:], hi.bitcast(F32), ALU.subtract).then_inc(x_split, 1)

            def one(g, nxt):
                gate(g, 0)
                if nxt is not None:
                    wt.write_low13(dve, nxt, 0)
                gate(g, 1)
                low_h(g, 0)
                low_x(g + 1)
                low_h(g, 1)
                if nxt is not None:
                    for i in range(1, 4):
                        wt.write_low13(dve, nxt, i)

            low_x(0)
            over_blocks(dve, one)


def combine(nc, io, dram, pos, wts, out):
    with ExitStack() as ctx:
        def sb(name, shape, dt=F32):
            return ctx.enter_context(nc.sbuf_tensor(name, shape, dt))

        def sem(name):
            return ctx.enter_context(nc.semaphore(name))

        B, Q = 8, 2
        y = [sb(f"cy{k}", [P, B, D]) for k in range(2)]
        h = sb("ch", [P, B, D])
        o = sb("co", [P, B, D])
        sqj = sb("csq", [P, 2, D])
        fg = sb("fg", [P, D])
        ssq, msq, rst, rh, rt = (sb(f"c_st{i}", [P, B]) for i in range(5))
        idx = sb("cidx", [P, 2, TT], I32)
        y_in = [sem(f"cy_in{b}") for b in range(B)]
        h_in, o_out = ([sem(f"{n}{b}") for b in range(B // Q)] for n in ("ch_in", "co_out"))
        fg_in, acc, sq, done, step = sem("fg_in"), sem("c_sums"), sem("c_squares"), sem("c_done"), sem("c_steps")
        idx_set = sem("c_idx")
        block = ctx.enter_context(nc.Block())

        @block.sync
        def _(sp):

            def load_h(i):
                sp.dma_start(h[:, i % B], dram["h"][i * P:(i + 1) * P, :]).then_inc(h_in[i % B // Q], 16)

            for i in range(B):
                load_h(i)
                if i == 1:
                    sp.dma_start(fg[:], io["final_norm_g"].rearrange("(a n) -> a n", a=1).partition_broadcast(P)).then_inc(fg_in, 16)
            for i in range(TT):
                sp.wait_ge(done, i + 1)
                if i + B < TT:
                    load_h(i + B)
                sp.dma_start(out[0, i * P:(i + 1) * P, :], o[:, i % B]).then_inc(o_out[i % B // Q], 16)
            for b in range(B // Q):
                sp.wait_ge(o_out[b], 16 * Q * TT // B)

        @block.gpsimd
        def _(pool):
            for k in range(2):
                pool.tensor_copy(idx[:, k], pos[:, :, k]).then_inc(idx_set, 1)
            pool.wait_ge(idx_set, 2)
            for i in range(TT):
                b = i % B
                if i >= B:
                    pool.wait_ge(acc, 2 * (i - B) + 2)
                for k in range(2):
                    pool.indirect_dma_start(y[k][:, b], None, dram["y"], bass.IndirectOffsetOnAxis(idx[:, k, i:i + 1], 0)).then_inc(y_in[b], 16)

        @block.scalar
        def _(act):
            for i in range(TT):
                b = i % B
                act.wait_ge(acc, 2 * i + 2)
                if i >= 2:
                    act.wait_ge(sq, i - 1)
                act.activation(sqj[:, i % 2], h[:, b], ACT.Square, accum_out=ssq[:, b:b + 1]).then_inc(sq, 1)

        @block.vector
        def _(dve):
            s = Steps(dve, step)

            def add(i):
                b, turn = i % B, i // B + 1
                dve.wait_ge(h_in[b // Q], 16 * Q * turn)
                dve.wait_ge(y_in[b], 32 * turn)
                for k in range(2):
                    dve.scalar_tensor_tensor(h[:, b], y[k][:, b], wts[:, i, k:k + 1], h[:, b], ALU.mult, ALU.add).then_inc(acc, 1)
                    dve.wait_ge(acc, 2 * i + k + 1)

            def norms(q):
                first = q * Q
                four = slice(first % B, first % B + Q)
                dve.wait_ge(sq, first + Q)
                s.link(dve.tensor_scalar(msq[:, four], ssq[:, four], 1.0 / D, EPS, ALU.mult, ALU.add))
                rsqrt_steps(dve, s, msq[:, four], rh[:, four], rst[:, four], rt[:, four])
                dve.wait_ge(fg_in, 16)
                for i in range(first, first + Q):
                    b = i % B
                    if i >= B:
                        dve.wait_ge(o_out[b // Q], 16 * Q * (i // B))
                    dve.scalar_tensor_tensor(o[:, b], h[:, b], rst[:, b:b + 1], fg[:], ALU.mult, ALU.mult).then_inc(done, 1)

            for q in range(TT // Q):
                for i in range(q * Q, (q + 1) * Q):
                    add(i)
                    if i % Q == 0 and q:
                        norms(q - 1)
            norms(TT // Q - 1)


def trunk(nc, io, out):
    dram = {
        "xT": nc.dram_tensor("xn1_feature_major", [KD, P, T], F32, kind="Internal").ap(),
        "ys": nc.dram_tensor("branches", [NBR, 2, P, T], F32, kind="Internal").ap(),
        "h": nc.dram_tensor("residual", [T, D], F32, kind="Internal").ap(),
        "xn": nc.dram_tensor("xn2", [T, D], F32, kind="Internal").ap(),
        "y": nc.dram_tensor("expert_rows", [NB * P, D], F32, kind="Internal").ap(),
    }
    with ExitStack() as ctx:
        wts = ctx.enter_context(nc.sbuf_tensor("wts", [P, TT, 2], F32))
        pos = ctx.enter_context(nc.sbuf_tensor("pos", [P, TT, 2], I32))
        table = ctx.enter_context(nc.sbuf_tensor("table", [P, NB + 2], I32))
        ends = ctx.enter_context(nc.sbuf_tensor("ends", [P, E + 1], I32))
        mix_branches(nc, io, dram)
        with nc.sbuf_tensor("logits", [P, TT, R], F32) as logits:
            merge_branches(nc, io, dram, logits)
            with ExitStack() as weights_ctx:
                wt = ExpertWeights(weights_ctx, nc, io)
                route(nc, logits, table, pos, wts, ends, wt)
                run_experts(nc, dram, table, ends, wt)
        combine(nc, io, dram, pos, wts, out)


_INS = ["x", "norm1_g", "w_in", "conv_a_w", "pool_w", "pool_b", "pool_scale", "s5_lambda_re", "s5_lambda_im", "s5_log_step",
        "s5_b_re", "s5_b_im", "s5_c_re", "s5_c_im", "s5_d", "s5_glu_w", "s5_glu_b", "lru_conv_w", "lru_conv_b", "lru_wa", "lru_ba",
        "lru_wx", "lru_bx", "lru_lambda", "merge_gate_w", "merge_gate_b", "branch_w", "w_out", "norm2_g", "router_group_w",
        "router_group_b", "router_expert_w", "router_expert_b", "expert_w1", "expert_w3", "expert_w2", "final_norm_g"]


def kernel(**inputs):
    import numpy as _np
    import concourse.bacc as _bacc
    from concourse import mybir as _mybir
    from concourse.bass_utils import run_bass_kernel_spmd as _run

    nc = _bacc.Bacc("TRN2", target_bir_lowering=False, num_devices=1)
    arrays, io = {}, {}
    for name in _INS:
        a = _np.ascontiguousarray(inputs[name])
        arrays[f"in_{name}_dram"] = a
        io[name] = nc.dram_tensor(f"in_{name}_dram", a.shape, _mybir.dt.from_np(a.dtype), kind="ExternalInput").ap()
    out = nc.dram_tensor("out_dram", (1, T, D), F32, kind="ExternalOutput").ap()
    trunk(nc, io, out)
    r = _run(nc, [arrays], core_ids=[0])
    return r.results[0]["out_dram"]
```
